# Optimizing a Trainium2 kernel written in Bass

```python
import jax, jax.numpy as jnp
from jax import lax
import numpy as np
import math

D_MODEL = 1024
BATCH = 1
SEQ = 256
DEPTH = 2

N_MIXERS = 2
N_A_LAYERS = (DEPTH + 1) // 2
N_B_LAYERS = DEPTH // 2

ATT_HEADS = 16
ATT_KV_HEADS = 4
HEAD_DIM = D_MODEL // ATT_HEADS
GROUP = ATT_HEADS // ATT_KV_HEADS
IDX_HEADS = 8
IDX_DIM = 64
TOPK_MAX = 256
Q_BLOCK = 128
ROPE_THETA = 10000.0
Q_COLS = ATT_HEADS * HEAD_DIM
KV_COLS = ATT_KV_HEADS * HEAD_DIM
IQ_COLS = IDX_HEADS * IDX_DIM
IK_COLS = IDX_DIM
IW_COLS = IDX_HEADS
IN_COLS = Q_COLS + 2 * KV_COLS + IQ_COLS + IK_COLS + IW_COLS

RWKV_HEAD = 64
RWKV_HEADS = D_MODEL // RWKV_HEAD
DECAY_LORA = 64
ICL_LORA = 64
GATE_LORA = 160
LNX_EPS = 64e-5

D_FF = 4 * D_MODEL
NORM_EPS = 1e-6


def rms_norm(x, g):
    xf = x.astype(jnp.float32)
    y = xf * lax.rsqrt(jnp.mean(xf * xf, axis=-1, keepdims=True) + NORM_EPS)
    return (y * g.astype(jnp.float32)).astype(x.dtype)

def rope_tables(length, dim):
    inv = 1.0 / (ROPE_THETA ** (jnp.arange(0, dim, 2, dtype=jnp.float32) / dim))
    ang = jnp.arange(length, dtype=jnp.float32)[:, None] * inv[None, :]
    return jnp.cos(ang), jnp.sin(ang)

def apply_rope(x, cos, sin):
    shape = (1, cos.shape[0]) + (1,) * (x.ndim - 3) + (cos.shape[1],)
    c = cos.reshape(shape)
    s = sin.reshape(shape)
    xf = x.astype(jnp.float32)
    x1, x2 = jnp.split(xf, 2, axis=-1)
    return jnp.concatenate([x1 * c - x2 * s, x2 * c + x1 * s], axis=-1).astype(x.dtype)

def dsa_mixer(h, w_in, w_o):
    B, L, _ = h.shape
    top_k = min(TOPK_MAX, L // 4)
    qb_len = min(Q_BLOCK, L)
    n_blk = L // qb_len
    proj = h @ w_in
    o0 = Q_COLS
    o1 = o0 + KV_COLS
    o2 = o1 + KV_COLS
    o3 = o2 + IQ_COLS
    o4 = o3 + IK_COLS
    q = proj[..., :o0].reshape(B, L, ATT_HEADS, HEAD_DIM)
    k = proj[..., o0:o1].reshape(B, L, ATT_KV_HEADS, HEAD_DIM)
    v = proj[..., o1:o2].reshape(B, L, ATT_KV_HEADS, HEAD_DIM)
    qi = proj[..., o2:o3].reshape(B, L, IDX_HEADS, IDX_DIM)
    ki = proj[..., o3:o4]
    wi = proj[..., o4:] * (IDX_HEADS ** -0.5 * IDX_DIM ** -0.5)
    cos, sin = rope_tables(L, HEAD_DIM)
    q = apply_rope(q, cos, sin)
    k = apply_rope(k, cos, sin)
    cos_i, sin_i = rope_tables(L, IDX_DIM)
    qi = apply_rope(qi, cos_i, sin_i)
    ki = apply_rope(ki, cos_i, sin_i)

    def to_blocks(a):
        return jnp.moveaxis(a.reshape((B, n_blk, qb_len) + a.shape[2:]), 1, 0)

    s_pos = jnp.arange(L, dtype=jnp.int32)

    def block_fn(args):
        q_blk, qi_blk, wi_blk, start = args
        t_pos = start + jnp.arange(qb_len, dtype=jnp.int32)
        rel = jax.nn.relu(jnp.einsum('bthd,bsd->bths', qi_blk, ki).astype(jnp.float32))
        score = jnp.einsum('bths,bth->bts', rel, wi_blk.astype(jnp.float32))
        causal = s_pos[None, :] <= t_pos[:, None]
        score = jnp.where(causal[None], score, -jnp.inf)
        _, sel = lax.top_k(score, top_k)
        valid = sel <= t_pos[None, :, None]
        k_sel = jax.vmap(lambda kb, ib: kb[ib])(k, sel)
        v_sel = jax.vmap(lambda vb, ib: vb[ib])(v, sel)
        qg = q_blk.reshape(B, qb_len, ATT_KV_HEADS, GROUP, HEAD_DIM)
        logits = jnp.einsum('btngd,btknd->btngk', qg, k_sel).astype(jnp.float32) * (HEAD_DIM ** -0.5)
        logits = jnp.where(valid[:, :, None, None, :], logits, -jnp.inf)
        p = jax.nn.softmax(logits, axis=-1).astype(v_sel.dtype)
        o = jnp.einsum('btngk,btknd->btngd', p, v_sel)
        return o.reshape(B, qb_len, ATT_HEADS * HEAD_DIM)

    starts = jnp.arange(n_blk, dtype=jnp.int32) * qb_len
    o = lax.map(block_fn, (to_blocks(q), to_blocks(qi), to_blocks(wi), starts))
    o = jnp.moveaxis(o, 0, 1).reshape(B, L, ATT_HEADS * HEAD_DIM)
    return o @ w_o

def token_shift(x):
    return jnp.pad(x, ((0, 0), (1, 0), (0, 0)))[:, :-1]

def rwkv7_mixer(h, mu, w_rkv, w0, w1, w2, a0, a1, a2, g1, g2, k_k, k_a, r_k, lnx_w, lnx_b, w_o):
    B, L, D = h.shape
    H, N = RWKV_HEADS, RWKV_HEAD
    f32 = jnp.float32
    xx = token_shift(h) - h
    xs = h[None] + xx[None] * mu[:, None, None, :]
    r, k, v = jnp.einsum('cbld,cde->cble', xs[:3], w_rkv)
    xw, xa, xg = xs[3], xs[4], xs[5]
    w_log = -jax.nn.softplus(-(w0 + jnp.tanh(xw @ w1) @ w2).astype(f32)) - 0.5
    decay = jnp.exp(-jnp.exp(w_log))
    a = jax.nn.sigmoid((a0 + (xa @ a1) @ a2).astype(f32))
    g = jax.nn.sigmoid(xg @ g1) @ g2
    kf = k.astype(f32)
    kk = (kf * k_k.astype(f32)).reshape(B, L, H, N)
    kk = kk * lax.rsqrt(jnp.maximum(jnp.sum(kk * kk, axis=-1, keepdims=True), 1e-24))
    kf = kf * (1.0 + (a - 1.0) * k_a.astype(f32))

    def heads(z):
        return z.reshape(B, L, H, N)

    rh, wh, kh, vh, ah = heads(r.astype(f32)), heads(decay), heads(kf), heads(v.astype(f32)), heads(a)
    bh = kk * ah

    def step(state, inp):
        r_t, w_t, k_t, v_t, kk_t, b_t = inp
        sa = jnp.einsum('bhvk,bhk->bhv', state, -kk_t)
        state = (state * w_t[:, :, None, :] + sa[..., None] * b_t[:, :, None, :]
                 + v_t[..., None] * k_t[:, :, None, :])
        y = jnp.einsum('bhvk,bhk->bhv', state, r_t)
        return state, y

    def tm(z):
        return jnp.moveaxis(z, 1, 0)

    state0 = jnp.zeros((B, H, N, N), f32)
    _, y = lax.scan(step, state0, (tm(rh), tm(wh), tm(kh), tm(vh), tm(kk), tm(bh)))
    y = jnp.moveaxis(y, 0, 1)
    mean = jnp.mean(y, axis=-1, keepdims=True)
    var = jnp.mean(jnp.square(y - mean), axis=-1, keepdims=True)
    y = ((y - mean) * lax.rsqrt(var + LNX_EPS) * lnx_w.astype(f32).reshape(H, N)
         + lnx_b.astype(f32).reshape(H, N))
    bonus = jnp.sum(rh * kh * r_k.astype(f32), axis=-1, keepdims=True) * vh
    out = (y + bonus).reshape(B, L, D).astype(h.dtype) * g
    return out @ w_o

def sqrelu_mlp(h, w_up, w_down):
    u = jax.nn.relu(h @ w_up)
    return (u * u) @ w_down

def first_inputs(seed: int = 0) -> dict:
    key = jax.random.key(seed)
    ks = jax.random.split(key, 32)
    D = D_MODEL

    def nrm(k, shape, scale):
        return jax.random.normal(k, shape, jnp.float32) * scale

    nA, nB = N_A_LAYERS, N_B_LAYERS
    return {
        "x": nrm(ks[0], (BATCH, SEQ, D), 1.0),
        "mixer_norm": 1.0 + nrm(ks[1], (DEPTH, D), 0.02),
        "mlp_norm": 1.0 + nrm(ks[2], (DEPTH, D), 0.02),
        "mlp_w_up": nrm(ks[3], (DEPTH, D, D_FF), D ** -0.5),
        "mlp_w_down": nrm(ks[4], (DEPTH, D_FF, D), D_FF ** -0.5),
        "final_norm": 1.0 + nrm(ks[5], (D,), 0.02),
        "dsa_w_in": nrm(ks[6], (nA, D, IN_COLS), D ** -0.5),
        "dsa_w_o": nrm(ks[7], (nA, Q_COLS, D), Q_COLS ** -0.5),
        "rwkv_mu": jax.random.uniform(ks[8], (nB, 6, D), jnp.float32),
        "rwkv_w_rkv": nrm(ks[9], (nB, 3, D, D), D ** -0.5),
        "rwkv_w0": jnp.linspace(-6.0, -1.0, D, dtype=jnp.float32)[None, :] + nrm(ks[10], (nB, D), 0.1),
        "rwkv_w1": nrm(ks[11], (nB, D, DECAY_LORA), D ** -0.5),
        "rwkv_w2": nrm(ks[12], (nB, DECAY_LORA, D), 0.1 * DECAY_LORA ** -0.5),
        "rwkv_a0": nrm(ks[13], (nB, D), 0.1),
        "rwkv_a1": nrm(ks[14], (nB, D, ICL_LORA), D ** -0.5),
        "rwkv_a2": nrm(ks[15], (nB, ICL_LORA, D), 0.1 * ICL_LORA ** -0.5),
        "rwkv_g1": nrm(ks[16], (nB, D, GATE_LORA), D ** -0.5),
        "rwkv_g2": nrm(ks[17], (nB, GATE_LORA, D), GATE_LORA ** -0.5),
        "rwkv_k_k": 0.85 + nrm(ks[18], (nB, D), 0.02),
        "rwkv_k_a": 1.0 + nrm(ks[19], (nB, D), 0.02),
        "rwkv_r_k": -0.04 + nrm(ks[20], (nB, RWKV_HEADS, RWKV_HEAD), 0.02),
        "rwkv_lnx_w": 1.0 + nrm(ks[21], (nB, D), 0.02),
        "rwkv_lnx_b": nrm(ks[22], (nB, D), 0.02),
        "rwkv_w_o": nrm(ks[23], (nB, D, D), D ** -0.5),
    }

def first_block(x, mixer_norm, mlp_norm, mlp_w_up, mlp_w_down, final_norm, dsa_w_in, dsa_w_o,
              rwkv_mu, rwkv_w_rkv, rwkv_w0, rwkv_w1, rwkv_w2, rwkv_a0, rwkv_a1, rwkv_a2,
              rwkv_g1, rwkv_g2, rwkv_k_k, rwkv_k_a, rwkv_r_k, rwkv_lnx_w, rwkv_lnx_b, rwkv_w_o):
    for i in range(DEPTH):
        h = rms_norm(x, mixer_norm[i])
        j = i // N_MIXERS
        if i % N_MIXERS == 0:
            x = x + dsa_mixer(h, dsa_w_in[j], dsa_w_o[j])
        else:
            x = x + rwkv7_mixer(h, rwkv_mu[j], rwkv_w_rkv[j], rwkv_w0[j], rwkv_w1[j], rwkv_w2[j],
                                rwkv_a0[j], rwkv_a1[j], rwkv_a2[j], rwkv_g1[j], rwkv_g2[j],
                                rwkv_k_k[j], rwkv_k_a[j], rwkv_r_k[j], rwkv_lnx_w[j],
                                rwkv_lnx_b[j], rwkv_w_o[j])
        x = x + sqrelu_mlp(rms_norm(x, mlp_norm[i]), mlp_w_up[i], mlp_w_down[i])
    return rms_norm(x, final_norm)


N_MIXERS_2 = 4
CONV_WIDTH = 3
CONV_DIM = D_MODEL
DIL_WINDOWS = (128, 512, 2048)
DIL_RATES = (1, 4, 16)
DIL_HEADS = 8
DIL_HEAD_DIM = D_MODEL // DIL_HEADS
DIL_DIM = DIL_HEADS * DIL_HEAD_DIM
SWA_HALF = 128
SWA_Q_HEADS = 16
SWA_KV_HEADS = 4
SWA_HEAD_DIM = 64
SWA_DIM = SWA_Q_HEADS * SWA_HEAD_DIM
DIFF_HEADS = 8
DIFF_HEAD_DIM = D_MODEL // (2 * DIFF_HEADS)
DIFF_DIM = DIFF_HEADS * 2 * DIFF_HEAD_DIM

SUBLN_EPS = 1e-5
NEG_INF = -1e30


def _layers_of_type(t):
    return len(range(t, DEPTH, N_MIXERS_2))

def rms_norm_2(x, g, eps):
    xf = x.astype(jnp.float32)
    y = xf * lax.rsqrt(jnp.mean(xf * xf, axis=-1, keepdims=True) + eps)
    return (y * g.astype(jnp.float32)).astype(x.dtype)

def rope_tables_2(seq, dim):
    inv = ROPE_THETA ** (-jnp.arange(0, dim, 2, dtype=jnp.float32) / dim)
    ang = jnp.arange(seq, dtype=jnp.float32)[:, None] * inv[None, :]
    return jnp.cos(ang), jnp.sin(ang)

def apply_rope_2(x, cos, sin):
    shp = (cos.shape[0],) + (1,) * (x.ndim - 3) + (cos.shape[1],)
    cos, sin = cos.reshape(shp), sin.reshape(shp)
    x1, x2 = jnp.split(x.astype(jnp.float32), 2, axis=-1)
    return jnp.concatenate([x1 * cos - x2 * sin, x2 * cos + x1 * sin], axis=-1).astype(x.dtype)

def adaln_pre_norm(x, c, g, w_mod, b_mod):
    mod = jax.nn.silu(c) @ w_mod + b_mod
    shift, scale, gate = jnp.split(mod, 3, axis=-1)
    h = rms_norm_2(x, g, NORM_EPS) * (1.0 + scale[:, None, :]) + shift[:, None, :]
    return h, gate

def banded_attention(q, k, v, half, sink=None):
    N, L, Hk, G, D = q.shape
    Dv = v.shape[-1]
    blk = half
    nb = -(-L // blk)
    Lp = nb * blk
    qp = jnp.pad(q, ((0, 0), (0, Lp - L), (0, 0), (0, 0), (0, 0))).reshape(N, nb, blk, Hk, G, D)
    kv_pad = ((0, 0), (blk, Lp - L + blk), (0, 0), (0, 0))
    kp = jnp.pad(k, kv_pad).reshape(N, nb + 2, blk, Hk, D)
    vp = jnp.pad(v, kv_pad).reshape(N, nb + 2, blk, Hk, Dv)
    band = lambda t: jnp.concatenate([t[:, :-2], t[:, 1:-1], t[:, 2:]], axis=2)
    kw, vw = band(kp), band(vp)
    qpos = jnp.arange(Lp).reshape(nb, blk)
    kpos = (jnp.arange(nb)[:, None] - 1) * blk + jnp.arange(3 * blk)[None, :]
    kk = kpos[:, None, :]
    valid = (jnp.abs(kk - qpos[:, :, None]) <= half) & (kk >= 0) & (kk < L)
    scale = D ** -0.5
    sink_f = None if sink is None else sink.astype(jnp.float32)[None, :, :, None]

    def one(args):
        qs, ks, vs = args
        s = jnp.einsum('bqhgd,bkhd->bhgqk', qs, ks, preferred_element_type=jnp.float32) * scale
        s = jnp.where(valid[:, None, None], s, NEG_INF)
        m = jnp.max(s, axis=-1)
        if sink_f is not None:
            m = jnp.maximum(m, sink_f)
        p = jnp.exp(s - m[..., None])
        l = jnp.sum(p, axis=-1)
        if sink_f is not None:
            l = l + jnp.exp(sink_f - m)
        o = jnp.einsum('bhgqk,bkhe->bqhge', p, vs.astype(jnp.float32))
        l_t = jnp.moveaxis(l, -1, 1)
        return o / l_t[..., None], jnp.moveaxis(m, -1, 1) + jnp.log(l_t)

    o, lse = lax.map(one, (qp, kw, vw))
    o = o.reshape(N, Lp, Hk, G, Dv)[:, :L]
    lse = lse.reshape(N, Lp, Hk, G)[:, :L]
    return o, lse

def to_strided(x, r):
    B, S = x.shape[:2]
    rest = x.shape[2:]
    x = x.reshape((B, S // r, r) + rest)
    return jnp.moveaxis(x, 2, 1).reshape((B * r, S // r) + rest)

def from_strided(x, r, B):
    L = x.shape[1]
    rest = x.shape[2:]
    x = x.reshape((B, r, L) + rest)
    return jnp.moveaxis(x, 1, 2).reshape((B, L * r) + rest)

def short_conv_mixer(h, w_in, conv_k, w_out):
    b_gate, c_gate, xin, z = jnp.split(h @ w_in, 4, axis=-1)
    t = c_gate * xin
    E = t.shape[-1]
    pad = (CONV_WIDTH - 1) // 2
    conv = lax.conv_general_dilated(
        t, conv_k.astype(t.dtype)[:, None, :], window_strides=(1,), padding=[(pad, pad)],
        dimension_numbers=('NWC', 'WIO', 'NWC'), feature_group_count=E)
    return (b_gate * conv * jax.nn.silu(z)) @ w_out

def dilated_mixer(h, w_in, w_out, cos, sin):
    B, S, _ = h.shape
    G, H, Dh = len(DIL_RATES), DIL_HEADS, DIL_HEAD_DIM
    E = H * Dh
    q, k, v, z = jnp.split(h @ w_in, [G * E, 2 * G * E, 2 * G * E + E], axis=-1)
    q = apply_rope_2(q.reshape(B, S, G, H, Dh), cos, sin)
    k = apply_rope_2(k.reshape(B, S, G, H, Dh), cos, sin)
    v = v.reshape(B, S, H, Dh)
    outs, lses = [], []
    for g in range(G):
        r = DIL_RATES[g]
        half = DIL_WINDOWS[g] // (2 * r)
        o, lse = banded_attention(to_strided(q[:, :, g], r)[:, :, :, None],
                                  to_strided(k[:, :, g], r), to_strided(v, r), half)
        outs.append(from_strided(o[:, :, :, 0], r, B))
        lses.append(from_strided(lse[..., 0], r, B))
    wts = jax.nn.softmax(jnp.stack(lses, axis=0), axis=0)
    o = jnp.sum(wts[..., None] * jnp.stack(outs, axis=0), axis=0)
    y = o.reshape(B, S, E).astype(h.dtype) * jax.nn.silu(z)
    return y @ w_out

def window_gqa_mixer(h, w_in, sink, w_out, cos, sin):
    B, S, _ = h.shape
    Hq, Hk, Dh = SWA_Q_HEADS, SWA_KV_HEADS, SWA_HEAD_DIM
    G = Hq // Hk
    q, k, v, z = jnp.split(h @ w_in, [Hq * Dh, Hq * Dh + Hk * Dh, Hq * Dh + 2 * Hk * Dh], axis=-1)
    q = apply_rope_2(q.reshape(B, S, Hk, G, Dh), cos, sin)
    k = apply_rope_2(k.reshape(B, S, Hk, Dh), cos, sin)
    v = v.reshape(B, S, Hk, Dh)
    o, _ = banded_attention(q, k, v, SWA_HALF, sink.reshape(Hk, G))
    y = o.reshape(B, S, Hq * Dh).astype(h.dtype) * jax.nn.silu(z)
    return y @ w_out

def diff_attention_mixer(h, w_in, lam_vecs, subln_g, w_out, cos, sin, layer_idx):
    B, S, _ = h.shape
    H, d = DIFF_HEADS, DIFF_HEAD_DIM
    q, k, v, z = jnp.split(h @ w_in, 4, axis=-1)
    q = apply_rope_2(q.reshape(B, S, H, 2, d), cos, sin)
    k = apply_rope_2(k.reshape(B, S, H, 2, d), cos, sin)
    v = v.reshape(B, S, H, 2 * d).astype(jnp.float32)
    lam_init = 0.8 - 0.6 * math.exp(-0.3 * layer_idx)
    lv = lam_vecs.astype(jnp.float32)
    lam = jnp.exp(jnp.sum(lv[0] * lv[1])) - jnp.exp(jnp.sum(lv[2] * lv[3])) + lam_init
    nb = S // Q_BLOCK
    qb = jnp.moveaxis(q.reshape(B, nb, Q_BLOCK, H, 2, d), 1, 0)
    scale = d ** -0.5

    def block(qs):
        s = jnp.einsum('bqhcd,bkhcd->bhcqk', qs, k, preferred_element_type=jnp.float32) * scale
        p = jax.nn.softmax(s, axis=-1)
        a = p[:, :, 0] - lam * p[:, :, 1]
        return jnp.einsum('bhqk,bkhe->bqhe', a, v)

    o = jnp.moveaxis(lax.map(block, qb), 0, 1).reshape(B, S, H, 2 * d)
    o = rms_norm_2(o, subln_g, SUBLN_EPS) * (1.0 - lam_init)
    y = o.reshape(B, S, H * 2 * d).astype(h.dtype) * jax.nn.silu(z)
    return y @ w_out

def second_inputs(seed: int = 0) -> dict:
    key = jax.random.key(seed)
    ks = iter(jax.random.split(key, 32))
    nrm = lambda shape, s: jax.random.normal(next(ks), shape, jnp.float32) * s
    D = D_MODEL
    nA, nB, nC, nD = (_layers_of_type(t) for t in range(N_MIXERS_2))
    G = len(DIL_RATES)
    swa_in = 2 * SWA_DIM + 2 * SWA_KV_HEADS * SWA_HEAD_DIM
    return dict(
        x=nrm((BATCH, SEQ, D), 1.0),
        c=nrm((BATCH, D), 1.0),
        norm_g=1.0 + nrm((DEPTH, D), 0.02),
        w_mod=nrm((DEPTH, D, 3 * D), 0.5 * D ** -0.5),
        b_mod=nrm((DEPTH, 3 * D), 0.02),
        conv_w_in=nrm((nA, D, 4 * CONV_DIM), D ** -0.5),
        conv_k=nrm((nA, CONV_WIDTH, CONV_DIM), CONV_WIDTH ** -0.5),
        conv_w_out=nrm((nA, CONV_DIM, D), CONV_DIM ** -0.5),
        dil_w_in=nrm((nB, D, (2 * G + 2) * DIL_DIM), D ** -0.5),
        dil_w_out=nrm((nB, DIL_DIM, D), DIL_DIM ** -0.5),
        swa_w_in=nrm((nC, D, swa_in), D ** -0.5),
        swa_sink=nrm((nC, SWA_Q_HEADS), 1.0),
        swa_w_out=nrm((nC, SWA_DIM, D), SWA_DIM ** -0.5),
        diff_w_in=nrm((nD, D, 4 * DIFF_DIM), D ** -0.5),
        diff_lambda=nrm((nD, 4, DIFF_HEAD_DIM), 0.1),
        diff_subln_g=1.0 + nrm((nD, 2 * DIFF_HEAD_DIM), 0.02),
        diff_w_out=nrm((nD, DIFF_DIM, D), DIFF_DIM ** -0.5),
        final_g=1.0 + nrm((D,), 0.02),
    )

def second_block(x, c, norm_g, w_mod, b_mod, conv_w_in, conv_k, conv_w_out, dil_w_in, dil_w_out,
              swa_w_in, swa_sink, swa_w_out, diff_w_in, diff_lambda, diff_subln_g, diff_w_out,
              final_g):
    S = x.shape[1]
    cos_dil, sin_dil = rope_tables_2(S, DIL_HEAD_DIM)
    cos_swa, sin_swa = rope_tables_2(S, SWA_HEAD_DIM)
    cos_diff, sin_diff = rope_tables_2(S, DIFF_HEAD_DIM)
    for i in range(DEPTH):
        kind, j = i % N_MIXERS_2, i // N_MIXERS_2
        h, gate = adaln_pre_norm(x, c, norm_g[i], w_mod[i], b_mod[i])
        if kind == 0:
            y = short_conv_mixer(h, conv_w_in[j], conv_k[j], conv_w_out[j])
        elif kind == 1:
            y = dilated_mixer(h, dil_w_in[j], dil_w_out[j], cos_dil, sin_dil)
        elif kind == 2:
            y = window_gqa_mixer(h, swa_w_in[j], swa_sink[j], swa_w_out[j], cos_swa, sin_swa)
        else:
            y = diff_attention_mixer(h, diff_w_in[j], diff_lambda[j], diff_subln_g[j],
                                     diff_w_out[j], cos_diff, sin_diff, i)
        x = x + gate[:, None, :] * y
    return rms_norm_2(x, final_g, NORM_EPS)


def setup_inputs(seed=0):
    out = dict(first_inputs(seed))
    for name, value in second_inputs(seed + 1).items():
        if name != "x":
            out[name + "_2"] = value
    return out


def reference(
    x, mixer_norm, mlp_norm, mlp_w_up, mlp_w_down, final_norm, dsa_w_in, dsa_w_o, rwkv_mu,
    rwkv_w_rkv, rwkv_w0, rwkv_w1, rwkv_w2, rwkv_a0, rwkv_a1, rwkv_a2, rwkv_g1, rwkv_g2,
    rwkv_k_k, rwkv_k_a, rwkv_r_k, rwkv_lnx_w, rwkv_lnx_b, rwkv_w_o, c_2, norm_g_2, w_mod_2,
    b_mod_2, conv_w_in_2, conv_k_2, conv_w_out_2, dil_w_in_2, dil_w_out_2, swa_w_in_2,
    swa_sink_2, swa_w_out_2, diff_w_in_2, diff_lambda_2, diff_subln_g_2, diff_w_out_2,
    final_g_2,
):
    x = first_block(
        x, mixer_norm, mlp_norm, mlp_w_up, mlp_w_down, final_norm, dsa_w_in, dsa_w_o, rwkv_mu,
        rwkv_w_rkv, rwkv_w0, rwkv_w1, rwkv_w2, rwkv_a0, rwkv_a1, rwkv_a2, rwkv_g1, rwkv_g2,
        rwkv_k_k, rwkv_k_a, rwkv_r_k, rwkv_lnx_w, rwkv_lnx_b, rwkv_w_o,
    )
    return second_block(
        x, c_2, norm_g_2, w_mod_2, b_mod_2, conv_w_in_2, conv_k_2, conv_w_out_2, dil_w_in_2,
        dil_w_out_2, swa_w_in_2, swa_sink_2, swa_w_out_2, diff_w_in_2, diff_lambda_2,
        diff_subln_g_2, diff_w_out_2, final_g_2,
    )


_drawn_inputs = setup_inputs


def setup_inputs(seed=0):
    import zlib

    import numpy as np

    out = dict(_drawn_inputs(seed))
    spreads = {}
    factors = {'rwkv_w1': 8.0,
     'rwkv_w2': 8.0,
     'rwkv_a0': 3.184,
     'rwkv_a1': 3.501,
     'rwkv_a2': 3.645,
     'rwkv_k_k': 4.519,
     'rwkv_k_a': 4.311,
     'rwkv_r_k': 3.441,
     'rwkv_lnx_w': 7.426,
     'rwkv_lnx_b': 7.47,
     'norm_g_2': 5.55,
     'final_g_2': 2.829}
    for name, (base, spread) in spreads.items():
        noise = np.random.default_rng([zlib.crc32(name.encode()), seed]).standard_normal(out[name].shape)
        drawn = base * np.exp(spread * noise) if base else spread * noise
        out[name] = __import__('jax').numpy.asarray(drawn.astype(out[name].dtype))
    for name, factor in factors.items():
        out[name] = (out[name] * factor).astype(out[name].dtype)
    return out
```

```python
from contextlib import ExitStack

import numpy as np

import concourse.bass as bass
from concourse import mybir

F32 = mybir.dt.float32
F32R = mybir.dt.float32r
BF16 = mybir.dt.bfloat16
ACT = mybir.ActivationFunctionType
ALU = mybir.AluOpType
AX = mybir.AxisListType

P = 128
SEQ = 256
TILES = SEQ // P
D = 1024
KT = D // P
EPS = 1e-6
ROPE_THETA = 10000.0
NEG = -1e30
TAKEN = -2e30

GRAN = 1024
BLOCK = 512
PER_BLOCK = 4
RING = 4

HEADS, KV_HEADS, HD = 16, 4, 64
GROUP = HEADS // KV_HEADS
IDX_HEADS = 8
TOPK = SEQ // 4
Q_COLS = HEADS * HD
KV_COLS = KV_HEADS * HD
IQ_COLS = IDX_HEADS * HD
OFF_K = Q_COLS
OFF_V = OFF_K + KV_COLS
OFF_IQ = OFF_V + KV_COLS
OFF_IK = OFF_IQ + IQ_COLS
OFF_IW = OFF_IK + HD
IDX_SCALE = IDX_HEADS ** -0.5 * HD ** -0.5

FF = 4 * D
FF_STEPS = FF // BLOCK

RN = 64
PAIRS = D // P
CHUNK = 64
CHUNKS = SEQ // CHUNK
DECAY_SCALE = -float(np.exp(-0.5))
LNX_EPS = 64e-5
LORA, GLORA = 64, 160

DIL_HEADS, DIL_HD, DIL_GROUPS = 8, 128, 3
DIL_RATES, DIL_HALF = (1, 4, 16), (64, 64, 64)

STREAM = {}
_at = 0
for _name, _blocks in (("dsa", 4), ("dsa_out", 2), ("mlp0", 16), ("rkv", 6), ("rwkv_out", 2), ("mlp1", 16),
                       ("conv", 8), ("conv_out", 2), ("dil", 16), ("dil_out", 2)):
    STREAM[_name] = _at
    _at += _blocks * PER_BLOCK


def rope_rows(dim, rows):
    inv = (1.0 / (np.float32(ROPE_THETA) ** (np.arange(0, dim, 2, dtype=np.float32) / np.float32(dim)))).astype(np.float32)
    ang = np.arange(SEQ, dtype=np.float32)[None, :] * inv[:, None]
    cos, sin = np.cos(ang), np.sin(ang)
    both = np.stack([np.concatenate([cos, cos]), np.concatenate([-sin, sin])], 1)
    return np.tile(both, (rows // dim, 1, 1)).astype(np.float32)


def shape_constants():
    p = np.arange(P)
    t = np.arange(SEQ)
    ident = np.eye(P, dtype=np.float32)
    row = p[:, None] % CHUNK
    col = np.arange(CHUNK)[None, :]
    strict, incl = (row < col).astype(np.float32), (row <= col).astype(np.float32)
    scan_mask = np.concatenate([strict, incl, strict, incl], 1)
    block16, block32 = (row // 16 == col // 16), (row // 32 == col // 32)
    split_mask = np.concatenate([block16, block32 & ~block16, ~block32], 1).astype(np.float32)
    head_mean = np.kron(np.eye(2), np.full((RN, RN), 1.0 / RN)).astype(np.float32)
    head_of = np.zeros((P, PAIRS, HEADS), np.float32)
    for pair in range(PAIRS):
        for h in range(2):
            head_of[h * RN:(h + 1) * RN, pair, 2 * pair + h] = 1.0
    rows_of = np.zeros((P, PAIRS, P), np.float32)
    rows_of[:HEADS] = head_of.transpose(2, 1, 0)
    parts = {
        "ident": ident,
        "rope64": rope_rows(HD, P),
        "rope128": rope_rows(DIL_HD, P),
        "unit": (row == col).astype(np.float32),
        "scan_mask": scan_mask,
        "split_mask": split_mask,
        "head_mean": head_mean,
        "keep": np.tile((t % CHUNK != 0).astype(np.float32), (P, 1)),
        "head_of": head_of,
        "ones": np.ones((P, P), np.float32),
    }
    causal = np.where(t[None, None, :] <= (p[:, None, None] + P * np.arange(TILES)[None, :, None]), 0.0, NEG)
    dil = np.zeros((P, TILES, DIL_GROUPS, SEQ))
    for i in range(TILES):
        for g in range(DIL_GROUPS):
            q, k, r = p[:, None] + P * i, t[None, :], DIL_RATES[g]
            seen = ((q - k) % r == 0) & (np.abs(q - k) <= DIL_HALF[g] * r)
            dil[:, i, g] = np.where(seen, 0.0, NEG)
    parts_bf = {"ident_bf": ident, "causal": causal, "dil_mask": dil}
    return parts, rows_of, parts_bf


def program(nc, A, out):
    parts, _, parts_bf = shape_constants()
    with ExitStack() as keep:
        def sem(name):
            return keep.enter_context(nc.semaphore(name))

        def room(stack):
            return lambda name, shape, dt=F32: stack.enter_context(nc.sbuf_tensor(name, shape, dt))

        sb = room(keep)
        bank = [keep.enter_context(nc.psum_tensor(f"bank{b}", [P, BLOCK], F32)) for b in range(8)]

        raw = sb("raw", [P, RING, GRAN])
        w_hi = sb("w_hi", [P, RING, GRAN], F32R)
        w_lo = sb("w_lo", [P, RING, GRAN], F32R)
        X = sb("X", [P, TILES, D])
        n_const = sum(int(np.prod(v.shape[1:])) for v in parts.values())
        n_const_bf = sum(int(np.prod(v.shape[1:])) for v in parts_bf.values())
        const = sb("const", [P, n_const])
        const_bf = sb("const_bf", [P, n_const_bf], BF16)
        gate = sb("gate", [P, 2, D])
        scale_row = sb("scale_row", [P, D])
        PROWS_A, PROWS_B = 128, 104
        pcol = sb("pcol", [P, PROWS_A + PROWS_B])
        mod_col = sb("mod_col", [P, 2, 2 * KT])
        gain = sb("gain", [P, 2, KT])
        c_col = sb("c_col", [P, KT])
        stat = sb("stat", [P, 8])
        half_neg = sb("half_neg", [P, SEQ])
        per_head = sb("per_head", [HEADS, SEQ])
        root_head = sb("root_head", [HEADS, SEQ])
        head_rk = sb("head_rk", [P, PAIRS, HEADS])

        view, at = {}, 0
        for name, v in parts.items():
            n = int(np.prod(v.shape[1:]))
            view[name] = const[:, at:at + n]
            at += n
        at = 0
        for name, v in parts_bf.items():
            n = int(np.prod(v.shape[1:]))
            view[name] = const_bf[:, at:at + n]
            at += n
        ident, ident_bf, ones, unit = view["ident"], view["ident_bf"], view["ones"], view["unit"]
        rope64 = view["rope64"].rearrange("p (a t) -> p a t", a=2)
        rope128 = view["rope128"].rearrange("p (a t) -> p a t", a=2)
        causal = view["causal"].rearrange("p (i s) -> p i s", i=TILES)
        dil_mask = view["dil_mask"].rearrange("p (i g s) -> p i g s", i=TILES, g=DIL_GROUPS)
        scan_mask = view["scan_mask"].rearrange("p (m t) -> p m t", m=4)
        split_mask = view["split_mask"].rearrange("p (m t) -> p m t", m=3)
        head_of = view["head_of"].rearrange("p (a h) -> p a h", a=PAIRS)

        def scope(plan):
            with ExitStack() as s:
                return plan(room(s))

        def scan_plan(t):
            return dict(
                prod=[t(f"prod{u}", [P, 4, SEQ]) for u in range(2)],
                aw=[t(f"aw{u}", [P, 4, 2, CHUNK]) for u in range(2)],
                tok=[t(f"tok{u}", [P, 2, TILES, P]) for u in range(2)],
                att=[t(f"att{u}", [P, 2, TILES, 4, CHUNK]) for u in range(2)],
                inv=[t(f"inv{u}", [P, 4, 4, CHUNK]) for u in range(2)],
                off=[t(f"off{u}", [P, 2, 4, CHUNK]) for u in range(2)],
                zz=[t(f"zz{u}", [P, 4, 2, CHUNK]) for u in range(2)],
            )

        def xn_plan(t):
            t("xn_under", [P, 3 * KT * SEQ])
            return t("xn", [P, TILES, D])

        scan = scope(scan_plan)
        state = scan["prod"][0][:, :, :].rearrange("p a (b n) -> p (a b) n", n=RN).rearrange("p (s a) n -> p s a n", s=2)
        xn = scope(xn_plan)
        act_f = sb("act_f", [P, KT, SEQ])
        act_hi, act_lo = [], []
        for u in range(2):
            act_hi.append(sb(f"act_hi{u}", [P, KT, SEQ], F32R))
            act_lo.append(sb(f"act_lo{u}", [P, KT, SEQ], F32R))

        def dsa_plan(t):
            return dict(
                qT=t("qT", [P, HEADS // 2, SEQ]), kT=t("kT", [P, KV_HEADS, SEQ]),
                k_rot=t("k_rot", [P, 2, SEQ]),
                qiT=t("qiT", [P, IDX_HEADS // 2, SEQ]), kiT=t("kiT", [P, SEQ]),
                v=t("v", [P, TILES, KV_COLS]), wi=t("wi", [P, TILES, IDX_HEADS]),
                xs=t("xs", [P, 2, BLOCK]), rot=t("rot", [P, 2, BLOCK]),
                relu=t("relu", [P, 4, BLOCK]), score=t("score", [P, TILES, SEQ]),
                top8=t("top8", [P, TILES, 8]), bias=t("sel_bias", [P, TILES, SEQ], BF16),
                p=t("probs", [P, 2, GROUP, SEQ]), pT=t("probsT", [P, 2, TILES, BLOCK]),
                mx=t("mx", [P, 2, GROUP]), nb=t("nb", [P, 2, GROUP]), den=t("den", [P, 2, GROUP]),
                rden=t("rden", [P, 2, GROUP]), o=t("o_dsa", [P, TILES, D]),
                w_ik=t("w_ik", [P, KT, 2 * HD]), w_iw=t("w_iw", [P, KT, IDX_HEADS]),
                prow_a=t("prow_a", [PROWS_A, P]), prow_b=t("prow_b", [PROWS_B, P]),
            )

        def mlp_plan(t):
            return dict(relu=t("ff_relu", [P, 2, BLOCK]), sq=t("ff_sq", [P, 2, BLOCK]),
                        mod_w=t("mod_w", [P, 3, D]),
                        mod_all=t("mod_all", [P, 3 * D]),
                        hi=t("ff_hi", [P, 2, 4, SEQ], F32R), lo=t("ff_lo", [P, 2, 4, SEQ], F32R))

        def rwkv_plan(t):
            with ExitStack() as s:
                tt = room(s)
                over = dict(rT=tt("rT", [P, PAIRS, SEQ]), kT=tt("kT_r", [P, PAIRS, SEQ]),
                            v=tt("v_r", [P, TILES, D]), rows_of=tt("rows_of", [HEADS, PAIRS, P]),
                            vst=tt("vst", [P, 2, TILES, P]),
                            mid=tt("mid", [P, 4, SEQ]), pc=tt("pc", [P, PAIRS, CHUNKS]))
                with ExitStack() as s2:
                    t2 = room(s2)
                    over.update(hT=t2("hT", [P, KT, SEQ + 1]), xx=t2("xx", [P, KT, SEQ]),
                                w1=t2("w1", [P, KT, LORA]), a1=t2("a1", [P, KT, LORA]),
                                g1=t2("g1", [P, KT, GLORA]), w2=t2("w2", [LORA, D]), a2=t2("a2", [LORA, D]))
                with ExitStack() as s2:
                    t2 = room(s2)
                    for n in ("sg", "a", "cum", "pinv", "kk"):
                        over[n] = t2(n, [P, PAIRS, SEQ])
                over["g2a"] = over["kk"][:, 0:4, :].rearrange("p a t -> p (a t)")
                over["g2b"] = over["kk"][0:GLORA - P, 4:8, :].rearrange("p a t -> p (a t)")
                return over

        def conv_plan(t):
            return dict(xin=t("xin", [P, 4, SEQ]), t=t("tpad", [P, 4, SEQ + 2]), cv=t("cv", [P, 4, SEQ]),
                        sz=t("sz", [P, 4, SEQ]), y=t("y_conv", [P, 4, SEQ]),
                        tmp=t("gated_conv", [P, 2, BLOCK]))

        def dil_plan(t):
            return dict(qk=t("qk", [P, 2 * DIL_GROUPS * DIL_HEADS, SEQ]), v=t("v_dil", [P, TILES, D]),
                        z=t("z_dil", [P, TILES, D]), xs=t("xs_d", [P, 2, BLOCK]), rot=t("rot_d", [P, 2, BLOCK]))

        def dil_att_plan(t):
            t("dil_under", [P, 64 * SEQ])
            return dict(p=t("p_dil", [P, 2, DIL_GROUPS, SEQ]), pT=t("pT_dil", [P, 2, TILES, P]),
                        mx=t("mx_d", [P, 2, 2]), nb=t("nb_d", [P, 2]), den=t("den_d", [P, 2, 2]), rden=t("rden_d", [P, 2, 2]),
                        tmp=t("gated_dil", [P, 2, BLOCK]))

        S = scope(dsa_plan)
        M = scope(mlp_plan)
        R = scope(rwkv_plan)
        C = scope(conv_plan)
        L = scope(dil_plan)
        LA = scope(dil_att_plan)

        def column(first, n=KT):
            return pcol[:, first:first + n]

        MIXER = [column(KT * l) for l in range(2)]
        MLPN = [column(16 + KT * l) for l in range(2)]
        NORM2 = [column(32 + KT * l) for l in range(2)]
        MU = [column(48 + KT * c) for c in range(6)]
        CONV_K = [column(96 + KT * w) for w in range(3)]
        COND = column(120)
        B_MOD = [column(PROWS_A + 24 * l, 16) for l in range(2)]
        W0, A0, K_K, K_A, R_K, LNX_W, LNX_B = (column(PROWS_A + 48 + KT * n) for n in range(7))

        loaded = [sem(f"granule_loaded{s}") for s in range(RING)]
        hi_ready, lo_ready, granule_used = sem("hi_ready"), sem("lo_ready"), sem("granule_used")
        x_loaded, rows_loaded, const_loaded = sem("x_loaded"), sem("rows_loaded"), sem("const_loaded")
        idx_w_loaded, lora_loaded, g2_loaded = sem("idx_w_loaded"), sem("lora_loaded"), sem("g2_loaded")
        scale_loaded, gate_loaded = sem("scale_loaded"), sem("gate_bias_loaded")
        half_ready = sem("half_ready")
        rows_turned, params_ready, cond_ready = sem("rows_turned"), sem("params_ready"), sem("cond_ready")
        squared, rstd_ready, rstd_step = sem("squared"), sem("rstd_ready"), sem("rstd_step")
        xn_ready, turned, f_ready = sem("xn_ready"), sem("turned"), sem("f_ready")
        act_hi_ready, act_lo_ready = sem("act_hi_ready"), sem("act_lo_ready")
        x_updated, x_step = sem("x_updated"), sem("x_step")
        idx_proj = sem("idx_proj")
        rope_x, rope_step, rope_done = sem("rope_x"), sem("rope_step"), sem("rope_done")
        k_spread, v_ready, wi_ready = sem("k_spread"), sem("v_ready"), sem("wi_ready")
        idx_full, idx_relu, scored, top_step, selected = (sem(n) for n in ("idx_full", "idx_relu", "scored", "top_step", "selected"))
        s_full, max_ready, nb_ready, p_ready = sem("s_full"), sem("max_ready"), sem("nb_ready"), sem("p_ready")
        pT_full, pT_ready, pT_ready_act, o_full, rden_ready, o_ready = (sem(n) for n in ("pT_full", "pT_ready", "pT_ready_act", "o_full", "rden_ready", "o_ready"))
        mod_loaded, mod_scaled, mod_used = ([sem(f"mod_{w}{n}") for n in range(3)] for w in ("loaded", "scaled", "used"))
        mod_full, mod_ready = sem("mod_full"), sem("mod_ready")
        up_relu, up_sq, mid_hi, mid_lo = sem("up_relu"), sem("up_sq"), sem("mid_hi"), sem("mid_lo")
        ff_opened = sem("ff_opened")
        hT_edge, shifted, mixed, mix_hi, mix_lo = (sem(n) for n in ("hT_edge", "shifted", "mixed", "mix_hi", "mix_lo"))
        rkv_copied = sem("rkv_copied")
        lora_full, mid_ready, lora2_full, lora2_ready = (sem(n) for n in ("lora_full", "mid_ready", "lora2_full", "lora2_ready"))
        rw_pe, rw_act, rw_dve, rw_root, rw_inverse = (sem(n) for n in ("rwkv_products", "rwkv_scalar", "rwkv_vector", "rwkv_root", "rwkv_inverse"))
        hT_ready = sem("hT_ready")
        chain_full, chain_scaled, chain_ready, y_full, y_ready = (sem(n) for n in ("chain_full", "chain_scaled", "chain_ready", "y_full", "y_ready"))
        vT_full, vT_ready, glora_full, glora_ready = (sem(n) for n in ("vT_full", "vT_ready", "glora_full", "glora_ready"))
        mean_full, centred, dev_sq, var_full, var_ready = (sem(n) for n in ("mean_full", "centred", "dev_sq", "var_full", "var_ready"))
        spread_full, normed, lnx_ready, bonus_full, out_step, mixer_out = (sem(n) for n in ("spread_full", "normed", "lnx_ready", "bonus_full", "out_step", "mixer_out"))
        sc_pe, sc_act, sc_dve, sc_pool = sem("scan_products"), sem("scan_scalar"), sem("scan_vector"), sem("scan_pool")
        conv_x, conv_t, conv_b, conv_z = (sem(n) for n in ("conv_x", "conv_t", "conv_b", "conv_z"))
        conv_edge, conv_tap, conv_y = sem("conv_edge"), sem("conv_tap"), sem("conv_y")
        vz_copied, probs_sum = sem("vz_copied"), sem("probs_sum")
        out_ready, stored = sem("out_ready"), sem("stored")

        SCAN_PE, SCAN_DVE, SCAN_ACT = 26, 20, 18

        block = keep.enter_context(nc.Block())

        def number(base, k, it, turn=8):
            return base + k if it is None else it * turn + (base + k)

        @block.sync
        def _(sp):
            def load(base, k, src, it=None, turn=8):
                g, slot = number(base, k, it, turn), (base + k) % RING
                if it is not None or g >= RING:
                    sp.wait_ge(lo_ready, g - RING + 1)
                dst = raw[:, slot, :]
                if len(src.shape) == 3:
                    dst = dst.rearrange("p (k n) -> p k n", k=src.shape[1])
                sp.dma_start(dst, src).then_inc(loaded[slot], 16)

            def columns(w):
                return w.rearrange("(k p) (b n) -> p k b n", p=P, n=BLOCK)

            def load_out(name, w):
                for n in range(2):
                    for q in range(PER_BLOCK):
                        load(STREAM[name], PER_BLOCK * n + q, columns(w)[:, 2 * q:2 * q + 2, n, :])

            def load_dsa():
                w = A["dsa_w_in"][0].rearrange("(k p) n -> p k n", p=P)
                for n, first in enumerate((OFF_IQ, OFF_K, 0, BLOCK)):
                    for q in range(PER_BLOCK):
                        load(STREAM["dsa"], PER_BLOCK * n + q, w[:, 2 * q:2 * q + 2, first:first + BLOCK])
                load_out("dsa_out", A["dsa_w_o"][0])

            def load_mlp(l):
                base = STREAM[f"mlp{l}"]
                up = columns(A["mlp_w_up"][l])
                down = A["mlp_w_down"][l].rearrange("(j q p) n -> p j q n", p=P, q=PER_BLOCK)
                for q in range(PER_BLOCK):
                    load(base, q, up[:, 2 * q:2 * q + 2, 0, :])
                with sp.Fori(0, FF_STEPS - 1) as it:
                    for q in range(PER_BLOCK):
                        load(base, PER_BLOCK + q, up[:, 2 * q:2 * q + 2, it + 1, :], it)
                    for q in range(PER_BLOCK):
                        load(base, 2 * PER_BLOCK + q, down[:, it, q, :], it)
                for q in range(PER_BLOCK):
                    load(base, 8 * FF_STEPS - PER_BLOCK + q, down[:, FF_STEPS - 1, q, :])

            def load_rwkv():
                w = A["rwkv_w_rkv"][0].rearrange("c (k p) (b n) -> p c k b n", p=P, n=BLOCK)
                with sp.Fori(0, 3) as it:
                    for n in range(2):
                        for q in range(PER_BLOCK):
                            load(STREAM["rkv"], PER_BLOCK * n + q, w[:, it, 2 * q:2 * q + 2, n, :], it)
                load_out("rwkv_out", A["rwkv_w_o"][0])

            def load_conv():
                w = A["conv_w_in_2"][0].rearrange("(k p) (c h n) -> p k c h n", p=P, h=2, n=BLOCK)
                for half in range(2):
                    for n, kind in enumerate((2, 1, 0, 3)):
                        for q in range(PER_BLOCK):
                            load(STREAM["conv"], 16 * half + PER_BLOCK * n + q, w[:, 2 * q:2 * q + 2, kind, half, :])
                load_out("conv_out", A["conv_w_out_2"][0])

            def load_dil():
                w = columns(A["dil_w_in_2"][0])
                with sp.Fori(0, 8) as it:
                    for n in range(2):
                        for q in range(PER_BLOCK):
                            load(STREAM["dil"], PER_BLOCK * n + q, w[:, 2 * q:2 * q + 2, it * 2 + n, :], it)
                load_out("dil_out", A["dil_w_out_2"][0])

            def store():
                for i in range(TILES):
                    sp.wait_ge(out_ready, i + 1)
                    sp.dma_start(out[0, i * P:(i + 1) * P, :], xn[:, i, :]).then_inc(stored, 16)
                sp.wait_ge(stored, 16 * TILES)

            for i in range(TILES):
                sp.dma_start(X[:, i, :], A["x"][0, i * P:(i + 1) * P, :]).then_inc(x_loaded, 16)
            load_dsa()
            load_mlp(0)
            load_rwkv()
            load_mlp(1)
            load_conv()
            load_dil()
            store()

        @block.gpsimd
        def _(pool):
            def rstd(n):
                for i in range(TILES):
                    count = TILES * n + i + 1
                    pool.wait_ge(squared, count)
                    pool.tensor_scalar(stat[:, 2 + i:3 + i], stat[:, i:i + 1], 1.0 / D, EPS, ALU.mult, ALU.add).then_inc(rstd_step, 1)
                    pool.wait_ge(rstd_step, count)
                    pool.tensor_tensor(stat[:, 4 + i:5 + i], stat[:, 2 + i:3 + i], half_neg[:, 0:1], ALU.pow).then_inc(rstd_ready, 1)

            def modulation(l):
                w = A["w_mod_2"][l].rearrange("(k p) (n c) -> n k p c", p=P, c=D)
                done = KT * l

                def load(n, k):
                    pool.dma_start(M["mod_w"][:, n, :], w[n, k]).then_inc(mod_loaded[n], 16)

                def take(n, k):
                    part, total = M["mod_w"][:, n, :], M["mod_all"][:, n * D:(n + 1) * D]
                    pool.wait_ge(mod_scaled[n], k + (done + 1))
                    if isinstance(k, int) and k == 0:
                        pool.tensor_copy(total, part).then_inc(mod_used[n], 1)
                    else:
                        pool.tensor_tensor(total, total, part, ALU.add).then_inc(mod_used[n], 1)
                    pool.wait_ge(mod_used[n], k + (done + 1))

                for n in range(3):
                    load(n, 0)
                for n in range(3):
                    take(n, 0)
                    load(n, 1)
                with pool.Fori(1, KT - 1) as k:
                    for n in range(3):
                        take(n, k)
                        load(n, k + 1)
                for n in range(3):
                    take(n, KT - 1)

            def load_lora():
                pool.wait_ge(x_updated, 8)
                pool.wait_ge(mod_ready, 4)
                for name in ("w1", "a1", "g1"):
                    pool.dma_start(R[name][:], A[f"rwkv_{name}"][0].rearrange("(k p) n -> p k n", p=P)).then_inc(lora_loaded, 16)
                for name in ("w2", "a2"):
                    pool.dma_start(R[name][:], A[f"rwkv_{name}"][0]).then_inc(lora_loaded, 16)
                pool.dma_start(R["rows_of"][:], A["rows_of"].rearrange("h (a p) -> h a p", p=P)).then_inc(lora_loaded, 16)
                pool.memset(R["hT"][:, :, 0:1], 0.0).then_inc(hT_edge, 1)

            def scan_values():
                with pool.Fori(0, PAIRS // 2) as it:
                    for u in range(2):
                        pool.wait_ge(sc_dve, it * SCAN_DVE + (2 + u))
                        pool.tensor_copy(R["vst"][:, u, :, :],
                                         R["v"][:, :, bass.ds(it * (2 * P) + u * P, P)]).then_inc(sc_pool, 1)

            def load_g2():
                pool.wait_ge(sc_dve, SCAN_DVE * (PAIRS // 2 - 1) + 3)
                g2 = A["rwkv_g2"][0]
                pool.dma_start(R["g2a"], g2[0:P, :]).then_inc(g2_loaded, 16)
                pool.dma_start(R["g2b"], g2[P:GLORA, :]).then_inc(g2_loaded, 16)

            def conv_edges():
                pool.wait_ge(x_updated, 16)
                pool.memset(C["t"][:, :, 0:1], 0.0).then_inc(conv_edge, 1)
                pool.memset(C["t"][:, :, SEQ + 1:SEQ + 2], 0.0).then_inc(conv_edge, 1)

            pool.memset(half_neg[:, :], -0.5).then_inc(half_ready, 1)
            pool.wait_ge(half_ready, 1)
            rstd(0)
            rstd(1)
            modulation(0)
            load_lora()
            rstd(2)
            scan_values()
            load_g2()
            rstd(3)
            modulation(1)
            rstd(4)
            conv_edges()
            rstd(5)
            rstd(6)
            rstd(7)

        @block.scalar
        def _(act):
            def split_hi(base, k, it=None, turn=8):
                g, slot = number(base, k, it, turn), (base + k) % RING
                lap = (base + k) // RING + 1
                act.wait_ge(loaded[slot], 16 * lap if it is None else it * (16 * turn // RING) + 16 * lap)
                if it is not None or g >= RING:
                    act.wait_ge(granule_used, g - RING + 1)
                act.activation(w_hi[:, slot, :], raw[:, slot, :], ACT.Copy).then_inc(hi_ready, 1)

            def split_block(base, k0, it=None, turn=8):
                for q in range(PER_BLOCK):
                    split_hi(base, k0 + q, it, turn)

            known = iter(range(1, PER_BLOCK * 6))

            def before_moving(sem_, count):
                value = act.to_reg(count)
                act.wait_ge(lo_ready, next(known))
                act.wait_ge(sem_, value)

            def square(i, sem_, count):
                act.wait_ge(sem_, count)
                act.activation(xn[:, i, :], X[:, i, :], ACT.Square, accum_out=stat[:, i:i + 1]).then_inc(squared, 1)

            def squares(*updated):
                for i in range(TILES):
                    square(i, x_updated, updated[i])

            def round_f(f):
                for b in range(4):
                    act.wait_ge(f_ready, 4 * f + b + 1)
                    act.activation(act_hi[0][:, 2 * b:2 * b + 2, :], act_f[:, 2 * b:2 * b + 2, :], ACT.Copy).then_inc(act_hi_ready, 1)

            def round_turned(n):
                for b in range(4):
                    act.wait_ge(turned, 4 * n + b + 1)
                    act.activation(act_hi[0][:, 2 * b:2 * b + 2, :].rearrange("p k t -> p (k t)"), bank[4 + b][:, :], ACT.Copy).then_inc(act_hi_ready, 1)

            def rope_move(r, k, src, xs, rot, n, half):
                if not isinstance(r, int) or r >= 2:
                    act.wait_ge(rope_done, r - 1)
                slot = k % 2
                act.activation(xs[:, slot, 0:n], src, ACT.Copy)
                for first in range(0, P, half):
                    to = first + half if (first // half) % 2 == 0 else first - half
                    mv = act.activation(rot[to:to + half, slot, 0:n], src[first:first + half, :], ACT.Copy)
                mv.then_inc(rope_x, 1)

            def init():
                act.dma_start(const[:, :], A["const"]).then_inc(const_loaded, 16)
                for to, name in ((0, "mixer_norm"), (16, "mlp_norm"), (32, "norm_g_2")):
                    act.dma_start(S["prow_a"][to:to + 16, :], A[name].rearrange("l (k p) -> (l k) p", p=P)).then_inc(rows_loaded, 16)
                act.dma_start(S["prow_a"][48:96, :], A["rwkv_mu"][0].rearrange("c (k p) -> (c k) p", p=P)).then_inc(rows_loaded, 16)
                act.dma_start(S["prow_a"][96:120, :], A["conv_k_2"][0].rearrange("w (k p) -> (w k) p", p=P)).then_inc(rows_loaded, 16)
                act.dma_start(S["prow_a"][120:128, :], A["c_2"].rearrange("b (k p) -> (b k) p", p=P)).then_inc(rows_loaded, 16)
                act.dma_start(S["prow_b"][0:48, :], A["b_mod_2"].rearrange("l (k p) -> (l k) p", p=P)).then_inc(rows_loaded, 16)
                for n, name in enumerate(("w0", "a0", "k_k", "k_a")):
                    act.dma_start(S["prow_b"][48 + KT * n:48 + KT * (n + 1), :],
                                  A["rwkv_" + name].rearrange("b (k p) -> (b k) p", p=P)).then_inc(rows_loaded, 16)
                act.dma_start(S["prow_b"][80:88, :], A["rwkv_r_k"][0].rearrange("(k h) n -> k (h n)", k=KT)).then_inc(rows_loaded, 16)
                for n, name in enumerate(("lnx_w", "lnx_b")):
                    act.dma_start(S["prow_b"][88 + KT * n:88 + KT * (n + 1), :],
                                  A["rwkv_" + name].rearrange("b (k p) -> (b k) p", p=P)).then_inc(rows_loaded, 16)
                w = A["dsa_w_in"][0].rearrange("(k p) n -> p k n", p=P)
                for half in range(2):
                    act.dma_start(S["w_ik"][:, :, half * HD:(half + 1) * HD], w[:, :, OFF_IK:OFF_IW]).then_inc(idx_w_loaded, 16)
                act.dma_start(S["w_iw"][:, :, :], w[:, :, OFF_IW:OFF_IW + IDX_HEADS]).then_inc(idx_w_loaded, 16)
                act.dma_start(const_bf[:, :], A["const_bf"]).then_inc(const_loaded, 16)
                act.dma_start(scale_row[:, :], A["final_norm"].partition_broadcast(P)).then_inc(scale_loaded, 16)
                for l in range(2):
                    act.dma_start(gate[:, l, :], A["b_mod_2"][l, 2 * D:3 * D].partition_broadcast(P)).then_inc(gate_loaded, 16)
                for i in range(TILES):
                    square(i, x_loaded, 16 * TILES)
                act.wait_ge(params_ready, 2)
                act.activation(c_col[:, :], COND, ACT.Silu).then_inc(cond_ready, 1)

            def dsa():
                base = STREAM["dsa"]

                def rope_bank(r, b, n=BLOCK):
                    rope_move(r, r, bank[b][:, 0:n], S["xs"], S["rot"], n, HD // 2)

                split_block(base, 0)
                round_f(0)
                act.wait_ge(idx_proj, 1)
                rope_bank(0, 4, SEQ)
                act.wait_ge(idx_proj, 2)
                act.activation(S["wi"][:, :, :], bank[5][:, 0:TILES * IDX_HEADS].rearrange("p (i h) -> p i h", i=TILES),
                               ACT.Copy, scale=IDX_SCALE).then_inc(wi_ready, 1)
                split_block(base, 4)
                act.wait_ge(granule_used, base + 4)
                rope_bank(1, 0)
                rope_bank(2, 1)
                split_block(base, 8)
                act.wait_ge(granule_used, base + 8)
                rope_bank(3, 2)
                act.activation(S["v"][:, :, :], bank[3][:, :].rearrange("p (i n) -> p i n", i=TILES), ACT.Copy).then_inc(v_ready, 1)
                split_block(base, 12)
                act.wait_ge(rope_done, 4)
                for n in range(KV_HEADS):
                    for half in range(2):
                        mv = act.activation(S["kT"][half * HD:(half + 1) * HD, n, :],
                                            S["k_rot"][(n % 2) * HD:(n % 2 + 1) * HD, n // 2, :], ACT.Copy)
                mv.then_inc(k_spread, 1)
                act.wait_ge(granule_used, base + 12)
                rope_bank(4, 0)
                rope_bank(5, 1)
                for step in range(4):
                    act.wait_ge(idx_full, step + 1)
                    for e in range(2):
                        n = 2 * step + e
                        if n >= 4:
                            act.wait_ge(scored, 2 * (n - 3))
                        act.activation(S["relu"][:, n % 4, :], bank[4 + n % 4][:, :], ACT.Relu).then_inc(idx_relu, 1)
                split_block(STREAM["dsa_out"], 0)
                act.wait_ge(granule_used, base + 16)
                rope_bank(6, 2)
                rope_bank(7, 3)

                units = TILES * KV_HEADS
                def exps(u):
                    slot = u % 2
                    act.wait_ge(nb_ready, u + 1)
                    if u >= 2:
                        act.wait_ge(pT_full, TILES * (u - 1))
                        act.wait_ge(rden_ready, u - 1)
                    for c in range(GROUP):
                        j, e = c // 2, c % 2
                        ex = act.activation(S["p"][:, slot, c, :], bank[2 * slot + e][:, j * SEQ:(j + 1) * SEQ], ACT.Exp,
                                            bias=S["nb"][:, slot, c:c + 1], scale=HD ** -0.5,
                                            accum_out=S["den"][:, slot, c:c + 1])
                    ex.then_inc(p_ready, 1)

                def copy_pT(u):
                    act.wait_ge(pT_full, TILES * u + 2)
                    if u >= 2:
                        act.wait_ge(o_full, u - 1)
                    act.activation(S["pT"][:, u % 2, 1, :], bank[5][:, :], ACT.Copy).then_inc(pT_ready_act, 1)

                for u in range(units):
                    exps(u)
                    copy_pT(u)
                round_turned(1)
                split_block(STREAM["dsa_out"], 4)

            def mlp(l):
                base, done = STREAM[f"mlp{l}"], 2 * FF_STEPS * l
                split_block(base, 0)
                squares(*((3, 4) if l == 0 else (11, 12)))
                round_f(1 + l)

                def relu(it, first_bank):
                    act.wait_ge(granule_used, it * 8 + (base + (4 if isinstance(it, int) and it == 0 else 0)))
                    for b in range(2):
                        act.activation(M["relu"][:, b, :], bank[first_bank + b][:, :], ACT.Relu).then_inc(up_relu, 1)

                def round_mid(it, slot):
                    for b in range(2):
                        act.wait_ge(up_sq, it * 2 + (done + b + 1))
                        act.activation(M["hi"][:, slot, 2 * b:2 * b + 2, :], M["sq"][:, b, :].rearrange("p (k t) -> p k t", k=2), ACT.Copy).then_inc(mid_hi, 1)

                def scale_mod(k):
                    for n in range(3):
                        if isinstance(k, int):
                            act.wait_ge(mod_loaded[n], 16 * (KT * l + k + 1))
                        else:
                            before_moving(mod_loaded[n], k * 16 + 16 * (KT * l + 1))
                        act.activation(M["mod_w"][:, n, :], M["mod_w"][:, n, :], ACT.Copy,
                                       scale=c_col[:, k:k + 1] if isinstance(k, int) else c_col[:, bass.ds(k, 1)]).then_inc(mod_scaled[n], 1)

                def step(it, first_bank):
                    split_block(base, 4, it)
                    relu(it, first_bank)
                    scale_mod(it)
                    split_hi(base, 8, it)
                    round_mid(it, 0)
                    for q in range(1, PER_BLOCK):
                        split_hi(base, 8 + q, it)

                step(0, 6)
                with act.Fori(1, FF_STEPS - 1) as it:
                    step(it, 0)
                last = FF_STEPS - 1
                scale_mod(last)
                relu(last, 0)
                split_hi(base, 4 + 8 * last)
                round_mid(last, 1)
                for q in range(1, PER_BLOCK):
                    split_hi(base, 4 + 8 * last + q)

            def rwkv_in():
                base = STREAM["rkv"]

                def round_mix(c):
                    for b in range(4):
                        act.wait_ge(mixed, 4 * c + b + 1)
                        act.activation(act_hi[c % 2][:, 2 * b:2 * b + 2, :], act_f[:, 2 * b:2 * b + 2, :], ACT.Copy).then_inc(mix_hi, 1)

                def leave(n):
                    act.wait_ge(granule_used, base + PER_BLOCK * (n + 1))
                    c, half = n // 2, n % 2
                    for j in range(2):
                        src = bank[2 * half + j][:, :]
                        if c < 2:
                            at = 4 * half + 2 * j
                            dst, src = R["rT" if c == 0 else "kT"][:, at:at + 2, :], src.rearrange("p (k t) -> p k t", k=2)
                        else:
                            dst = R["v"][:, j, half * BLOCK:(half + 1) * BLOCK]
                        act.activation(dst, src, ACT.Copy).then_inc(rkv_copied, 1)

                split_block(base, 0)
                squares(6, 8)
                round_mix(0)
                split_block(base, 4)
                round_mix(1)
                leave(0)
                split_block(base, 8)
                leave(1)
                round_mix(2)
                split_block(base, 12)
                leave(2)
                split_block(base, 16)
                leave(3)
                act.wait_ge(lora_full, 1)
                act.activation(R["mid"][0:LORA, 0, :], bank[4][0:LORA, 0:SEQ], ACT.Tanh).then_inc(mid_ready, 1)
                split_block(base, 20)
                leave(4)
                act.wait_ge(lora_full, 2)
                act.activation(R["mid"][0:LORA, 1, :], bank[5][0:LORA, 0:SEQ], ACT.Copy).then_inc(mid_ready, 1)
                split_block(STREAM["rwkv_out"], 0)
                leave(5)
                act.wait_ge(lora_full, 3)
                act.activation(R["mid"][:, 2, :], bank[6][:, 0:SEQ], ACT.Sigmoid)
                act.activation(R["mid"][0:GLORA - P, 3, :], bank[6][0:GLORA - P, SEQ:2 * SEQ], ACT.Sigmoid).then_inc(mid_ready, 1)

            def root(ready, count):
                act.wait_ge(ready, count)
                act.activation(root_head[:, :], per_head[:, :], ACT.Sqrt).then_inc(rw_root, 1)

            def rwkv_mid():
                for b in range(8):
                    act.wait_ge(lora2_full, b + 1)
                    for j in range(2):
                        pair = 2 * (b % 4) + j
                        bias, dst = (W0, R["sg"]) if b < 4 else (A0, R["a"])
                        sg = act.activation(dst[:, pair, :], bank[b][:, j * SEQ:(j + 1) * SEQ], ACT.Sigmoid, bias=bias[:, pair:pair + 1])
                    sg.then_inc(lora2_ready, 1)
                act.wait_ge(rw_dve, 1)
                act.activation(R["pinv"][:, :, :], R["kk"][:, :, :], ACT.Square).then_inc(rw_act, 1)
                root(rw_dve, 4)
                act.activation(R["sg"][:, :, :], R["sg"][:, :, :], ACT.Exp, scale=DECAY_SCALE)
                act.wait_ge(rw_pe, 6)
                act.activation(R["pinv"][:, :, :], R["cum"][:, :, :], ACT.Exp, scale=-DECAY_SCALE).then_inc(rw_act, 1)
                act.wait_ge(rw_act, 2)
                act.activation(R["cum"][:, :, :], R["cum"][:, :, :], ACT.Exp, scale=DECAY_SCALE).then_inc(rw_act, 2)
                act.wait_ge(rw_act, 4)
                act.activation(R["pc"][:, :, :], R["cum"][:, :, :].rearrange("p a (c t) -> p a c t", c=CHUNKS)[:, :, :, CHUNK - 1], ACT.Copy).then_inc(sc_act, 1)

            def scan_loop():
                with act.Fori(0, PAIRS // 2) as it:
                    def products(n):
                        act.wait_ge(sc_pe, it * SCAN_PE + n)

                    def step(first, move):
                        for u in range(2):
                            products(first + u)
                            move(u).then_inc(sc_act, 1)

                    def tiles(ap, a):
                        return ap.rearrange("p (a m t) -> p a m t", a=a, m=4)

                    for u in range(2):
                        products(1 + 2 * u)
                        B, aw, tok = 4 * u, scan["aw"][u], scan["tok"][u]
                        act.activation(aw[:, :, 0, :].rearrange("p (h i) k -> p i h k", h=2),
                                       bank[B][:, 0:SEQ].rearrange("p (i h k) -> p i h k", i=TILES, h=2), ACT.Copy)
                        act.activation(tok[:, 0, :, :], bank[B][:, SEQ:].rearrange("p (i n) -> p i n", i=TILES), ACT.Copy)
                        act.activation(tok[:, 1, :, :], bank[B + 1][:, 0:SEQ].rearrange("p (i n) -> p i n", i=TILES), ACT.Copy).then_inc(sc_act, 1)
                    for u in range(2):
                        products(5 + u)
                        act.activation(scan["inv"][u][:, 1:3, :, :], tiles(bank[4 * u][:, :], 2), ACT.Copy)
                        act.activation(scan["aw"][u][:, :, 1, :], bank[4 * u + 1][:, 0:SEQ].rearrange("p (m t) -> p m t", m=4), ACT.Copy).then_inc(sc_act, 1)
                    for first, b in ((7, 2), (9, 0), (11, 1)):
                        step(first, lambda u: act.activation(scan["inv"][u][:, 2:4, :, :], tiles(bank[4 * u + b][:, :], 2), ACT.Copy))
                    for first, b in ((15, 0), (19, 1)):
                        step(first, lambda u: act.activation(scan["inv"][u][:, 2:3, :, :], tiles(bank[4 * u + b][:, 0:SEQ], 1), ACT.Copy))
                    step(23, lambda u: act.activation(scan["zz"][u][:, :, :, :], bank[4 * u][:, :].rearrange("p (m a t) -> p m a t", m=4, a=2), ACT.Copy))
                    for u in range(2):
                        before_moving(sc_pe, it * SCAN_PE + (25 + u))
                        for par in range(2):
                            dst = R["cum"][:, bass.ds(it * 2 + u, 1), :].rearrange("p a (i c t) -> p (a i) c t", i=TILES, c=2)[:, :, par, :]
                            mv = act.activation(dst, bank[4 * u + 2 + par][:, 0:P].rearrange("p (i t) -> p i t", i=TILES), ACT.Copy)
                        mv.then_inc(sc_act, 1)

            def rwkv_out():
                for b in range(4):
                    act.wait_ge(vT_full, b + 1)
                    act.activation(R["kT"][:, 2 * b:2 * b + 2, :], bank[4 + b][:, :].rearrange("p (k t) -> p k t", k=2), ACT.Copy).then_inc(vT_ready, 1)
                for b in range(4):
                    act.wait_ge(glora_full, b + 1)
                    act.activation(R["a"][:, 2 * b:2 * b + 2, :], bank[4 + b][:, :].rearrange("p (k t) -> p k t", k=2), ACT.Copy).then_inc(glora_ready, 1)
                for b in range(4):
                    act.wait_ge(centred, b + 1)
                    act.activation(R["pinv"][:, 2 * b:2 * b + 2, :], R["cum"][:, 2 * b:2 * b + 2, :], ACT.Square).then_inc(dev_sq, 1)
                root(var_ready, 1)
                for b in range(4):
                    act.wait_ge(normed, b + 1)
                    for pair in (2 * b, 2 * b + 1):
                        ln = act.activation(R["cum"][:, pair, :], R["cum"][:, pair, :], ACT.Identity, bias=LNX_B[:, pair:pair + 1], scale=LNX_W[:, pair:pair + 1])
                    ln.then_inc(lnx_ready, 1)
                for b in range(4):
                    act.wait_ge(mixed, 24 + b + 1)
                    act.activation(act_hi[0][:, 2 * b:2 * b + 2, :], act_f[:, 2 * b:2 * b + 2, :], ACT.Copy).then_inc(mix_hi, 1)
                split_block(STREAM["rwkv_out"], 4)

            def conv():
                base = STREAM["conv"]
                split_block(base, 0)
                squares(14, 16)
                squares(17, 18)
                act.wait_ge(x_updated, 18)
                act.dma_start(scale_row[:, :], A["final_g_2"].partition_broadcast(P)).then_inc(scale_loaded, 16)
                round_f(3)

                def two(ap, j):
                    return ap[:, 2 * j:2 * j + 2, :]

                def psum(b):
                    return bank[b][:, :].rearrange("p (k t) -> p k t", k=2)

                for half in range(2):
                    at = 16 * half
                    split_block(base, at + 4)
                    act.wait_ge(granule_used, base + at + 4)
                    if half:
                        act.wait_ge(conv_t, half)
                    for j in range(2):
                        mv = act.activation(two(C["xin"], j), psum(j), ACT.Copy)
                    mv.then_inc(conv_x, 1)
                    split_block(base, at + 8)
                    split_block(base, at + 12)
                    if half == 0:
                        split_block(base, 16)
                    else:
                        split_block(STREAM["conv_out"], 0)
                    act.wait_ge(granule_used, base + at + 16)
                    if half:
                        act.wait_ge(conv_y, 2 * half)
                    for j in range(2):
                        act.activation(two(C["sz"], j), psum(6 + j), ACT.Silu).then_inc(conv_z, 1)
                    for j in range(2):
                        act.wait_ge(conv_y, 2 * half + j + 1)
                        dst = slice(4 * half + 2 * j, 4 * half + 2 * j + 2)
                        act.activation(act_hi[1][:, dst, :], two(C["y"], j), ACT.Copy).then_inc(act_hi_ready, 1)
                split_block(STREAM["conv_out"], 4)

            def dilated():
                base = STREAM["dil"]
                split_block(base, 0)
                squares(21, 22)
                round_f(4)
                with act.Fori(0, 6) as it:
                    for n in range(2):
                        split_block(base, 4 * n + 4, it)
                        act.wait_ge(granule_used, it * 8 + (base + 4 * (n + 1)))
                        for j in range(2):
                            rope_move(it * 4 + (8 + 2 * n + j), 2 * n + j, bank[2 * n + j][:, :], L["xs"], L["rot"], BLOCK, DIL_HD // 2)
                for n in range(4):
                    if n < 3:
                        split_block(base, PER_BLOCK * (13 + n))
                    else:
                        split_block(STREAM["dil_out"], 0)
                    act.wait_ge(granule_used, base + PER_BLOCK * (13 + n))
                    for i in range(TILES):
                        dst = L["v" if n < 2 else "z"][:, i, n % 2 * BLOCK:(n % 2 + 1) * BLOCK]
                        act.activation(dst, bank[2 * (n % 2) + i][:, :], ACT.Copy if n < 2 else ACT.Silu).then_inc(vz_copied, 1)

                units = DIL_HEADS * TILES

                def exps(u):
                    slot = u % 2
                    act.wait_ge(nb_ready, 8 + u + 1)
                    if u >= 2:
                        act.wait_ge(pT_full, 16 + u - 1)
                    for b, to in ((0, slice(0, 2)), (1, slice(2, 3))):
                        n = SEQ * (2 - b)
                        ex = act.activation(LA["p"][:, slot, to, :], bank[2 * slot + b][:, 0:n].rearrange("p (g s) -> p g s", s=SEQ), ACT.Exp,
                                            bias=LA["nb"][:, slot:slot + 1], scale=DIL_HD ** -0.5, accum_out=LA["den"][:, slot, b:b + 1])
                    ex.then_inc(p_ready, 1)

                def copy_pT(u):
                    act.wait_ge(pT_full, 16 + u + 1)
                    if u >= 2:
                        act.wait_ge(o_full, 8 + u - 1)
                    act.activation(LA["pT"][:, u % 2, :, :], bank[4 + u % 2][:, 0:SEQ].rearrange("p (s t) -> p s t", s=TILES), ACT.Copy).then_inc(pT_ready_act, 1)

                exps(0)
                for u in range(units):
                    if u + 1 < units:
                        exps(u + 1)
                    copy_pT(u)
                round_turned(7)
                split_block(STREAM["dil_out"], 4)

            def final_norm():
                squares(25, 26)

            init()
            dsa()
            mlp(0)
            rwkv_in()
            rwkv_mid()
            scan_loop()
            rwkv_out()
            mlp(1)
            conv()
            dilated()
            final_norm()

        @block.vector
        def _(dve):
            def split_lo(base, k, it=None, turn=8):
                g, slot = number(base, k, it, turn), (base + k) % RING
                dve.wait_ge(hi_ready, g + 1)
                dve.tensor_tensor(w_lo[:, slot, :], raw[:, slot, :], w_hi[:, slot, :].bitcast(F32), ALU.subtract).then_inc(lo_ready, 1)

            def split_block(base, k0, it=None, turn=8):
                for q in range(PER_BLOCK):
                    split_lo(base, k0 + q, it, turn)

            def normalise(n):
                for i in range(TILES):
                    dve.wait_ge(rstd_ready, TILES * n + i + 1)
                    dve.tensor_scalar(xn[:, i, :], X[:, i, :], stat[:, 4 + i:5 + i], None, ALU.mult).then_inc(xn_ready, 1)

            def scale_turned(n, dst, g, ready, shift=None):
                for b in range(4):
                    dve.wait_ge(turned, 4 * n + b + 1)
                    for kk in range(2):
                        kt = 2 * b + kk
                        src = bank[4 + b][:, kk * SEQ:(kk + 1) * SEQ]
                        if shift is None:
                            st = dve.tensor_scalar(dst[:, kt, :], src, g[:, kt:kt + 1], None, ALU.mult)
                        else:
                            st = dve.tensor_scalar(dst[:, kt, :], src, g[:, kt:kt + 1], shift[:, kt:kt + 1], ALU.mult, ALU.add)
                    st.then_inc(ready, 1)

            def rest_f(s):
                for b in range(4):
                    dve.wait_ge(act_hi_ready, 4 * s + b + 1)
                    at = (slice(None), slice(2 * b, 2 * b + 2), slice(None))
                    dve.tensor_tensor(act_lo[0][at], act_f[at], act_hi[0][at].bitcast(F32), ALU.subtract).then_inc(act_lo_ready, 1)

            def rest_turned(s):
                for b in range(4):
                    dve.wait_ge(act_hi_ready, 4 * s + b + 1)
                    at = (slice(None), slice(2 * b, 2 * b + 2), slice(None))
                    dve.tensor_tensor(act_lo[0][at], bank[4 + b][:, :].rearrange("p (k t) -> p k t", k=2),
                                      act_hi[0][at].bitcast(F32), ALU.subtract).then_inc(act_lo_ready, 1)

            def rope_sum(r, k, dst, xs, rot, table, n):
                slot, groups = k % 2, n // SEQ
                def tab(a):
                    return table[:, a:a + 1, :].broadcast_to([P, groups, SEQ])
                def grp(t):
                    return t[:, slot, 0:n].rearrange("p (g t) -> p g t", g=groups)
                dve.wait_ge(rope_x, r + 1)
                dve.tensor_tensor(dst, grp(xs), tab(0), ALU.mult)
                dve.tensor_tensor(grp(rot), grp(rot), tab(1), ALU.mult).then_inc(rope_step, 1)
                dve.wait_ge(rope_step, r + 1)
                dve.tensor_tensor(dst, dst, grp(rot), ALU.add).then_inc(rope_done, 1)

            def add_out(name, n, l=None, tmp=None):
                dve.wait_ge(granule_used, STREAM[name] + PER_BLOCK * (n + 1))
                for i in range(TILES):
                    at = slice(n * BLOCK, (n + 1) * BLOCK)
                    to, src = X[:, i, at], bank[2 * n + i][:, :]
                    if l is not None:
                        step = 4 * l + 2 * n + i
                        if n:
                            dve.wait_ge(x_updated, (18 if l == 0 else 22) + i + 1)
                        dve.tensor_tensor(tmp[:, i, :], src, gate[:, l, at], ALU.mult).then_inc(x_step, 1)
                        dve.wait_ge(x_step, step + 1)
                        src = tmp[:, i, :]
                    dve.tensor_tensor(to, to, src, ALU.add).then_inc(x_updated, 1)

            def take_out(name, following, l=None, tmp=None):
                add_out(name, 0, l, tmp)
                if following:
                    for q in range(PER_BLOCK - 1):
                        split_lo(STREAM[following], q)
                add_out(name, 1, l, tmp)
                if following:
                    split_lo(STREAM[following], PER_BLOCK - 1)

            def init():
                dve.wait_ge(const_loaded, 32)
                dve.wait_ge(rows_turned, 1)
                dve.tensor_copy(pcol[:, 0:PROWS_A], bank[4][:, 0:PROWS_A]).then_inc(params_ready, 1)
                dve.wait_ge(rows_turned, 2)
                dve.tensor_copy(pcol[:, PROWS_A:], bank[5][:, 0:PROWS_B]).then_inc(params_ready, 1)
                dve.wait_ge(params_ready, 2)
                dve.tensor_tensor(head_rk[:, :, :], head_of, R_K.unsqueeze(2).broadcast_to([P, PAIRS, HEADS]), ALU.mult)

            def dsa():
                base = STREAM["dsa"]

                def rope(r, dst, n=BLOCK):
                    rope_sum(r, r, dst, S["xs"], S["rot"], rope64, n)

                normalise(0)
                split_block(base, 0)
                scale_turned(0, act_f, MIXER[0], f_ready)
                rest_f(0)
                rope(0, S["kiT"][:, :].unsqueeze(1), SEQ)
                split_block(base, 4)
                rope(1, S["qiT"][:, 0:2, :])
                rope(2, S["qiT"][:, 2:4, :])
                split_block(base, 8)
                rope(3, S["k_rot"][:, :, :])
                split_block(base, 12)
                rope(4, S["qT"][:, 0:2, :])
                rope(5, S["qT"][:, 2:4, :])
                dve.wait_ge(wi_ready, 1)
                for step in range(4):
                    i = step // 2
                    for e in range(2):
                        n = 2 * step + e
                        dve.wait_ge(idx_relu, n + 1)
                        for j in range(2):
                            h = 4 * (step % 2) + 2 * j + e
                            m = 2 * n + j
                            first = n % 4 == 0 and j == 0
                            if not first:
                                dve.wait_ge(scored, m)
                            dve.scalar_tensor_tensor(S["score"][:, i, :], S["relu"][:, n % 4, j * SEQ:(j + 1) * SEQ],
                                                     S["wi"][:, i, h:h + 1], causal[:, i, :] if first else S["score"][:, i, :],
                                                     ALU.mult, ALU.add).then_inc(scored, 1)
                split_block(STREAM["dsa_out"], 0)
                rope(6, S["qT"][:, 4:6, :])
                rope(7, S["qT"][:, 6:8, :])
                step = 0
                dve.wait_ge(scored, 16)
                for turn in range(TOPK // 8):
                    for i in range(TILES):
                        if turn:
                            dve.wait_ge(top_step, step - 1)
                        dve.max(S["top8"][:, i, :], S["score"][:, i, :]).then_inc(top_step, 1)
                        step += 1
                    for i in range(TILES):
                        dve.wait_ge(top_step, step - 1)
                        dve.match_replace(S["score"][:, i, :], S["top8"][:, i, :], S["score"][:, i, :], TAKEN).then_inc(top_step, 1)
                        step += 1
                for i in range(TILES):
                    dve.wait_ge(top_step, step - 1 + i)
                    dve.tensor_scalar(S["score"][:, i, :], S["score"][:, i, :], (TAKEN + NEG) / 2, NEG, ALU.is_gt, ALU.mult).then_inc(top_step, 1)
                    dve.wait_ge(top_step, step + 1 + i)
                    dve.tensor_tensor(S["bias"][:, i, :], S["score"][:, i, :], causal[:, i, :], ALU.add).then_inc(selected, 1)

                units = TILES * KV_HEADS

                def maxima(u):
                    slot = u % 2
                    dve.wait_ge(s_full, u + 1)
                    if u >= 2:
                        dve.wait_ge(p_ready, u - 1)
                    for e in range(2):
                        mx = dve.tensor_reduce(S["mx"][:, slot, :].rearrange("p (j e) -> p e j", e=2)[:, e, :],
                                               bank[2 * slot + e][:, :].rearrange("p (j t) -> p j t", j=2), AX.X, ALU.max)
                    mx.then_inc(max_ready, 1)
                    dve.wait_ge(max_ready, u + 1)
                    dve.tensor_scalar(S["nb"][:, slot, :], S["mx"][:, slot, :], -HD ** -0.5, None, ALU.mult).then_inc(nb_ready, 1)

                def copy_pT(u):
                    slot = u % 2
                    dve.wait_ge(pT_full, TILES * u + 1)
                    if u >= 2:
                        dve.wait_ge(o_full, u - 1)
                        dve.wait_ge(o_ready, u - 1)
                    dve.tensor_copy(S["pT"][:, slot, 0, :], bank[4][:, :]).then_inc(pT_ready, 1)
                    dve.wait_ge(p_ready, u + 1)
                    dve.reciprocal(S["rden"][:, slot, :], S["den"][:, slot, :]).then_inc(rden_ready, 1)

                def output(u):
                    i, n, slot = u // KV_HEADS, u % KV_HEADS, u % 2
                    dve.wait_ge(o_full, u + 1)
                    dve.wait_ge(rden_ready, u + 1)
                    dve.tensor_tensor(S["o"][:, i, n * SEQ:(n + 1) * SEQ].rearrange("p (c d) -> p c d", c=GROUP),
                                      bank[6 + slot][:, 0:GROUP * HD].rearrange("p (c d) -> p c d", c=GROUP),
                                      S["rden"][:, slot, :].unsqueeze(2).broadcast_to([P, GROUP, HD]), ALU.mult).then_inc(o_ready, 1)

                maxima(0)
                for u in range(units):
                    if u + 1 < units:
                        maxima(u + 1)
                    if u >= 1:
                        output(u - 1)
                    copy_pT(u)
                output(units - 1)
                rest_turned(1)
                split_block(STREAM["dsa_out"], 4)
                take_out("dsa_out", "mlp0")

            def mlp(l, following):
                base, done = STREAM[f"mlp{l}"], 2 * FF_STEPS * l
                normalise(1 + 2 * l)
                scale_turned(2 + 2 * l, act_f, MLPN[l], f_ready)
                rest_f(2 + l)

                def square(it):
                    if not isinstance(it, int) or it > 0:
                        dve.wait_ge(mid_lo, it * 2 + done)
                    for b in range(2):
                        dve.wait_ge(up_relu, it * 2 + (done + b + 1))
                        dve.tensor_tensor(M["sq"][:, b, :], M["relu"][:, b, :], M["relu"][:, b, :], ALU.mult).then_inc(up_sq, 1)

                def rest_mid(it, slot):
                    for b in range(2):
                        at = (slice(None), slot, slice(2 * b, 2 * b + 2), slice(None))
                        dve.wait_ge(mid_hi, it * 2 + (done + b + 1))
                        dve.tensor_tensor(M["lo"][at], M["sq"][:, b, :].rearrange("p (k t) -> p k t", k=2),
                                          M["hi"][at].bitcast(F32), ALU.subtract).then_inc(mid_lo, 1)

                def step(it):
                    split_block(base, 4, it)
                    square(it)
                    split_lo(base, 8, it)
                    rest_mid(it, 0)
                    for q in range(1, PER_BLOCK):
                        split_lo(base, 8 + q, it)

                step(0)
                with dve.Fori(1, FF_STEPS - 1) as it:
                    step(it)
                last = FF_STEPS - 1
                square(last)
                split_lo(base, 4 + 8 * last)
                rest_mid(last, 1)
                for q in range(1, PER_BLOCK):
                    split_lo(base, 4 + 8 * last + q)
                for q in range(PER_BLOCK - 1):
                    split_lo(STREAM[following], q)
                dve.wait_ge(granule_used, base + 8 * FF_STEPS)
                for i in range(TILES):
                    for n in range(2):
                        to = X[:, i, n * BLOCK:(n + 1) * BLOCK]
                        dve.tensor_tensor(to, to, bank[2 + 2 * i + n][:, :], ALU.add).then_inc(x_updated, 1)
                split_lo(STREAM[following], PER_BLOCK - 1)
                modulation(l)

            def modulation(l):
                dve.wait_ge(mod_full, 3 * l + 1)
                dve.tensor_tensor(mod_col[:, l, :], bank[7][:, 0:2 * KT], B_MOD[l], ALU.add).then_inc(mod_ready, 1)
                dve.wait_ge(mod_ready, 4 * l + 1)
                dve.scalar_tensor_tensor(gain[:, l, :], mod_col[:, l, KT:2 * KT], 1.0, NORM2[l], ALU.add, ALU.mult).then_inc(mod_ready, 1)
                dve.wait_ge(gate_loaded, 32)
                for n, b in enumerate((6, 0)):
                    dve.wait_ge(mod_full, 3 * l + 2 + n)
                    to = gate[:, l, n * BLOCK:(n + 1) * BLOCK]
                    dve.tensor_tensor(to, to, bank[b][:, :], ALU.add).then_inc(mod_ready, 1)

            def rwkv_in():
                base = STREAM["rkv"]
                hT, xx = R["hT"], R["xx"]
                normalise(2)
                dve.wait_ge(hT_edge, 1)
                scale_turned(3, hT[:, :, 1:SEQ + 1], MIXER[1], hT_ready)
                for b in range(4):
                    dve.wait_ge(hT_ready, b + 1)
                    at = slice(2 * b, 2 * b + 2)
                    dve.tensor_tensor(xx[:, at, :], hT[:, at, 0:SEQ], hT[:, at, 1:SEQ + 1], ALU.subtract).then_inc(shifted, 1)

                def mix(c):
                    for b in range(4):
                        dve.wait_ge(shifted, b + 1)
                        for kt in (2 * b, 2 * b + 1):
                            mm = dve.scalar_tensor_tensor(act_f[:, kt, :], xx[:, kt, :], MU[c][:, kt:kt + 1],
                                                          hT[:, kt, 1:SEQ + 1], ALU.mult, ALU.add)
                        mm.then_inc(mixed, 1)

                def rest_mix(c):
                    for b in range(4):
                        dve.wait_ge(mix_hi, 4 * c + b + 1)
                        at = (slice(None), slice(2 * b, 2 * b + 2), slice(None))
                        dve.tensor_tensor(act_lo[c % 2][at], act_f[at], act_hi[c % 2][at].bitcast(F32), ALU.subtract).then_inc(mix_lo, 1)

                mix(0)
                rest_mix(0)
                split_block(base, 4)
                dve.wait_ge(mix_lo, 4)
                mix(1)
                rest_mix(1)
                split_block(base, 8)
                dve.wait_ge(mix_lo, 8)
                mix(2)
                rest_mix(2)
                split_block(base, 12)
                dve.wait_ge(mix_lo, 12)
                mix(3)
                split_block(base, 16)
                dve.wait_ge(lora_full, 1)
                mix(4)
                split_block(base, 20)
                dve.wait_ge(lora_full, 2)
                mix(5)
                split_block(STREAM["rwkv_out"], 0)

            def invert(n):
                dve.wait_ge(rw_root, n)
                dve.reciprocal(root_head[:, :], root_head[:, :]).then_inc(rw_inverse, 1)

            def rwkv_mid():
                def all_pairs(column):
                    return column.unsqueeze(2).broadcast_to([P, PAIRS, SEQ])

                rT, kT, kk, a, sg, cum, pinv = (R[n][:, :, :] for n in ("rT", "kT", "kk", "a", "sg", "cum", "pinv"))
                dve.wait_ge(rkv_copied, 8)
                dve.wait_ge(lora2_full, 8)
                dve.tensor_tensor(kk, kT, all_pairs(K_K), ALU.mult).then_inc(rw_dve, 1)
                dve.wait_ge(lora2_ready, 8)
                for pair in range(PAIRS):
                    sc = dve.tensor_tensor_scan(cum[:, pair, :], view["keep"], sg[:, pair, :], 0.0, ALU.mult, ALU.add)
                sc.then_inc(rw_dve, 1)
                dve.wait_ge(rw_dve, 2)
                dve.tensor_tensor(sg, cum, sg, ALU.subtract).then_inc(rw_dve, 1)
                dve.wait_ge(rw_pe, 1)
                dve.tensor_scalar(per_head[:, :], bank[0][0:HEADS, 0:SEQ], 1e-24, None, ALU.max).then_inc(rw_dve, 1)
                dve.scalar_tensor_tensor(pinv, a, -1.0, all_pairs(K_A), ALU.add, ALU.mult).then_inc(rw_dve, 1)
                invert(1)
                dve.wait_ge(rw_dve, 5)
                dve.scalar_tensor_tensor(kT, pinv, 1.0, kT, ALU.add, ALU.mult).then_inc(rw_dve, 1)
                dve.wait_ge(rw_dve, 6)
                dve.tensor_tensor(pinv, rT, kT, ALU.mult).then_inc(rw_dve, 1)
                for b in range(4):
                    dve.wait_ge(rw_pe, 2 + b)
                    at = slice(2 * b, 2 * b + 2)
                    nk = dve.tensor_tensor(R["kk"][:, at, :], R["kk"][:, at, :], bank[4 + b][:, :].rearrange("p (k t) -> p k t", k=2), ALU.mult)
                nk.then_inc(rw_dve, 1)
                dve.wait_ge(rw_dve, 8)
                dve.tensor_tensor(a, kk, a, ALU.mult).then_inc(rw_dve, 1)
                dve.wait_ge(rw_pe, 6)
                dve.tensor_copy(R["mid"][0:HEADS, 0, :], bank[1][0:HEADS, 0:SEQ]).then_inc(sc_dve, 1)

            def scan_loop():
                dve.wait_ge(rw_act, 4)
                dve.wait_ge(rw_dve, 9)
                with dve.Fori(0, PAIRS // 2) as it:
                    def pair(t, u):
                        return t[:, bass.ds(it * 2 + u, 1), :]

                    def before(n):
                        dve.wait_ge(sc_dve, it * SCAN_DVE + (n + 1))

                    def products(n):
                        dve.wait_ge(sc_pe, it * SCAN_PE + n)

                    for u in range(2):
                        prod = scan["prod"][u]
                        before(u)
                        dve.scalar_tensor_tensor(prod[:, 0:1, :], pair(R["kk"], u), -1.0, pair(R["sg"], u), ALU.mult, ALU.mult)
                        dve.tensor_tensor(prod[:, 1:2, :], pair(R["rT"], u), pair(R["cum"], u), ALU.mult)
                        dve.tensor_tensor(prod[:, 2:3, :], pair(R["a"], u), pair(R["pinv"], u), ALU.mult)
                        dve.tensor_tensor(prod[:, 3:4, :], pair(R["kT"], u), pair(R["pinv"], u), ALU.mult).then_inc(sc_dve, 1)
                    for u in range(2):
                        att, inv, off = scan["att"][u], scan["inv"][u], scan["off"][u]
                        n = 3 + 3 * u
                        products(2 * u + 2)
                        for h in range(2):
                            dv = dve.tensor_tensor(att[:, h, :, :, :], bank[4 * u + 2 + h][:, :].rearrange("p (i m t) -> p i m t", i=TILES, m=4),
                                                   scan_mask.unsqueeze(1).broadcast_to([P, TILES, 4, CHUNK]), ALU.mult)
                        dv.then_inc(sc_dve, 1)
                        before(n)
                        N = att[:, :, :, 0, :].rearrange("p h i t -> p (h i) t")

                        def cut(m):
                            return split_mask[:, m:m + 1, :].broadcast_to([P, 4, CHUNK])

                        dve.tensor_tensor(inv[:, 3, :, :], N, cut(0), ALU.mult).then_inc(sc_dve, 1)
                        for m in range(2):
                            dve.tensor_tensor(off[:, m, :, :], N, cut(1 + m), ALU.mult)
                        before(n + 1)
                        dve.tensor_tensor(inv[:, 0, :, :], inv[:, 3, :, :], unit.unsqueeze(1).broadcast_to([P, 4, CHUNK]), ALU.add).then_inc(sc_dve, 1)

                    def grow(n, step, bank_of, both=True):
                        for u in range(2):
                            to = scan["inv"][u][:, 0:2 if both else 1, :, :].rearrange("p a m t -> p (a m) t")
                            products(step + u)
                            dve.tensor_tensor(to, to, bank[4 * u + bank_of][:, 0:512 if both else 256].rearrange("p (m t) -> p m t", t=CHUNK),
                                              ALU.add).then_inc(sc_dve, 1)

                    grow(9, 9, 3)
                    grow(11, 11, 2)
                    grow(13, 13, 3)
                    grow(15, 17, 2)
                    grow(17, 21, 3, False)
                    for u in range(2):
                        products(25 + u)
                        for par in range(2):
                            def out(t):
                                return pair(t, u).rearrange("p a (i c t) -> p (a i) c t", i=TILES, c=2)[:, :, par, :]

                            def part(m):
                                return bank[4 * u + par][:, m * P:(m + 1) * P].rearrange("p (i t) -> p i t", i=TILES)

                            rho = scan["prod"][u][:, 1, :].rearrange("p (i c t) -> p i c t", i=TILES, c=2)[:, :, par, :]
                            dve.tensor_tensor(out(R["sg"]), part(0), unit.unsqueeze(1).broadcast_to([P, TILES, RN]), ALU.add)
                            dve.tensor_tensor(out(R["rT"]), part(1), rho, ALU.add)
                            pc = pair(R["pc"], u).rearrange("p a (i c) -> p (a i) c", c=2)[:, :, par:par + 1].broadcast_to([P, TILES, RN])
                            dv = dve.tensor_tensor(out(R["pinv"]), part(2), pc, ALU.mult)
                        dv.then_inc(sc_dve, 1)

            def rwkv_out():
                all_dve, all_pe = SCAN_DVE * (PAIRS // 2), SCAN_PE * (PAIRS // 2)
                F, G, Y = R["sg"], R["pinv"], R["cum"]

                def chunk(t, c):
                    return t[:, :, c * CHUNK:(c + 1) * CHUNK]

                def rows(b):
                    return bank[b][:, :].rearrange("p (a n) -> p a n", a=PAIRS)

                def add_y(c):
                    dve.wait_ge(y_full, c)
                    dve.tensor_tensor(chunk(Y, c), chunk(Y, c), rows(2 + c % 2), ALU.add).then_inc(y_ready, 1)

                dve.wait_ge(sc_act, 1 + SCAN_ACT * (PAIRS // 2))
                for c in range(1, CHUNKS - 1):
                    dve.wait_ge(chain_full, c)
                    st = state[:, c - 1, :, :]
                    dve.tensor_tensor(st, rows(c - 1), R["pc"][:, :, c:c + 1].broadcast_to([P, PAIRS, RN]), ALU.mult).then_inc(chain_scaled, 1)
                    dve.wait_ge(chain_scaled, c)
                    dve.tensor_tensor(st, st, chunk(G, c), ALU.add).then_inc(chain_ready, 1)
                    add_y(c)
                add_y(CHUNKS - 1)
                for b in range(4):
                    at = slice(2 * b, 2 * b + 2)
                    dve.wait_ge(mean_full, b + 1)
                    dve.tensor_tensor(Y[:, at, :], Y[:, at, :], bank[4 + b][:, :].rearrange("p (k t) -> p k t", k=2), ALU.subtract).then_inc(centred, 1)
                for b in range(4):
                    at = slice(2 * b, 2 * b + 2)
                    dve.wait_ge(bonus_full, b + 1)
                    dve.wait_ge(vT_ready, 4)
                    dve.tensor_tensor(R["kT"][:, at, :], R["kT"][:, at, :], bank[b][:, :].rearrange("p (k t) -> p k t", k=2), ALU.mult).then_inc(out_step, 1)
                dve.wait_ge(var_full, 1)
                dve.tensor_scalar(per_head[:, :], bank[4][0:HEADS, 0:SEQ], 1.0 / RN, LNX_EPS, ALU.mult, ALU.add).then_inc(var_ready, 1)
                invert(2)
                for b in range(4):
                    at = slice(2 * b, 2 * b + 2)
                    dve.wait_ge(spread_full, b + 1)
                    dve.tensor_tensor(Y[:, at, :], Y[:, at, :], bank[4 + b][:, :].rearrange("p (k t) -> p k t", k=2), ALU.mult).then_inc(normed, 1)
                for b in range(4):
                    at = slice(2 * b, 2 * b + 2)
                    dve.wait_ge(lnx_ready, b + 1)
                    dve.tensor_tensor(Y[:, at, :], Y[:, at, :], R["kT"][:, at, :], ALU.add).then_inc(out_step, 1)
                for b in range(4):
                    at = slice(2 * b, 2 * b + 2)
                    dve.wait_ge(out_step, 4 + b + 1)
                    dve.wait_ge(glora_ready, b + 1)
                    dve.tensor_tensor(act_f[:, at, :], Y[:, at, :], R["a"][:, at, :], ALU.mult).then_inc(mixed, 1)
                for b in range(4):
                    at = (slice(None), slice(2 * b, 2 * b + 2), slice(None))
                    dve.wait_ge(mix_hi, 12 + b + 1)
                    dve.tensor_tensor(act_lo[0][at], act_f[at], act_hi[0][at].bitcast(F32), ALU.subtract).then_inc(mix_lo, 1)
                split_block(STREAM["rwkv_out"], 4)
                take_out("rwkv_out", "mlp1")

            def mid_norm():
                dve.wait_ge(scale_loaded, 16)
                for i in range(TILES):
                    dve.wait_ge(rstd_ready, TILES * 4 + i + 1)
                    dve.scalar_tensor_tensor(X[:, i, :], X[:, i, :], stat[:, 4 + i:5 + i], scale_row[:, :], ALU.mult, ALU.mult).then_inc(x_updated, 1)

            def conv():
                base = STREAM["conv"]
                dve.wait_ge(x_updated, 18)
                normalise(5)
                dve.wait_ge(mod_ready, 8)
                scale_turned(5, act_f, gain[:, 0, :], f_ready, mod_col[:, 0, 0:KT])
                rest_f(4)

                def two(ap, j):
                    return ap[:, 2 * j:2 * j + 2, :]

                def psum(b):
                    return bank[b][:, :].rearrange("p (k t) -> p k t", k=2)

                dve.wait_ge(conv_edge, 2)
                for half in range(2):
                    at = 16 * half
                    split_block(base, at + 4)
                    split_block(base, at + 8)
                    dve.wait_ge(granule_used, base + at + 8)
                    dve.wait_ge(conv_x, half + 1)
                    for j in range(2):
                        tt = dve.tensor_tensor(two(C["t"], j)[:, :, 1:SEQ + 1], psum(2 + j), two(C["xin"], j), ALU.mult)
                    tt.then_inc(conv_t, 1)
                    split_block(base, at + 12)
                    dve.wait_ge(conv_t, half + 1)
                    for w in range(3):
                        for f in range(4):
                            kt = 4 * half + f
                            taps = CONV_K[w][:, kt:kt + 1]
                            if w == 0:
                                tap = dve.tensor_scalar(C["cv"][:, f, :], C["t"][:, f, 0:SEQ], taps, None, ALU.mult)
                            else:
                                tap = dve.scalar_tensor_tensor(C["cv"][:, f, :], C["t"][:, f, w:w + SEQ], taps, C["cv"][:, f, :], ALU.mult, ALU.add)
                        tap.then_inc(conv_tap, 1)
                        dve.wait_ge(conv_tap, 3 * half + w + 1)
                    dve.wait_ge(granule_used, base + at + 12)
                    for j in range(2):
                        yy = dve.tensor_tensor(two(C["y"], j), psum(4 + j), two(C["cv"], j), ALU.mult)
                    yy.then_inc(conv_b, 1)
                    if half == 0:
                        split_block(base, 16)
                    else:
                        split_block(STREAM["conv_out"], 0)
                    dve.wait_ge(conv_b, half + 1)
                    for j in range(2):
                        dve.wait_ge(conv_z, 2 * half + j + 1)
                        dve.tensor_tensor(two(C["y"], j), two(C["y"], j), two(C["sz"], j), ALU.mult).then_inc(conv_y, 1)
                    for j in range(2):
                        dve.wait_ge(act_hi_ready, 4 * 5 + 2 * half + j + 1)
                        dst = slice(4 * half + 2 * j, 4 * half + 2 * j + 2)
                        dve.tensor_tensor(act_lo[1][:, dst, :], two(C["y"], j), act_hi[1][:, dst, :].bitcast(F32), ALU.subtract).then_inc(act_lo_ready, 1)
                split_block(STREAM["conv_out"], 4)
                take_out("conv_out", "dil", 0, C["tmp"])

            def dilated():
                base = STREAM["dil"]
                normalise(6)
                scale_turned(6, act_f, gain[:, 1, :], f_ready, mod_col[:, 1, 0:KT])
                rest_f(6)
                with dve.Fori(0, 6) as it:
                    for n in range(2):
                        split_block(base, 4 * n + 4, it)
                        for j in range(2):
                            rope_sum(it * 4 + (8 + 2 * n + j), 2 * n + j, L["qk"][:, bass.ds(it * 8 + (4 * n + 2 * j), 2), :], L["xs"], L["rot"], rope128, BLOCK)
                for n in range(13, 16):
                    split_block(base, PER_BLOCK * n)
                split_block(STREAM["dil_out"], 0)

                units = DIL_HEADS * TILES

                def maxima(u):
                    slot = u % 2
                    dve.wait_ge(s_full, 8 + u + 1)
                    if u >= 2:
                        dve.wait_ge(p_ready, 8 + u - 1)
                    dve.tensor_reduce(LA["mx"][:, slot, 0:1], bank[2 * slot][:, :], AX.X, ALU.max)
                    dve.tensor_reduce(LA["mx"][:, slot, 1:2], bank[2 * slot + 1][:, 0:SEQ], AX.X, ALU.max).then_inc(max_ready, 1)
                    dve.wait_ge(max_ready, 8 + u + 1)
                    dve.tensor_scalar(LA["nb"][:, slot:slot + 1], LA["mx"][:, slot, 0:1], LA["mx"][:, slot, 1:2], -DIL_HD ** -0.5, ALU.max, ALU.mult).then_inc(nb_ready, 1)

                def join(u):
                    p, den, rden = LA["p"][:, u % 2], LA["den"][:, u % 2], LA["rden"][:, u % 2]
                    dve.wait_ge(p_ready, 8 + u + 1)
                    if u >= 2:
                        dve.wait_ge(o_ready, 8 + u - 1)
                    dve.tensor_tensor(p[:, 0, :], p[:, 0, :], p[:, 1, :], ALU.add)
                    dve.tensor_tensor(rden[:, 0:1], den[:, 0:1], den[:, 1:2], ALU.add).then_inc(probs_sum, 1)
                    dve.wait_ge(probs_sum, 2 * u + 1)
                    dve.reciprocal(rden[:, 1:2], rden[:, 0:1])
                    dve.tensor_tensor(p[:, 0, :], p[:, 0, :], p[:, 2, :], ALU.add).then_inc(probs_sum, 1)

                def output(u):
                    h, i, slot = u // TILES, u % TILES, u % 2
                    dve.wait_ge(o_full, 8 + u + 1)
                    dve.wait_ge(probs_sum, 2 * u + 2)
                    z = L["z"][:, i, h * P:(h + 1) * P]
                    dve.scalar_tensor_tensor(z, bank[6 + slot][:, 0:P], LA["rden"][:, slot, 1:2], z, ALU.mult, ALU.mult).then_inc(o_ready, 1)

                dve.wait_ge(vz_copied, 8)
                maxima(0)
                for u in range(units):
                    join(u)
                    if u + 1 < units:
                        maxima(u + 1)
                    if u >= 1:
                        output(u - 1)
                output(units - 1)
                rest_turned(7)
                split_block(STREAM["dil_out"], 4)
                take_out("dil_out", None, 1, LA["tmp"])

            def final_norm():
                dve.wait_ge(scale_loaded, 32)
                for i in range(TILES):
                    dve.wait_ge(rstd_ready, TILES * 7 + i + 1)
                    dve.scalar_tensor_tensor(xn[:, i, :], X[:, i, :], stat[:, 4 + i:5 + i], scale_row[:, :], ALU.mult, ALU.mult).then_inc(out_ready, 1)

            init()
            dsa()
            mlp(0, "rkv")
            rwkv_in()
            rwkv_mid()
            scan_loop()
            rwkv_out()
            mlp(1, "conv")
            mid_norm()
            conv()
            dilated()
            final_norm()

        @block.tensor
        def _(pe):
            def token_granule(g, slot, hi, lo, kts, n, banks, first, last, used=True):
                pe.wait_ge(lo_ready, g + 1)
                for i in range(TILES):
                    for kk, kt in enumerate(kts):
                        at = slice(kk * n, (kk + 1) * n)
                        x_hi, x_lo = hi[:, kt, i * P:(i + 1) * P], lo[:, kt, i * P:(i + 1) * P]
                        begin, end = first and kk == 0, last and kk == len(kts) - 1
                        dst = banks[i]
                        pe.matmul(dst, x_hi, w_hi[:, slot, at], start=begin, stop=False, skip_group_check=True)
                        pe.matmul(dst, x_hi, w_lo[:, slot, at], start=False, stop=False, skip_group_check=True)
                        mm = pe.matmul(dst, x_lo, w_hi[:, slot, at], start=False, stop=end, skip_group_check=True)
                mm.then_inc(granule_used, 1)

            def feature_granule(g, slot, hi, lo, q, banks, groups=range(4), inc=True):
                if inc:
                    pe.wait_ge(lo_ready, g + 1)
                for f in groups:
                    dst = banks[f // 2][:, (f % 2) * SEQ:(f % 2 + 1) * SEQ]
                    for kk in range(2):
                        kt = 2 * q + kk
                        at = slice(kk * BLOCK + f * P, kk * BLOCK + (f + 1) * P)
                        begin = q == 0 and kk == 0 and f % 2 == 0
                        end = q == PER_BLOCK - 1 and kk == 1
                        pe.matmul(dst, w_hi[:, slot, at], hi[:, kt, :], start=begin, stop=False, skip_group_check=True)
                        pe.matmul(dst, w_hi[:, slot, at], lo[:, kt, :], start=False, stop=False, skip_group_check=True)
                        mm = pe.matmul(dst, w_lo[:, slot, at], hi[:, kt, :], start=False, stop=end, skip_group_check=True)
                if inc:
                    mm.then_inc(granule_used, 1)
                return mm

            def token_block(base, k0, hi, lo, banks, it=None):
                for q in range(PER_BLOCK):
                    token_granule(number(base, k0 + q, it), (base + k0 + q) % RING, hi, lo, (2 * q, 2 * q + 1), BLOCK,
                                  banks, q == 0, q == PER_BLOCK - 1)

            def feature_block(base, k0, hi, lo, banks, it=None):
                for q in range(PER_BLOCK):
                    feature_granule(number(base, k0 + q, it), (base + k0 + q) % RING, hi, lo, q, banks)

            def turn(n, src, ready=None):
                for i in range(TILES):
                    if ready is not None:
                        pe.wait_ge(xn_ready, ready + i + 1)
                    for b in range(4):
                        for kk in range(2):
                            kt = 2 * b + kk
                            mm = pe.transpose(bank[4 + b][:, (kk * TILES + i) * P:(kk * TILES + i + 1) * P],
                                              src[:, i, kt * P:(kt + 1) * P], ident)
                        if i == TILES - 1:
                            mm.then_inc(turned, 1)

            def wait_act(s, q):
                pe.wait_ge(act_lo_ready, 4 * s + q + 1)

            def out_linear(name, s, u=0):
                for b in range(2):
                    for q in range(PER_BLOCK):
                        if b == 0 and s is not None:
                            wait_act(s, q)
                        g = STREAM[name] + PER_BLOCK * b + q
                        token_granule(g, g % RING, act_hi[u], act_lo[u], (2 * q, 2 * q + 1), BLOCK,
                                      (bank[2 * b][:, :], bank[2 * b + 1][:, :]), q == 0, q == PER_BLOCK - 1)

            def init():
                pe.wait_ge(const_loaded, 32)
                pe.wait_ge(rows_loaded, 16 * 14)
                pe.transpose(bank[4][:, 0:PROWS_A], S["prow_a"][:, :], ident).then_inc(rows_turned, 1)
                pe.transpose(bank[5][:, 0:PROWS_B], S["prow_b"][:, :], ident[0:PROWS_B, 0:PROWS_B]).then_inc(rows_turned, 1)
                pe.wait_ge(params_ready, 2)

            def dsa():
                base = STREAM["dsa"]
                hi, lo = act_hi[0], act_lo[0]

                def block(k0, banks):
                    for q in range(PER_BLOCK):
                        if k0 == 0:
                            wait_act(0, q)
                        feature_granule(base + k0 + q, (base + k0 + q) % RING, hi, lo, q, banks)

                turn(0, xn, 0)
                pe.wait_ge(f_ready, 4)
                pe.wait_ge(idx_w_loaded, 48)
                for kt in range(KT):
                    mm = pe.matmul(bank[4][:, 0:SEQ], S["w_ik"][:, kt, :], act_f[:, kt, :], start=kt == 0, stop=kt == KT - 1)
                mm.then_inc(idx_proj, 1)
                for i in range(TILES):
                    for kt in range(KT):
                        mm = pe.matmul(bank[5][:, i * IDX_HEADS:(i + 1) * IDX_HEADS], act_f[:, kt, i * P:(i + 1) * P],
                                       S["w_iw"][:, kt, :], start=kt == 0, stop=kt == KT - 1)
                mm.then_inc(idx_proj, 1)
                block(0, (bank[0], bank[1]))
                for q in range(PER_BLOCK):
                    g = base + 4 + q
                    slot = g % RING
                    pe.wait_ge(lo_ready, g + 1)
                    feature_granule(g, slot, hi, lo, q, (bank[2],), range(2), False)
                    for i in range(TILES):
                        for kk in range(2):
                            kt = 2 * q + kk
                            at = slice(kk * BLOCK + KV_COLS, (kk + 1) * BLOCK)
                            x_hi, x_lo = hi[:, kt, i * P:(i + 1) * P], lo[:, kt, i * P:(i + 1) * P]
                            dst = bank[3][:, i * KV_COLS:(i + 1) * KV_COLS]
                            begin, end = q == 0 and kk == 0 and i == 0, q == PER_BLOCK - 1 and kk == 1
                            pe.matmul(dst, x_hi, w_hi[:, slot, at], start=begin, stop=False, skip_group_check=True)
                            pe.matmul(dst, x_hi, w_lo[:, slot, at], start=False, stop=False, skip_group_check=True)
                            mm = pe.matmul(dst, x_lo, w_hi[:, slot, at], start=False, stop=end, skip_group_check=True)
                    mm.then_inc(granule_used, 1)
                pe.wait_ge(rope_x, 3)
                block(8, (bank[0], bank[1]))
                pe.wait_ge(wi_ready, 1)
                pe.wait_ge(rope_done, 3)
                for step in range(4):
                    i = step // 2
                    if step >= 2:
                        pe.wait_ge(idx_relu, 2 * (step - 1))
                    for j in range(2):
                        for e in range(2):
                            pair = 2 * (step % 2) + j
                            at = slice(e * HD, (e + 1) * HD)
                            mm = pe.matmul(bank[4 + 2 * (step % 2) + e][:, j * SEQ:(j + 1) * SEQ],
                                           S["qiT"][at, pair, i * P:(i + 1) * P], S["kiT"][at, :], start=True, stop=True)
                    mm.then_inc(idx_full, 1)
                pe.wait_ge(rope_x, 4)
                pe.wait_ge(v_ready, 1)
                block(12, (bank[2], bank[3]))

                units = TILES * KV_HEADS

                def logits(u):
                    i, n, slot = u // KV_HEADS, u % KV_HEADS, u % 2
                    if u >= 2:
                        pe.wait_ge(p_ready, u - 1)
                    for e in range(2):
                        pe.matmul(bank[2 * slot + e][:, :].rearrange("p (j s) -> p j s", j=2), ident_bf,
                                  S["bias"][:, i:i + 1, :].broadcast_to([P, 2, SEQ]), start=True, stop=False, skip_group_check=True)
                    for j in range(2):
                        for e in range(2):
                            at = slice(e * HD, (e + 1) * HD)
                            mm = pe.matmul(bank[2 * slot + e][:, j * SEQ:(j + 1) * SEQ],
                                           S["qT"][at, 2 * n + j, i * P:(i + 1) * P], S["kT"][at, n, :],
                                           start=False, stop=True, skip_group_check=True)
                    mm.then_inc(s_full, 1)

                def turn_probs(u):
                    pe.wait_ge(p_ready, u + 1)
                    if u >= 1:
                        pe.wait_ge(pT_ready, u)
                        pe.wait_ge(pT_ready_act, u)
                    for s in range(TILES):
                        for c in range(GROUP):
                            mm = pe.transpose(bank[4 + s][:, c * P:(c + 1) * P], S["p"][:, u % 2, c, s * P:(s + 1) * P], ident)
                        mm.then_inc(pT_full, 1)

                def values(u):
                    n, slot = u % KV_HEADS, u % 2
                    pe.wait_ge(pT_ready, u + 1)
                    pe.wait_ge(pT_ready_act, u + 1)
                    if u >= 2:
                        pe.wait_ge(o_ready, u - 1)
                    for c in range(GROUP):
                        for s in range(TILES):
                            mm = pe.matmul(bank[6 + slot][:, c * HD:(c + 1) * HD], S["pT"][:, slot, s, c * P:(c + 1) * P],
                                           S["v"][:, s, n * HD:(n + 1) * HD], start=s == 0, stop=s == TILES - 1)
                    mm.then_inc(o_full, 1)

                pe.wait_ge(rope_x, 8)
                pe.wait_ge(rope_done, 8)
                pe.wait_ge(k_spread, 1)
                pe.wait_ge(selected, TILES)
                logits(0)
                for u in range(units):
                    if u + 1 < units:
                        logits(u + 1)
                    if u >= 1:
                        values(u - 1)
                    turn_probs(u)
                values(units - 1)
                pe.wait_ge(o_ready, units)
                turn(1, S["o"])
                out_linear("dsa_out", 1)

            def mlp(l):
                base, done = STREAM[f"mlp{l}"], 2 * FF_STEPS * l
                hi, lo = act_hi[0], act_lo[0]
                turn(2 + 2 * l, xn, TILES * (1 + 2 * l))
                for q in range(PER_BLOCK):
                    wait_act(2 + l, q)
                    feature_granule(base + q, (base + q) % RING, hi, lo, q, (bank[6], bank[7]))

                def down(it, k0, slot, first, last):
                    for q in range(PER_BLOCK):
                        g, at_slot = it * 8 + (base + k0 + q), (base + k0 + q) % RING
                        pe.wait_ge(lo_ready, g + 1)
                        if q % 2 == 0:
                            pe.wait_ge(mid_lo, it * 2 + (done + q // 2 + 1))
                        for i in range(TILES):
                            x_hi, x_lo = (m[:, slot, q, i * P:(i + 1) * P] for m in (M["hi"], M["lo"]))
                            for n in range(2):
                                at = slice(n * BLOCK, (n + 1) * BLOCK)
                                dst = bank[2 + 2 * i + n][:, :]
                                pe.matmul(dst, x_hi, w_hi[:, at_slot, at], start=first and q == 0, stop=False, skip_group_check=True)
                                pe.matmul(dst, x_hi, w_lo[:, at_slot, at], start=False, stop=False, skip_group_check=True)
                                mm = pe.matmul(dst, x_lo, w_hi[:, at_slot, at], start=False, stop=last and q == PER_BLOCK - 1,
                                               skip_group_check=True)
                        mm.then_inc(granule_used, 1)

                def step(it, first):
                    if not first:
                        pe.wait_ge(up_relu, it * 2 + (done + 2))
                    feature_block(base, 4, hi, lo, (bank[0], bank[1]), it)
                    down(it, 8, 0, first, False)

                step(0, True)
                with pe.Fori(1, FF_STEPS - 1) as it:
                    step(it, False)
                down(FF_STEPS - 1, 4, 1, False, True)
                modulation(l)

            def modulation(l):
                for n in range(3):
                    pe.wait_ge(mod_used[n], KT * (l + 1))
                pe.wait_ge(up_relu, 2 * FF_STEPS * (l + 1))
                for k in range(2 * KT):
                    mm = pe.matmul(bank[7][:, k:k + 1], M["mod_all"][:, k * P:(k + 1) * P], ones[:, 0:1], start=True, stop=True)
                mm.then_inc(mod_full, 1)
                for n, b in enumerate((6, 0)):
                    at = 2 * D + n * BLOCK
                    pe.matmul(bank[b][:, :], ones, M["mod_all"][:, at:at + BLOCK], start=True, stop=True).then_inc(mod_full, 1)
                pe.wait_ge(mod_ready, 4 * (l + 1))

            def rwkv_in():
                base = STREAM["rkv"]
                turn(3, xn, 2 * TILES)

                def lora(m, names):
                    for at, width in names:
                        for kt in range(KT):
                            if at == 0 and kt % 2 == 0:
                                pe.wait_ge(mixed, 4 * (3 + m) + kt // 2 + 1)
                            mm = pe.matmul(bank[4 + m][0:width, (at > 0) * SEQ:((at > 0) + 1) * SEQ],
                                           R[("w1", "a1", "g1")[m]][:, kt, at:at + width], act_f[:, kt, :],
                                           start=kt == 0, stop=kt == KT - 1)
                    mm.then_inc(lora_full, 1)

                pe.wait_ge(lora_loaded, 16 * 6)
                for n in range(6):
                    c = n // 2
                    hi, lo, banks = act_hi[c % 2], act_lo[c % 2], (bank[2 * (n % 2)], bank[2 * (n % 2) + 1])
                    if n >= 2:
                        pe.wait_ge(rkv_copied, 2 * (n - 1))
                    for q in range(PER_BLOCK):
                        if n % 2 == 0:
                            pe.wait_ge(mix_lo, 4 * c + q + 1)
                        g = base + PER_BLOCK * n + q
                        if c < 2:
                            feature_granule(g, g % RING, hi, lo, q, banks)
                        else:
                            token_granule(g, g % RING, hi, lo, (2 * q, 2 * q + 1), BLOCK, (banks[0][:, :], banks[1][:, :]),
                                          q == 0, q == PER_BLOCK - 1)
                    if n == 3:
                        lora(0, ((0, LORA),))
                    if n == 4:
                        lora(1, ((0, LORA),))
                lora(2, ((0, P), (P, GLORA - P)))

            def rwkv_mid():
                pe.wait_ge(mid_ready, 3)
                pe.wait_ge(rkv_copied, 12)
                for b in range(8):
                    for j in range(2):
                        pair = 2 * (b % 4) + j
                        mm = pe.matmul(bank[b][:, j * SEQ:(j + 1) * SEQ], R["w2" if b < 4 else "a2"][:, pair * P:(pair + 1) * P],
                                       R["mid"][0:LORA, b // 4, :], start=True, stop=True)
                    mm.then_inc(lora2_full, 1)

                def head_sums(b, values, of):
                    for pair in range(PAIRS):
                        mm = pe.matmul(bank[b][0:HEADS, 0:SEQ], of[:, pair, :], values[:, pair, :], start=pair == 0, stop=pair == PAIRS - 1)
                    return mm

                pe.wait_ge(lora2_ready, 8)
                pe.wait_ge(rw_act, 1)
                head_sums(0, R["pinv"], head_of).then_inc(rw_pe, 1)
                pe.wait_ge(rw_inverse, 1)
                for b in range(4):
                    spread(4 + b, root_head).then_inc(rw_pe, 1)
                pe.wait_ge(rw_dve, 7)
                head_sums(1, R["pinv"], head_rk).then_inc(rw_pe, 1)

            def spread(b, rows, first=None):
                first = 2 * (b % 4)
                for j in range(2):
                    mm = pe.matmul(bank[b][:, j * SEQ:(j + 1) * SEQ], R["rows_of"][:, first + j, :], rows[0:HEADS, :], start=True, stop=True)
                return mm

            def scan_loop():
                known = iter(range(1, SCAN_PE + 1))
                with pe.Fori(0, PAIRS // 2) as it:
                    def of(sem_, per, n):
                        pe.wait_ge(sem_, it * per + n)

                    def before(sem_, per, n):
                        value = pe.to_reg(it * per + n)
                        pe.wait_ge(hi_ready, next(known))
                        pe.wait_ge(sem_, value)

                    halves = [slice(0, CHUNK), slice(CHUNK, P)]

                    def each(steps):
                        for m in range(4):
                            for at in halves:
                                for b, col, left, right in steps:
                                    mm = pe.matmul(bank[b][at, (4 * col + m) * CHUNK:(4 * col + m + 1) * CHUNK],
                                                   left(at, m), right(at, m), start=True, stop=True)
                        return mm

                    def inv(u, a):
                        return lambda at, m: scan["inv"][u][at, a, m, :]

                    def off(u, a):
                        return lambda at, m: scan["off"][u][at, a, m, :]

                    Q, QT, M, N = range(4)
                    for u in range(2):
                        B, prod = 4 * u, scan["prod"][u]
                        of(sc_act, SCAN_ACT, 1)
                        of(sc_dve, SCAN_DVE, 2 + u)
                        for k, (b, col) in ((0, (0, 0)), (2, (0, 2)), (3, (1, 0))):
                            for i in range(TILES):
                                mm = pe.transpose(bank[B + b][:, (col + i) * P:(col + i + 1) * P], prod[:, k, i * P:(i + 1) * P], ident)
                        mm.then_inc(sc_pe, 1)
                        for i in range(TILES):
                            for par, to in enumerate(halves):
                                c = slice((2 * i + par) * CHUNK, (2 * i + par + 1) * CHUNK)
                                for k in range(2):
                                    for h, rows in enumerate(halves):
                                        mm = pe.matmul(bank[B + 2 + h][to, (2 * i + k) * P:(2 * i + k + 1) * P].rearrange("p (a t) -> p a t", a=2),
                                                       prod[rows, 2 + k, c], prod[rows, 0:2, c], start=True, stop=True)
                        mm.then_inc(sc_pe, 1)
                    for u in range(2):
                        B = 4 * u
                        of(sc_dve, SCAN_DVE, 6 + 3 * u)
                        of(sc_act, SCAN_ACT, 2 + u)
                        before(sc_pool, 2, u + 1)
                        eye = lambda at, m: unit[at, :]
                        each([(B, 0, inv(u, Q), eye), (B, 1, inv(u, N), eye),
                              (B + 1, 0, lambda at, m: scan["att"][u][at, m // 2, m % 2, 2, :],
                               lambda at, m: R["vst"][at, u, m % 2, m // 2 * RN:(m // 2 + 1) * RN])]).then_inc(sc_pe, 1)

                    def squares(u, b):
                        return [(b, 0, inv(u, N), inv(u, M)), (b, 1, inv(u, M), inv(u, N))]

                    def inverses(u, b):
                        return [(b, 0, inv(u, M), inv(u, Q)), (b, 1, inv(u, N), inv(u, QT))]

                    def step(scalar, vector, steps):
                        for u in range(2):
                            if scalar and vector:
                                of(sc_act, SCAN_ACT, 1 + scalar + u)
                            before(*((sc_dve, SCAN_DVE, 1 + vector + u) if vector else (sc_act, SCAN_ACT, 1 + scalar + u)))
                            each(steps(u, 4 * u)).then_inc(sc_pe, 1)

                    step(3, None, lambda u, B: squares(u, B + 2))
                    step(5, None, lambda u, B: inverses(u, B + 3) + squares(u, B))
                    step(7, 9, lambda u, B: inverses(u, B + 2) + squares(u, B + 1))
                    step(9, 11, lambda u, B: inverses(u, B + 3))
                    step(None, 13, lambda u, B: [(B, 0, off(u, 0), inv(u, QT))])
                    step(11, None, lambda u, B: [(B + 2, 0, inv(u, M), inv(u, Q)), (B + 2, 1, inv(u, Q), inv(u, M))])
                    step(None, 15, lambda u, B: [(B + 1, 0, off(u, 1), inv(u, QT))])
                    step(13, None, lambda u, B: [(B + 3, 0, inv(u, M), inv(u, Q))])
                    for u in range(2):
                        before(sc_dve, SCAN_DVE, 18 + u)
                        for m in range(4):
                            for at in halves:
                                mm = pe.matmul(bank[4 * u][at, m * P:(m + 1) * P].rearrange("p (a t) -> p a t", a=2),
                                               scan["inv"][u][at, Q, m, :], scan["aw"][u][at, m, :, :], start=True, stop=True)
                        mm.then_inc(sc_pe, 1)
                    for u in range(2):
                        zz, tok, att = scan["zz"][u], scan["tok"][u], scan["att"][u]
                        before(sc_act, SCAN_ACT, 16 + u)
                        for i in range(TILES):
                            for h, to in enumerate(halves):
                                for par, at in enumerate(halves):
                                    m, own, out_ = 2 * h + i, bank[4 * u + par], bank[4 * u + 2 + par]
                                    beta, kappa = (tok[at, k, i, h * RN:(h + 1) * RN] for k in range(2))
                                    val = R["vst"][at, u, i, h * RN:(h + 1) * RN]
                                    removed, none = zz[at, m, 0, :], zz[at, m, 1, :]
                                    transition, queries, state_in = (own[to, k * P + i * RN:k * P + (i + 1) * RN] for k in range(3))
                                    outputs = out_[to, i * RN:(i + 1) * RN]
                                    pe.matmul(transition, removed, beta, start=True, stop=True)
                                    pe.matmul(queries, removed, att[at, h, i, 1, :], start=True, stop=True)
                                    pe.matmul(state_in, beta, none, start=True, stop=False)
                                    pe.matmul(state_in, kappa, val, start=False, stop=True)
                                    pe.matmul(outputs, none, att[at, h, i, 1, :], start=True, stop=False)
                                    mm = pe.matmul(outputs, val, att[at, h, i, 3, :], start=False, stop=True)
                        mm.then_inc(sc_pe, 1)

            def rwkv_out():
                halves = [slice(0, RN), slice(RN, P)]

                def chunk_products(b, left, right):
                    for pair in range(PAIRS):
                        for at in halves:
                            mm = pe.matmul(bank[b][at, pair * RN:(pair + 1) * RN], left(at, pair), right(at, pair), start=True, stop=True)
                    return mm

                def chunk(t, c):
                    return lambda at, pair: t[at, pair, c * CHUNK:(c + 1) * CHUNK]

                def states(c):
                    return chunk(R["pinv"], 0) if c == 1 else lambda at, pair: state[at, c - 2, pair, :]

                pe.wait_ge(sc_dve, 1 + SCAN_DVE * (PAIRS // 2))
                pe.wait_ge(sc_act, 1 + SCAN_ACT * (PAIRS // 2))
                for c in range(1, CHUNKS):
                    if c > 1:
                        pe.wait_ge(chain_ready, c - 1)
                    if c < CHUNKS - 1:
                        chunk_products(c - 1, chunk(R["sg"], c), states(c)).then_inc(chain_full, 1)
                    if c > 2:
                        pe.wait_ge(y_ready, c - 2)
                    chunk_products(2 + c % 2, states(c), chunk(R["rT"], c)).then_inc(y_full, 1)
                    if c == 1:
                        for b in range(4):
                            for j in range(2):
                                for i in range(TILES):
                                    pair = 2 * b + j
                                    mm = pe.transpose(bank[4 + b][:, (TILES * j + i) * P:(TILES * j + i + 1) * P], R["v"][:, i, pair * P:(pair + 1) * P], ident)
                            mm.then_inc(vT_full, 1)
                pe.wait_ge(g2_loaded, 32)
                for b in range(4):
                    pe.wait_ge(vT_ready, b + 1)
                    for j in range(2):
                        at, dst = slice((2 * b + j) * P, (2 * b + j + 1) * P), bank[4 + b][:, j * SEQ:(j + 1) * SEQ]
                        pe.matmul(dst, R["g2a"][:, at], R["mid"][:, 2, :], start=True, stop=False)
                        mm = pe.matmul(dst, R["g2b"][:, at], R["mid"][0:GLORA - P, 3, :], start=False, stop=True)
                    mm.then_inc(glora_full, 1)
                pe.wait_ge(y_ready, CHUNKS - 1)
                for b in range(4):
                    spread(b, R["mid"][:, 0, :]).then_inc(bonus_full, 1)
                for b in range(4):
                    pe.wait_ge(glora_ready, b + 1)
                    pe.matmul(bank[4 + b][:, :], view["head_mean"], R["cum"][:, 2 * b:2 * b + 2, :], start=True, stop=True).then_inc(mean_full, 1)
                pe.wait_ge(centred, 4)
                for pair in range(PAIRS):
                    if pair % 2 == 0:
                        pe.wait_ge(dev_sq, pair // 2 + 1)
                    mm = pe.matmul(bank[4][0:HEADS, 0:SEQ], head_of[:, pair, :], R["pinv"][:, pair, :], start=pair == 0, stop=pair == PAIRS - 1)
                mm.then_inc(var_full, 1)
                pe.wait_ge(rw_inverse, 2)
                for b in range(4):
                    spread(4 + b, root_head).then_inc(spread_full, 1)
                for n in range(2):
                    for q in range(PER_BLOCK):
                        if n == 0:
                            pe.wait_ge(mix_lo, 12 + q + 1)
                        g = STREAM["rwkv_out"] + PER_BLOCK * n + q
                        token_granule(g, g % RING, act_hi[0], act_lo[0], (2 * q, 2 * q + 1), BLOCK,
                                      (bank[2 * n][:, :], bank[2 * n + 1][:, :]), q == 0, q == PER_BLOCK - 1)

            def conv():
                base = STREAM["conv"]
                hi, lo = act_hi[0], act_lo[0]
                turn(5, xn, 4 * TILES)
                for half in range(2):
                    for n, (left, count) in enumerate(((conv_x, 1), (conv_t, 1), (conv_b, 1), (conv_z, 2))):
                        if half:
                            pe.wait_ge(left, count)
                        for q in range(PER_BLOCK):
                            if n == half == 0:
                                wait_act(4, q)
                            g = base + 16 * half + 4 * n + q
                            feature_granule(g, g % RING, hi, lo, q, (bank[2 * n], bank[2 * n + 1]))
                pe.wait_ge(conv_x, 2)
                pe.wait_ge(conv_t, 2)
                out_linear("conv_out", 5, 1)

            def dilated():
                base = STREAM["dil"]
                hi, lo = act_hi[0], act_lo[0]
                turn(6, xn, 5 * TILES)
                for q in range(PER_BLOCK):
                    wait_act(6, q)
                with pe.Fori(0, 6) as it:
                    for n in range(2):
                        pe.wait_ge(rope_x, it * 4 + (6 + 2 * n))
                        feature_block(base, 4 * n, hi, lo, (bank[2 * n], bank[2 * n + 1]), it)
                for n in range(4):
                    if n < 2:
                        pe.wait_ge(rope_x, 30 + 2 * n)
                    else:
                        pe.wait_ge(vz_copied, 2 * (n - 1))
                    token_block(base, PER_BLOCK * (12 + n), hi, lo, [bank[2 * (n % 2) + i][:, :] for i in range(TILES)])

                units = DIL_HEADS * TILES

                def logits(u):
                    h, i, slot = u // TILES, u % TILES, u % 2
                    if u >= 2:
                        pe.wait_ge(p_ready, 8 + u - 1)
                    pe.matmul(bank[2 * slot][:, :].rearrange("p (g s) -> p g s", g=2), ident_bf, dil_mask[:, i, 0:2, :], start=True, stop=False, skip_group_check=True)
                    pe.matmul(bank[2 * slot + 1][:, 0:SEQ], ident_bf, dil_mask[:, i, 2, :], start=True, stop=False, skip_group_check=True)
                    for g in range(DIL_GROUPS):
                        q = g * DIL_HEADS + h
                        mm = pe.matmul(bank[2 * slot + g // 2][:, g % 2 * SEQ:(g % 2 + 1) * SEQ], L["qk"][:, q, i * P:(i + 1) * P],
                                       L["qk"][:, DIL_GROUPS * DIL_HEADS + q, :], start=False, stop=True, skip_group_check=True)
                    mm.then_inc(s_full, 1)

                def turn_probs(u):
                    pe.wait_ge(probs_sum, 2 * u + 2)
                    if u >= 2:
                        pe.wait_ge(pT_ready_act, 8 + u - 1)
                    for s in range(TILES):
                        mm = pe.transpose(bank[4 + u % 2][:, s * P:(s + 1) * P], LA["p"][:, u % 2, 0, s * P:(s + 1) * P], ident)
                    mm.then_inc(pT_full, 1)

                def values(u):
                    h, slot = u // TILES, u % 2
                    pe.wait_ge(pT_ready_act, 8 + u + 1)
                    if u >= 2:
                        pe.wait_ge(o_ready, 8 + u - 1)
                    for s in range(TILES):
                        mm = pe.matmul(bank[6 + slot][:, 0:P], LA["pT"][:, slot, s, :], L["v"][:, s, h * P:(h + 1) * P], start=s == 0, stop=s == TILES - 1)
                    mm.then_inc(o_full, 1)

                pe.wait_ge(vz_copied, 8)
                pe.wait_ge(rope_done, 32)
                logits(0)
                for u in range(units):
                    if u + 1 < units:
                        logits(u + 1)
                    if u >= 1:
                        values(u - 1)
                    turn_probs(u)
                values(units - 1)
                pe.wait_ge(o_ready, 8 + units)
                turn(7, L["z"])
                out_linear("dil_out", 7)

            init()
            dsa()
            mlp(0)
            rwkv_in()
            rwkv_mid()
            scan_loop()
            rwkv_out()
            mlp(1)
            conv()
            dilated()


def kernel(**inputs):
    import ml_dtypes
    from concourse import bacc as _bacc
    from concourse.bass_utils import run_bass_kernel_spmd

    parts, rows_of, parts_bf = shape_constants()
    arrays = {name: np.asarray(value) for name, value in inputs.items() if np.size(value)}
    arrays["const"] = np.concatenate([v.reshape(P, -1) for v in parts.values()], 1)
    arrays["const_bf"] = np.concatenate([v.reshape(P, -1) for v in parts_bf.values()], 1).astype(ml_dtypes.bfloat16)
    arrays["rows_of"] = rows_of[:HEADS].reshape(HEADS, -1)
    nc = _bacc.Bacc("TRN2", target_bir_lowering=False, num_devices=1)
    A = {name: nc.dram_tensor(f"in_{name}_dram", value.shape, mybir.dt.from_np(value.dtype), kind="ExternalInput").ap()
         for name, value in arrays.items()}
    out = nc.dram_tensor("out_dram", (1, SEQ, D), F32, kind="ExternalOutput").ap()
    program(nc, A, out)
    feed = {f"in_{name}_dram": value for name, value in arrays.items()}
    result = run_bass_kernel_spmd(nc, [feed], core_ids=[0])
    return np.asarray(result.results[0]["out_dram"])
```

```python
from contextlib import ExitStack

import numpy as np

import concourse.bass as bass
from concourse import mybir

F32 = mybir.dt.float32
F32R = mybir.dt.float32r
BF16 = mybir.dt.bfloat16
ACT = mybir.ActivationFunctionType
ALU = mybir.AluOpType
AX = mybir.AxisListType

P = 128
SEQ = 256
TILES = SEQ // P
D = 1024
KT = D // P
EPS = 1e-6
ROPE_THETA = 10000.0
NEG = -1e30
TAKEN = -2e30

GRAN = 1024
BLOCK = 512
PER_BLOCK = 4
RING = 4

HEADS, KV_HEADS, HD = 16, 4, 64
GROUP = HEADS // KV_HEADS
IDX_HEADS = 8
TOPK = SEQ // 4
Q_COLS = HEADS * HD
KV_COLS = KV_HEADS * HD
IQ_COLS = IDX_HEADS * HD
OFF_K = Q_COLS
OFF_V = OFF_K + KV_COLS
OFF_IQ = OFF_V + KV_COLS
OFF_IK = OFF_IQ + IQ_COLS
OFF_IW = OFF_IK + HD
IDX_SCALE = IDX_HEADS ** -0.5 * HD ** -0.5

FF = 4 * D
FF_STEPS = FF // BLOCK

RN = 64
PAIRS = D // P
CHUNK = 64
CHUNKS = SEQ // CHUNK
DECAY_SCALE = -float(np.exp(-0.5))
LNX_EPS = 64e-5
LORA, GLORA = 64, 160

DIL_HEADS, DIL_HD, DIL_GROUPS = 8, 128, 3
DIL_RATES, DIL_HALF = (1, 4, 16), (64, 64, 64)

STREAM = {}
_at = 0
for _name, _blocks in (("dsa", 4), ("dsa_out", 2), ("mlp0", 16), ("rkv", 6), ("rwkv_out", 2), ("mlp1", 16),
                       ("conv", 8), ("conv_out", 2), ("dil", 16), ("dil_out", 2)):
    STREAM[_name] = _at
    _at += _blocks * PER_BLOCK


def rope_rows(dim, rows):
    inv = (1.0 / (np.float32(ROPE_THETA) ** (np.arange(0, dim, 2, dtype=np.float32) / np.float32(dim)))).astype(np.float32)
    ang = np.arange(SEQ, dtype=np.float32)[None, :] * inv[:, None]
    cos, sin = np.cos(ang), np.sin(ang)
    both = np.stack([np.concatenate([cos, cos]), np.concatenate([-sin, sin])], 1)
    return np.tile(both, (rows // dim, 1, 1)).astype(np.float32)


def shape_constants():
    p = np.arange(P)
    t = np.arange(SEQ)
    ident = np.eye(P, dtype=np.float32)
    row = p[:, None] % CHUNK
    col = np.arange(CHUNK)[None, :]
    strict, incl = (row < col).astype(np.float32), (row <= col).astype(np.float32)
    scan_mask = np.concatenate([strict, incl], 1)
    block16, block32 = (row // 16 == col // 16), (row // 32 == col // 32)
    split_mask = np.concatenate([block16, block32 & ~block16, ~block32], 1).astype(np.float32)
    head_mean = np.kron(np.eye(2), np.full((RN, RN), 1.0 / RN)).astype(np.float32)
    head_of = np.zeros((P, PAIRS, HEADS), np.float32)
    for pair in range(PAIRS):
        for h in range(2):
            head_of[h * RN:(h + 1) * RN, pair, 2 * pair + h] = 1.0
    rows_of = np.zeros((P, PAIRS, P), np.float32)
    rows_of[:HEADS] = head_of.transpose(2, 1, 0)
    parts = {
        "ident": ident,
        "rope64": rope_rows(HD, P),
        "rope128": rope_rows(DIL_HD, P),
        "unit": (row == col).astype(np.float32),
        "scan_mask": scan_mask,
        "split_mask": split_mask,
        "head_mean": head_mean,
        "keep": np.tile((t % CHUNK != 0).astype(np.float32), (P, 1)),
        "head_of": head_of,
        "ones": np.ones((P, P), np.float32),
    }
    causal = np.where(t[None, None, :] <= (p[:, None, None] + P * np.arange(TILES)[None, :, None]), 0.0, NEG)
    dil = np.zeros((P, TILES, DIL_GROUPS, SEQ))
    for i in range(TILES):
        for g in range(DIL_GROUPS):
            q, k, r = p[:, None] + P * i, t[None, :], DIL_RATES[g]
            seen = ((q - k) % r == 0) & (np.abs(q - k) <= DIL_HALF[g] * r)
            dil[:, i, g] = np.where(seen, 0.0, NEG)
    parts_bf = {"ident_bf": ident, "causal": causal, "dil_mask": dil}
    return parts, rows_of, parts_bf


def program(nc, A, out):
    parts, _, parts_bf = shape_constants()
    with ExitStack() as keep:
        def sem(name):
            return keep.enter_context(nc.semaphore(name))

        def room(stack):
            return lambda name, shape, dt=F32: stack.enter_context(nc.sbuf_tensor(name, shape, dt))

        sb = room(keep)
        bank = [keep.enter_context(nc.psum_tensor(f"bank{b}", [P, BLOCK], F32)) for b in range(8)]

        raw = sb("raw", [P, RING, GRAN])
        w_hi = sb("w_hi", [P, RING, GRAN], F32R)
        w_lo = sb("w_lo", [P, RING, GRAN], F32R)
        X = sb("X", [P, TILES, D])
        n_const = sum(int(np.prod(v.shape[1:])) for v in parts.values())
        n_const_bf = sum(int(np.prod(v.shape[1:])) for v in parts_bf.values())
        const = sb("const", [P, n_const])
        const_bf = sb("const_bf", [P, n_const_bf], BF16)
        gate = sb("gate", [P, 2, D])
        scale_row = sb("scale_row", [P, D])
        PROWS_A, PROWS_B = 128, 104
        pcol = sb("pcol", [P, PROWS_A + PROWS_B])
        mod_col = sb("mod_col", [P, 2, 2 * KT])
        gain = sb("gain", [P, 2, KT])
        c_col = sb("c_col", [P, KT])
        stat = sb("stat", [P, 8])
        half_neg = sb("half_neg", [P, SEQ])
        per_head = sb("per_head", [HEADS, SEQ])
        root_head = sb("root_head", [HEADS, SEQ])
        head_rk = sb("head_rk", [P, PAIRS, HEADS])

        view, at = {}, 0
        for name, v in parts.items():
            n = int(np.prod(v.shape[1:]))
            view[name] = const[:, at:at + n]
            at += n
        at = 0
        for name, v in parts_bf.items():
            n = int(np.prod(v.shape[1:]))
            view[name] = const_bf[:, at:at + n]
            at += n
        ident, ident_bf, ones, unit = view["ident"], view["ident_bf"], view["ones"], view["unit"]
        rope64 = view["rope64"].rearrange("p (a t) -> p a t", a=2)
        rope128 = view["rope128"].rearrange("p (a t) -> p a t", a=2)
        causal = view["causal"].rearrange("p (i s) -> p i s", i=TILES)
        dil_mask = view["dil_mask"].rearrange("p (i g s) -> p i g s", i=TILES, g=DIL_GROUPS)
        scan_mask = view["scan_mask"].rearrange("p (m t) -> p m t", m=2)
        split_mask = view["split_mask"].rearrange("p (m t) -> p m t", m=3)
        head_of = view["head_of"].rearrange("p (a h) -> p a h", a=PAIRS)

        def scope(plan):
            with ExitStack() as s:
                return plan(room(s))

        def scan_plan(t):
            return dict(
                prod=[t(f"prod{u}", [P, CHUNKS, 2, 2, CHUNK]) for u in range(2)],
                bk=[t(f"bk{u}", [P, CHUNKS, 2, CHUNK]) for u in range(2)],
                tok=[t(f"tok{u}", [P, CHUNKS, P]) for u in range(2)],
                aw=[t(f"aw{u}", [P, CHUNKS, 2, CHUNK]) for u in range(2)],
                att=[t(f"att{u}", [P, 8, 2, CHUNK]) for u in range(2)],
                zz=[t(f"zz{u}", [P, 8, 2, CHUNK]) for u in range(2)],
                n=[t(f"n{u}", [P, CHUNKS, P]) for u in range(2)],
            )

        def xn_plan(t):
            t("xn_under", [P, 3 * KT * SEQ])
            return t("xn", [P, TILES, D])

        scan = scope(scan_plan)
        state = scan["prod"][0][:, :, :, :, :].rearrange("p c a h n -> p (c a h) n").rearrange("p (s a) n -> p s a n", s=2)
        xn = scope(xn_plan)
        act_f = sb("act_f", [P, KT, SEQ])
        act_hi, act_lo = [], []
        for u in range(2):
            act_hi.append(sb(f"act_hi{u}", [P, KT, SEQ], F32R))
            act_lo.append(sb(f"act_lo{u}", [P, KT, SEQ], F32R))

        def dsa_plan(t):
            return dict(
                qT=t("qT", [P, HEADS // 2, SEQ]), kT=t("kT", [P, KV_HEADS, SEQ]),
                k_rot=t("k_rot", [P, 2, SEQ]),
                qiT=t("qiT", [P, IDX_HEADS // 2, SEQ]), kiT=t("kiT", [P, SEQ]),
                v=t("v", [P, TILES, KV_COLS]), wi=t("wi", [P, TILES, IDX_HEADS]),
                xs=t("xs", [P, 2, BLOCK]), rot=t("rot", [P, 2, BLOCK]),
                relu=t("relu", [P, 4, BLOCK]), score=t("score", [P, TILES, SEQ]),
                top8=t("top8", [P, TILES, 8]), bias=t("sel_bias", [P, TILES, SEQ], BF16),
                p=t("probs", [P, 2, GROUP, SEQ]), pT=t("probsT", [P, 2, TILES, BLOCK]),
                mx=t("mx", [P, 2, GROUP]), nb=t("nb", [P, 2, GROUP]), den=t("den", [P, 2, GROUP]),
                rden=t("rden", [P, 2, GROUP]), o=t("o_dsa", [P, TILES, D]),
                w_ik=t("w_ik", [P, KT, 2 * HD]), w_iw=t("w_iw", [P, KT, IDX_HEADS]),
                prow_a=t("prow_a", [PROWS_A, P]), prow_b=t("prow_b", [PROWS_B, P]),
            )

        def mlp_plan(t):
            return dict(relu=t("ff_relu", [P, 2, BLOCK]), sq=t("ff_sq", [P, 2, BLOCK]),
                        mod_w=t("mod_w", [P, 3, D]),
                        mod_all=t("mod_all", [P, 3 * D]),
                        hi=t("ff_hi", [P, 2, 4, SEQ], F32R), lo=t("ff_lo", [P, 2, 4, SEQ], F32R))

        def rwkv_plan(t):
            with ExitStack() as s:
                tt = room(s)
                over = dict(rT=tt("rT", [P, PAIRS, SEQ]), kT=tt("kT_r", [P, PAIRS, SEQ]),
                            v_inv=tt("v_inv", [P, CHUNKS, D]), rows_of=tt("rows_of", [HEADS, PAIRS, P]),
                            mid=tt("mid", [P, 4, SEQ]), pc=tt("pc", [P, PAIRS, CHUNKS]))
                over["v"] = over["v_inv"][:, 0:2, :].rearrange("p a n -> p (a n)").rearrange("p (c n) -> p c n", c=CHUNKS)
                over["inv"] = [over["v_inv"][:, 2 + u, :].rearrange("p (a c t) -> p a c t", a=2, c=CHUNKS) for u in range(2)]
                with ExitStack() as s2:
                    t2 = room(s2)
                    over.update(hT=t2("hT", [P, KT, SEQ + 1]), xx=t2("xx", [P, KT, SEQ]),
                                w1=t2("w1", [P, KT, LORA]), a1=t2("a1", [P, KT, LORA]),
                                g1=t2("g1", [P, KT, GLORA]), w2=t2("w2", [LORA, D]), a2=t2("a2", [LORA, D]))
                with ExitStack() as s2:
                    t2 = room(s2)
                    for n in ("sg", "a", "cum", "pinv", "kk"):
                        over[n] = t2(n, [P, PAIRS, SEQ])
                over["g2a"] = over["kk"][:, 0:4, :].rearrange("p a t -> p (a t)")
                over["g2b"] = over["kk"][0:GLORA - P, 4:8, :].rearrange("p a t -> p (a t)")
                return over

        def conv_plan(t):
            return dict(xin=t("xin", [P, 4, SEQ]), t=t("tpad", [P, 4, SEQ + 2]), cv=t("cv", [P, 4, SEQ]),
                        sz=t("sz", [P, 4, SEQ]), y=t("y_conv", [P, 4, SEQ]),
                        tmp=t("gated_conv", [P, 2, BLOCK]))

        def dil_plan(t):
            return dict(qk=t("qk", [P, 2 * DIL_GROUPS * DIL_HEADS, SEQ]), v=t("v_dil", [P, TILES, D]),
                        z=t("z_dil", [P, TILES, D]), xs=t("xs_d", [P, 2, BLOCK]), rot=t("rot_d", [P, 2, BLOCK]))

        def dil_att_plan(t):
            t("dil_under", [P, 64 * SEQ])
            return dict(p=t("p_dil", [P, 2, DIL_GROUPS, SEQ]), pT=t("pT_dil", [P, 2, TILES, P]),
                        mx=t("mx_d", [P, 2, 2]), nb=t("nb_d", [P, 2]), den=t("den_d", [P, 2, 2]), rden=t("rden_d", [P, 2, 2]),
                        tmp=t("gated_dil", [P, 2, BLOCK]))

        S = scope(dsa_plan)
        M = scope(mlp_plan)
        R = scope(rwkv_plan)
        C = scope(conv_plan)
        L = scope(dil_plan)
        LA = scope(dil_att_plan)

        def column(first, n=KT):
            return pcol[:, first:first + n]

        MIXER = [column(KT * l) for l in range(2)]
        MLPN = [column(16 + KT * l) for l in range(2)]
        NORM2 = [column(32 + KT * l) for l in range(2)]
        MU = [column(48 + KT * c) for c in range(6)]
        CONV_K = [column(96 + KT * w) for w in range(3)]
        COND = column(120)
        B_MOD = [column(PROWS_A + 24 * l, 16) for l in range(2)]
        W0, A0, K_K, K_A, R_K, LNX_W, LNX_B = (column(PROWS_A + 48 + KT * n) for n in range(7))

        loaded = [sem(f"granule_loaded{s}") for s in range(RING)]
        hi_ready, lo_ready, granule_used = sem("hi_ready"), sem("lo_ready"), sem("granule_used")
        x_loaded, rows_loaded, const_loaded = sem("x_loaded"), sem("rows_loaded"), sem("const_loaded")
        idx_w_loaded, lora_loaded, g2_loaded = sem("idx_w_loaded"), sem("lora_loaded"), sem("g2_loaded")
        scale_loaded, gate_loaded = sem("scale_loaded"), sem("gate_bias_loaded")
        half_ready = sem("half_ready")
        rows_turned, params_ready, cond_ready = sem("rows_turned"), sem("params_ready"), sem("cond_ready")
        squared, rstd_ready, rstd_step = sem("squared"), sem("rstd_ready"), sem("rstd_step")
        xn_ready, turned, f_ready = sem("xn_ready"), sem("turned"), sem("f_ready")
        act_hi_ready, act_lo_ready = sem("act_hi_ready"), sem("act_lo_ready")
        x_updated, x_step = sem("x_updated"), sem("x_step")
        idx_proj = sem("idx_proj")
        rope_x, rope_step, rope_done = sem("rope_x"), sem("rope_step"), sem("rope_done")
        k_spread, v_ready, wi_ready = sem("k_spread"), sem("v_ready"), sem("wi_ready")
        idx_full, idx_relu, scored, top_step, selected = (sem(n) for n in ("idx_full", "idx_relu", "scored", "top_step", "selected"))
        s_full, max_ready, nb_ready, p_ready = sem("s_full"), sem("max_ready"), sem("nb_ready"), sem("p_ready")
        pT_full, pT_ready, pT_ready_act, o_full, rden_ready, o_ready = (sem(n) for n in ("pT_full", "pT_ready", "pT_ready_act", "o_full", "rden_ready", "o_ready"))
        mod_loaded, mod_scaled, mod_used = ([sem(f"mod_{w}{n}") for n in range(3)] for w in ("loaded", "scaled", "used"))
        mod_full, mod_ready = sem("mod_full"), sem("mod_ready")
        up_relu, up_sq, mid_hi, mid_lo = sem("up_relu"), sem("up_sq"), sem("mid_hi"), sem("mid_lo")
        ff_opened = sem("ff_opened")
        hT_edge, shifted, mixed, mix_hi, mix_lo = (sem(n) for n in ("hT_edge", "shifted", "mixed", "mix_hi", "mix_lo"))
        rkv_copied = sem("rkv_copied")
        lora_full, mid_ready, lora2_full, lora2_ready = (sem(n) for n in ("lora_full", "mid_ready", "lora2_full", "lora2_ready"))
        rw_pe, rw_act, rw_dve, rw_root, rw_inverse = (sem(n) for n in ("rwkv_products", "rwkv_scalar", "rwkv_vector", "rwkv_root", "rwkv_inverse"))
        hT_ready = sem("hT_ready")
        chain_full, chain_scaled, chain_ready, y_full, y_ready = (sem(n) for n in ("chain_full", "chain_scaled", "chain_ready", "y_full", "y_ready"))
        vT_full, vT_ready, glora_full, glora_ready = (sem(n) for n in ("vT_full", "vT_ready", "glora_full", "glora_ready"))
        mean_full, centred, dev_sq, var_full, var_ready = (sem(n) for n in ("mean_full", "centred", "dev_sq", "var_full", "var_ready"))
        spread_full, normed, lnx_ready, bonus_full, out_step, mixer_out = (sem(n) for n in ("spread_full", "normed", "lnx_ready", "bonus_full", "out_step", "mixer_out"))
        sc_zero = sem("scan_zeros")
        sc_pe, sc_act, sc_dve, sc_pool, sc_prod = sem("scan_products"), sem("scan_scalar"), sem("scan_vector"), sem("scan_pool"), sem("scan_operands")
        conv_x, conv_t, conv_b, conv_z = (sem(n) for n in ("conv_x", "conv_t", "conv_b", "conv_z"))
        conv_edge, conv_tap, conv_y = sem("conv_edge"), sem("conv_tap"), sem("conv_y")
        vz_copied, probs_sum = sem("vz_copied"), sem("probs_sum")
        out_ready, stored = sem("out_ready"), sem("stored")

        SCAN_PE, SCAN_DVE, SCAN_ACT, SCAN_BASE, SCAN_TURNS = 30, 24, 22, 2, PAIRS // 2

        block = keep.enter_context(nc.Block())

        def number(base, k, it, turn=8):
            return base + k if it is None else it * turn + (base + k)

        @block.sync
        def _(sp):
            def load(base, k, src, it=None, turn=8):
                g, slot = number(base, k, it, turn), (base + k) % RING
                if it is not None or g >= RING:
                    sp.wait_ge(lo_ready, g - RING + 1)
                dst = raw[:, slot, :]
                if len(src.shape) == 3:
                    dst = dst.rearrange("p (k n) -> p k n", k=src.shape[1])
                sp.dma_start(dst, src).then_inc(loaded[slot], 16)

            def columns(w):
                return w.rearrange("(k p) (b n) -> p k b n", p=P, n=BLOCK)

            def load_out(name, w):
                for n in range(2):
                    for q in range(PER_BLOCK):
                        load(STREAM[name], PER_BLOCK * n + q, columns(w)[:, 2 * q:2 * q + 2, n, :])

            def load_dsa():
                w = A["dsa_w_in"][0].rearrange("(k p) n -> p k n", p=P)
                for n, first in enumerate((OFF_IQ, OFF_K, 0, BLOCK)):
                    for q in range(PER_BLOCK):
                        load(STREAM["dsa"], PER_BLOCK * n + q, w[:, 2 * q:2 * q + 2, first:first + BLOCK])
                load_out("dsa_out", A["dsa_w_o"][0])

            def load_mlp(l):
                base = STREAM[f"mlp{l}"]
                up = columns(A["mlp_w_up"][l])
                down = A["mlp_w_down"][l].rearrange("(j q p) n -> p j q n", p=P, q=PER_BLOCK)
                for q in range(PER_BLOCK):
                    load(base, q, up[:, 2 * q:2 * q + 2, 0, :])
                with sp.Fori(0, FF_STEPS - 1) as it:
                    for q in range(PER_BLOCK):
                        load(base, PER_BLOCK + q, up[:, 2 * q:2 * q + 2, it + 1, :], it)
                    for q in range(PER_BLOCK):
                        load(base, 2 * PER_BLOCK + q, down[:, it, q, :], it)
                for q in range(PER_BLOCK):
                    load(base, 8 * FF_STEPS - PER_BLOCK + q, down[:, FF_STEPS - 1, q, :])

            def load_rwkv():
                w = A["rwkv_w_rkv"][0].rearrange("c (k p) (b n) -> p c k b n", p=P, n=BLOCK)
                with sp.Fori(0, 3) as it:
                    for n in range(2):
                        for q in range(PER_BLOCK):
                            load(STREAM["rkv"], PER_BLOCK * n + q, w[:, it, 2 * q:2 * q + 2, n, :], it)
                load_out("rwkv_out", A["rwkv_w_o"][0])

            def load_conv():
                w = A["conv_w_in_2"][0].rearrange("(k p) (c h n) -> p k c h n", p=P, h=2, n=BLOCK)
                for half in range(2):
                    for n, kind in enumerate((2, 1, 0, 3)):
                        for q in range(PER_BLOCK):
                            load(STREAM["conv"], 16 * half + PER_BLOCK * n + q, w[:, 2 * q:2 * q + 2, kind, half, :])
                load_out("conv_out", A["conv_w_out_2"][0])

            def load_dil():
                w = columns(A["dil_w_in_2"][0])
                with sp.Fori(0, 8) as it:
                    for n in range(2):
                        for q in range(PER_BLOCK):
                            load(STREAM["dil"], PER_BLOCK * n + q, w[:, 2 * q:2 * q + 2, it * 2 + n, :], it)
                load_out("dil_out", A["dil_w_out_2"][0])

            def store():
                for i in range(TILES):
                    sp.wait_ge(out_ready, i + 1)
                    sp.dma_start(out[0, i * P:(i + 1) * P, :], xn[:, i, :]).then_inc(stored, 16)
                sp.wait_ge(stored, 16 * TILES)

            for i in range(TILES):
                sp.dma_start(X[:, i, :], A["x"][0, i * P:(i + 1) * P, :]).then_inc(x_loaded, 16)
            load_dsa()
            load_mlp(0)
            load_rwkv()
            load_mlp(1)
            load_conv()
            load_dil()
            store()

        @block.gpsimd
        def _(pool):
            def rstd(n):
                for i in range(TILES):
                    count = TILES * n + i + 1
                    pool.wait_ge(squared, count)
                    pool.tensor_scalar(stat[:, 2 + i:3 + i], stat[:, i:i + 1], 1.0 / D, EPS, ALU.mult, ALU.add).then_inc(rstd_step, 1)
                    pool.wait_ge(rstd_step, count)
                    pool.tensor_tensor(stat[:, 4 + i:5 + i], stat[:, 2 + i:3 + i], half_neg[:, 0:1], ALU.pow).then_inc(rstd_ready, 1)

            def modulation(l):
                w = A["w_mod_2"][l].rearrange("(k p) (n c) -> n k p c", p=P, c=D)
                done = KT * l

                def load(n, k):
                    pool.dma_start(M["mod_w"][:, n, :], w[n, k]).then_inc(mod_loaded[n], 16)

                def take(n, k):
                    part, total = M["mod_w"][:, n, :], M["mod_all"][:, n * D:(n + 1) * D]
                    pool.wait_ge(mod_scaled[n], k + (done + 1))
                    if isinstance(k, int) and k == 0:
                        pool.tensor_copy(total, part).then_inc(mod_used[n], 1)
                    else:
                        pool.tensor_tensor(total, total, part, ALU.add).then_inc(mod_used[n], 1)
                    pool.wait_ge(mod_used[n], k + (done + 1))

                for n in range(3):
                    load(n, 0)
                for n in range(3):
                    take(n, 0)
                    load(n, 1)
                with pool.Fori(1, KT - 1) as k:
                    for n in range(3):
                        take(n, k)
                        load(n, k + 1)
                for n in range(3):
                    take(n, KT - 1)

            def load_lora():
                pool.wait_ge(x_updated, 8)
                pool.wait_ge(mod_ready, 4)
                for name in ("w1", "a1", "g1"):
                    pool.dma_start(R[name][:], A[f"rwkv_{name}"][0].rearrange("(k p) n -> p k n", p=P)).then_inc(lora_loaded, 16)
                for name in ("w2", "a2"):
                    pool.dma_start(R[name][:], A[f"rwkv_{name}"][0]).then_inc(lora_loaded, 16)
                pool.dma_start(R["rows_of"][:], A["rows_of"].rearrange("h (a p) -> h a p", p=P)).then_inc(lora_loaded, 16)
                pool.memset(R["hT"][:, :, 0:1], 0.0).then_inc(hT_edge, 1)

            def scan_zeros():
                pool.wait_ge(lora_full, 3)
                for u in range(2):
                    pool.memset(scan["prod"][u][:, :, :, :, :], 0.0)
                    pool.memset(scan["n"][u][:, :, :], 0.0).then_inc(sc_zero, 1)
                pool.wait_ge(sc_zero, 2)

            def scan_values():
                with pool.Fori(0, SCAN_TURNS) as it:
                    for u in range(2):
                        pool.wait_ge(sc_dve, it * SCAN_DVE + (SCAN_BASE - 1 + u))
                        for h, rows in enumerate((slice(CHUNK, P), slice(0, CHUNK))):
                            copied = pool.tensor_copy(scan["zz"][u][rows, CHUNKS * h:CHUNKS * (h + 1), 1, :],
                                                      R["v"][rows, :, bass.ds(it * P + u * CHUNK, CHUNK)])
                        copied.then_inc(sc_pool, 1)

            def load_g2():
                pool.wait_ge(sc_prod, 2 * SCAN_TURNS)
                g2 = A["rwkv_g2"][0]
                pool.dma_start(R["g2a"], g2[0:P, :]).then_inc(g2_loaded, 16)
                pool.dma_start(R["g2b"], g2[P:GLORA, :]).then_inc(g2_loaded, 16)

            def conv_edges():
                pool.wait_ge(x_updated, 16)
                pool.memset(C["t"][:, :, 0:1], 0.0).then_inc(conv_edge, 1)
                pool.memset(C["t"][:, :, SEQ + 1:SEQ + 2], 0.0).then_inc(conv_edge, 1)

            pool.memset(half_neg[:, :], -0.5).then_inc(half_ready, 1)
            pool.wait_ge(half_ready, 1)
            rstd(0)
            rstd(1)
            modulation(0)
            load_lora()
            rstd(2)
            scan_zeros()
            scan_values()
            load_g2()
            rstd(3)
            modulation(1)
            rstd(4)
            conv_edges()
            rstd(5)
            rstd(6)
            rstd(7)

        @block.scalar
        def _(act):
            def split_hi(base, k, it=None, turn=8):
                g, slot = number(base, k, it, turn), (base + k) % RING
                lap = (base + k) // RING + 1
                act.wait_ge(loaded[slot], 16 * lap if it is None else it * (16 * turn // RING) + 16 * lap)
                if it is not None or g >= RING:
                    act.wait_ge(granule_used, g - RING + 1)
                act.activation(w_hi[:, slot, :], raw[:, slot, :], ACT.Copy).then_inc(hi_ready, 1)

            def split_block(base, k0, it=None, turn=8):
                for q in range(PER_BLOCK):
                    split_hi(base, k0 + q, it, turn)

            known = iter(range(1, PER_BLOCK * 6))

            def before_moving(sem_, count):
                value = act.to_reg(count)
                act.wait_ge(lo_ready, next(known))
                act.wait_ge(sem_, value)

            def square(i, sem_, count):
                act.wait_ge(sem_, count)
                act.activation(xn[:, i, :], X[:, i, :], ACT.Square, accum_out=stat[:, i:i + 1]).then_inc(squared, 1)

            def squares(*updated):
                for i in range(TILES):
                    square(i, x_updated, updated[i])

            def round_f(f):
                for b in range(4):
                    act.wait_ge(f_ready, 4 * f + b + 1)
                    act.activation(act_hi[0][:, 2 * b:2 * b + 2, :], act_f[:, 2 * b:2 * b + 2, :], ACT.Copy).then_inc(act_hi_ready, 1)

            def round_turned(n):
                for b in range(4):
                    act.wait_ge(turned, 4 * n + b + 1)
                    act.activation(act_hi[0][:, 2 * b:2 * b + 2, :].rearrange("p k t -> p (k t)"), bank[4 + b][:, :], ACT.Copy).then_inc(act_hi_ready, 1)

            def rope_move(r, k, src, xs, rot, n, half):
                if not isinstance(r, int) or r >= 2:
                    act.wait_ge(rope_done, r - 1)
                slot = k % 2
                act.activation(xs[:, slot, 0:n], src, ACT.Copy)
                for first in range(0, P, half):
                    to = first + half if (first // half) % 2 == 0 else first - half
                    mv = act.activation(rot[to:to + half, slot, 0:n], src[first:first + half, :], ACT.Copy)
                mv.then_inc(rope_x, 1)

            def init():
                act.dma_start(const[:, :], A["const"]).then_inc(const_loaded, 16)
                for to, name in ((0, "mixer_norm"), (16, "mlp_norm"), (32, "norm_g_2")):
                    act.dma_start(S["prow_a"][to:to + 16, :], A[name].rearrange("l (k p) -> (l k) p", p=P)).then_inc(rows_loaded, 16)
                act.dma_start(S["prow_a"][48:96, :], A["rwkv_mu"][0].rearrange("c (k p) -> (c k) p", p=P)).then_inc(rows_loaded, 16)
                act.dma_start(S["prow_a"][96:120, :], A["conv_k_2"][0].rearrange("w (k p) -> (w k) p", p=P)).then_inc(rows_loaded, 16)
                act.dma_start(S["prow_a"][120:128, :], A["c_2"].rearrange("b (k p) -> (b k) p", p=P)).then_inc(rows_loaded, 16)
                act.dma_start(S["prow_b"][0:48, :], A["b_mod_2"].rearrange("l (k p) -> (l k) p", p=P)).then_inc(rows_loaded, 16)
                for n, name in enumerate(("w0", "a0", "k_k", "k_a")):
                    act.dma_start(S["prow_b"][48 + KT * n:48 + KT * (n + 1), :],
                                  A["rwkv_" + name].rearrange("b (k p) -> (b k) p", p=P)).then_inc(rows_loaded, 16)
                act.dma_start(S["prow_b"][80:88, :], A["rwkv_r_k"][0].rearrange("(k h) n -> k (h n)", k=KT)).then_inc(rows_loaded, 16)
                for n, name in enumerate(("lnx_w", "lnx_b")):
                    act.dma_start(S["prow_b"][88 + KT * n:88 + KT * (n + 1), :],
                                  A["rwkv_" + name].rearrange("b (k p) -> (b k) p", p=P)).then_inc(rows_loaded, 16)
                w = A["dsa_w_in"][0].rearrange("(k p) n -> p k n", p=P)
                for half in range(2):
                    act.dma_start(S["w_ik"][:, :, half * HD:(half + 1) * HD], w[:, :, OFF_IK:OFF_IW]).then_inc(idx_w_loaded, 16)
                act.dma_start(S["w_iw"][:, :, :], w[:, :, OFF_IW:OFF_IW + IDX_HEADS]).then_inc(idx_w_loaded, 16)
                act.dma_start(const_bf[:, :], A["const_bf"]).then_inc(const_loaded, 16)
                act.dma_start(scale_row[:, :], A["final_norm"].partition_broadcast(P)).then_inc(scale_loaded, 16)
                for l in range(2):
                    act.dma_start(gate[:, l, :], A["b_mod_2"][l, 2 * D:3 * D].partition_broadcast(P)).then_inc(gate_loaded, 16)
                for i in range(TILES):
                    square(i, x_loaded, 16 * TILES)
                act.wait_ge(params_ready, 2)
                act.activation(c_col[:, :], COND, ACT.Silu).then_inc(cond_ready, 1)

            def dsa():
                base = STREAM["dsa"]

                def rope_bank(r, b, n=BLOCK):
                    rope_move(r, r, bank[b][:, 0:n], S["xs"], S["rot"], n, HD // 2)

                split_block(base, 0)
                round_f(0)
                act.wait_ge(idx_proj, 1)
                rope_bank(0, 4, SEQ)
                act.wait_ge(idx_proj, 2)
                act.activation(S["wi"][:, :, :], bank[5][:, 0:TILES * IDX_HEADS].rearrange("p (i h) -> p i h", i=TILES),
                               ACT.Copy, scale=IDX_SCALE).then_inc(wi_ready, 1)
                split_block(base, 4)
                act.wait_ge(granule_used, base + 4)
                rope_bank(1, 0)
                rope_bank(2, 1)
                split_block(base, 8)
                act.wait_ge(granule_used, base + 8)
                rope_bank(3, 2)
                act.activation(S["v"][:, :, :], bank[3][:, :].rearrange("p (i n) -> p i n", i=TILES), ACT.Copy).then_inc(v_ready, 1)
                split_block(base, 12)
                act.wait_ge(rope_done, 4)
                for n in range(KV_HEADS):
                    for half in range(2):
                        mv = act.activation(S["kT"][half * HD:(half + 1) * HD, n, :],
                                            S["k_rot"][(n % 2) * HD:(n % 2 + 1) * HD, n // 2, :], ACT.Copy)
                mv.then_inc(k_spread, 1)
                act.wait_ge(granule_used, base + 12)
                rope_bank(4, 0)
                rope_bank(5, 1)
                for step in range(4):
                    act.wait_ge(idx_full, step + 1)
                    for e in range(2):
                        n = 2 * step + e
                        if n >= 4:
                            act.wait_ge(scored, 2 * (n - 3))
                        act.activation(S["relu"][:, n % 4, :], bank[4 + n % 4][:, :], ACT.Relu).then_inc(idx_relu, 1)
                split_block(STREAM["dsa_out"], 0)
                act.wait_ge(granule_used, base + 16)
                rope_bank(6, 2)
                rope_bank(7, 3)

                units = TILES * KV_HEADS
                def exps(u):
                    slot = u % 2
                    act.wait_ge(nb_ready, u + 1)
                    if u >= 2:
                        act.wait_ge(pT_full, TILES * (u - 1))
                        act.wait_ge(rden_ready, u - 1)
                    for c in range(GROUP):
                        j, e = c // 2, c % 2
                        ex = act.activation(S["p"][:, slot, c, :], bank[2 * slot + e][:, j * SEQ:(j + 1) * SEQ], ACT.Exp,
                                            bias=S["nb"][:, slot, c:c + 1], scale=HD ** -0.5,
                                            accum_out=S["den"][:, slot, c:c + 1])
                    ex.then_inc(p_ready, 1)

                def copy_pT(u):
                    act.wait_ge(pT_full, TILES * u + 2)
                    if u >= 2:
                        act.wait_ge(o_full, u - 1)
                    act.activation(S["pT"][:, u % 2, 1, :], bank[5][:, :], ACT.Copy).then_inc(pT_ready_act, 1)

                for u in range(units):
                    exps(u)
                    copy_pT(u)
                round_turned(1)
                split_block(STREAM["dsa_out"], 4)

            def mlp(l):
                base, done = STREAM[f"mlp{l}"], 2 * FF_STEPS * l
                split_block(base, 0)
                squares(*((3, 4) if l == 0 else (11, 12)))
                round_f(1 + l)

                def relu(it, first_bank):
                    act.wait_ge(granule_used, it * 8 + (base + (4 if isinstance(it, int) and it == 0 else 0)))
                    for b in range(2):
                        act.activation(M["relu"][:, b, :], bank[first_bank + b][:, :], ACT.Relu).then_inc(up_relu, 1)

                def round_mid(it, slot):
                    for b in range(2):
                        act.wait_ge(up_sq, it * 2 + (done + b + 1))
                        act.activation(M["hi"][:, slot, 2 * b:2 * b + 2, :], M["sq"][:, b, :].rearrange("p (k t) -> p k t", k=2), ACT.Copy).then_inc(mid_hi, 1)

                def scale_mod(k):
                    for n in range(3):
                        if isinstance(k, int):
                            act.wait_ge(mod_loaded[n], 16 * (KT * l + k + 1))
                        else:
                            before_moving(mod_loaded[n], k * 16 + 16 * (KT * l + 1))
                        act.activation(M["mod_w"][:, n, :], M["mod_w"][:, n, :], ACT.Copy,
                                       scale=c_col[:, k:k + 1] if isinstance(k, int) else c_col[:, bass.ds(k, 1)]).then_inc(mod_scaled[n], 1)

                def step(it, first_bank):
                    if isinstance(it, int):
                        split_block(base, 4, it)
                        relu(it, first_bank)
                    else:
                        relu(it, first_bank)
                        split_block(base, 4, it)
                    scale_mod(it)
                    split_hi(base, 8, it)
                    round_mid(it, 0)
                    for q in range(1, PER_BLOCK):
                        split_hi(base, 8 + q, it)

                step(0, 6)
                with act.Fori(1, FF_STEPS - 1) as it:
                    step(it, 0)
                last = FF_STEPS - 1
                scale_mod(last)
                relu(last, 0)
                split_hi(base, 4 + 8 * last)
                round_mid(last, 1)
                for q in range(1, PER_BLOCK):
                    split_hi(base, 4 + 8 * last + q)

            def rwkv_in():
                base = STREAM["rkv"]

                def round_mix(c):
                    for b in range(4):
                        act.wait_ge(mixed, 4 * c + b + 1)
                        act.activation(act_hi[c % 2][:, 2 * b:2 * b + 2, :], act_f[:, 2 * b:2 * b + 2, :], ACT.Copy).then_inc(mix_hi, 1)

                def leave(n):
                    act.wait_ge(granule_used, base + PER_BLOCK * (n + 1))
                    c, half = n // 2, n % 2
                    for j in range(2):
                        src = bank[2 * half + j][:, :]
                        if c < 2:
                            at = 4 * half + 2 * j
                            dst, src = R["rT" if c == 0 else "kT"][:, at:at + 2, :], src.rearrange("p (k t) -> p k t", k=2)
                            act.activation(dst, src, ACT.Copy).then_inc(rkv_copied, 1)
                        else:
                            for par in range(2):
                                of = src[par * CHUNK:(par + 1) * CHUNK, :].rearrange("p (a h v) -> p a h v", h=2, v=RN)
                                for h, rows in enumerate((slice(CHUNK, P), slice(0, CHUNK))):
                                    at = slice(half * BLOCK // 2, (half + 1) * BLOCK // 2)
                                    mv = act.activation(R["v"][rows, 2 * j + par, at].rearrange("p (a v) -> p a v", v=RN), of[:, :, h, :], ACT.Copy)
                            mv.then_inc(rkv_copied, 1)

                split_block(base, 0)
                squares(6, 8)
                round_mix(0)
                split_block(base, 4)
                round_mix(1)
                leave(0)
                split_block(base, 8)
                leave(1)
                round_mix(2)
                split_block(base, 12)
                leave(2)
                split_block(base, 16)
                leave(3)
                act.wait_ge(lora_full, 1)
                act.activation(R["mid"][0:LORA, 0, :], bank[4][0:LORA, 0:SEQ], ACT.Tanh).then_inc(mid_ready, 1)
                split_block(base, 20)
                leave(4)
                act.wait_ge(lora_full, 2)
                act.activation(R["mid"][0:LORA, 1, :], bank[5][0:LORA, 0:SEQ], ACT.Copy).then_inc(mid_ready, 1)
                split_block(STREAM["rwkv_out"], 0)
                leave(5)
                act.wait_ge(lora_full, 3)
                act.activation(R["mid"][:, 2, :], bank[6][:, 0:SEQ], ACT.Sigmoid)
                act.activation(R["mid"][0:GLORA - P, 3, :], bank[6][0:GLORA - P, SEQ:2 * SEQ], ACT.Sigmoid).then_inc(mid_ready, 1)

            def root(ready, count):
                act.wait_ge(ready, count)
                act.activation(root_head[:, :], per_head[:, :], ACT.Sqrt).then_inc(rw_root, 1)

            def rwkv_mid():
                for b in range(8):
                    act.wait_ge(lora2_full, b + 1)
                    for j in range(2):
                        pair = 2 * (b % 4) + j
                        bias, dst = (W0, R["sg"]) if b < 4 else (A0, R["a"])
                        sg = act.activation(dst[:, pair, :], bank[b][:, j * SEQ:(j + 1) * SEQ], ACT.Sigmoid, bias=bias[:, pair:pair + 1])
                    sg.then_inc(lora2_ready, 1)
                act.wait_ge(rw_dve, 1)
                act.activation(R["pinv"][:, :, :], R["kk"][:, :, :], ACT.Square).then_inc(rw_act, 1)
                root(rw_dve, 4)
                act.activation(R["sg"][:, :, :], R["sg"][:, :, :], ACT.Exp, scale=DECAY_SCALE)
                act.wait_ge(rw_pe, 6)
                act.activation(R["pinv"][:, :, :], R["cum"][:, :, :], ACT.Exp, scale=-DECAY_SCALE).then_inc(rw_act, 1)
                act.wait_ge(rw_act, 2)
                act.activation(R["cum"][:, :, :], R["cum"][:, :, :], ACT.Exp, scale=DECAY_SCALE).then_inc(rw_act, 2)
                act.wait_ge(rw_act, 4)
                for half in range(2):
                    at = slice(4 * half, 4 * half + 4)
                    act.activation(R["pc"][:, at, :], R["cum"][:, at, :].rearrange("p a (c t) -> p a c t", c=CHUNKS)[:, :, :, CHUNK - 1], ACT.Copy).then_inc(sc_act, 1)

            def scan_loop():
                with act.Fori(0, SCAN_TURNS) as it:
                    def step(first, move):
                        for u in range(2):
                            act.wait_ge(sc_pe, it * SCAN_PE + (first + u * (2 if first == 1 else 1)))
                            move(u, 4 * u).then_inc(sc_act, 1)

                    def tiles(b):
                        return bank[b][:, :].rearrange("p (c t) -> p c t", c=CHUNKS)

                    def M(u):
                        return R["inv"][u][:, 1, :, :]

                    def N(u):
                        return scan["n"][u][:, :, :]

                    def keep_turned(u, B):
                        act.activation(scan["tok"][u][:, :, :], bank[B][:, :].rearrange("p (c n) -> p c n", c=CHUNKS), ACT.Copy)
                        for h, rows in enumerate((slice(0, CHUNK), slice(CHUNK, P))):
                            kept = act.activation(scan["aw"][u][rows, :, 0, :], tiles(B + 1)[rows, :, h * RN:(h + 1) * RN], ACT.Copy)
                        return kept

                    def keep(to, b):
                        return lambda u, B: act.activation(to(u), tiles(B + b), ACT.Copy)

                    def both(first, second):
                        def move(u, B):
                            first(u, B)
                            return second(u, B)
                        return move

                    step(1, keep_turned)
                    step(5, both(keep(M, 2), lambda u, B: act.activation(scan["aw"][u][:, :, 1, :], bank[B + 3][:, 0:CHUNKS * CHUNK].rearrange("p (c t) -> p c t", c=CHUNKS), ACT.Copy)))
                    step(7, keep(N, 0))
                    step(9, both(keep(N, 3), keep(M, 0)))
                    step(11, keep(M, 2))
                    step(15, keep(M, 0))
                    step(17, keep(M, 1))
                    step(21, keep(M, 3))
                    step(23, keep(M, 0))

                    def keep_removed(u, B):
                        for h, rows in enumerate((slice(0, CHUNK), slice(CHUNK, P))):
                            kept = act.activation(scan["zz"][u][rows, CHUNKS * h:CHUNKS * h + 2, :, :],
                                                  bank[B + 2][rows, 0:2 * P].rearrange("p (c a t) -> p c a t", c=2, a=2), ACT.Copy)
                        return kept

                    step(27, keep_removed)
                    for u in range(2):
                        before_moving(sc_pe, it * SCAN_PE + (29 + u))
                        act.activation(R["cum"][:, bass.ds(it * 2 + u, 1), :], bank[4 * u + 1][:, 0:SEQ].unsqueeze(1), ACT.Copy).then_inc(sc_act, 1)

            def rwkv_out():
                for b in range(4):
                    act.wait_ge(vT_full, b + 1)
                    halves = (slice(0, RN), slice(RN, P))
                    for j, rows in enumerate(halves):
                        for h, to in enumerate(halves):
                            moved = act.activation(R["kT"][to, 2 * b + j, :].rearrange("p (k t) -> p k t", k=CHUNKS),
                                                   bank[4 + b][rows, :].rearrange("p (k x t) -> p k x t", k=CHUNKS, x=2)[:, :, 1 - h, :], ACT.Copy)
                    moved.then_inc(vT_ready, 1)
                for b in range(4):
                    act.wait_ge(glora_full, b + 1)
                    act.activation(R["a"][:, 2 * b:2 * b + 2, :], bank[4 + b][:, :].rearrange("p (k t) -> p k t", k=2), ACT.Copy).then_inc(glora_ready, 1)
                for b in range(4):
                    act.wait_ge(centred, b + 1)
                    act.activation(R["pinv"][:, 2 * b:2 * b + 2, :], R["cum"][:, 2 * b:2 * b + 2, :], ACT.Square).then_inc(dev_sq, 1)
                root(var_ready, 1)
                for b in range(4):
                    act.wait_ge(normed, b + 1)
                    for pair in (2 * b, 2 * b + 1):
                        ln = act.activation(R["cum"][:, pair, :], R["cum"][:, pair, :], ACT.Identity, bias=LNX_B[:, pair:pair + 1], scale=LNX_W[:, pair:pair + 1])
                    ln.then_inc(lnx_ready, 1)
                for b in range(4):
                    act.wait_ge(mixed, 24 + b + 1)
                    act.activation(act_hi[0][:, 2 * b:2 * b + 2, :], act_f[:, 2 * b:2 * b + 2, :], ACT.Copy).then_inc(mix_hi, 1)
                split_block(STREAM["rwkv_out"], 4)

            def conv():
                base = STREAM["conv"]
                split_block(base, 0)
                squares(14, 16)
                squares(17, 18)
                act.wait_ge(x_updated, 18)
                act.dma_start(scale_row[:, :], A["final_g_2"].partition_broadcast(P)).then_inc(scale_loaded, 16)
                round_f(3)

                def two(ap, j):
                    return ap[:, 2 * j:2 * j + 2, :]

                def psum(b):
                    return bank[b][:, :].rearrange("p (k t) -> p k t", k=2)

                for half in range(2):
                    at = 16 * half
                    split_block(base, at + 4)
                    act.wait_ge(granule_used, base + at + 4)
                    if half:
                        act.wait_ge(conv_t, half)
                    for j in range(2):
                        mv = act.activation(two(C["xin"], j), psum(j), ACT.Copy)
                    mv.then_inc(conv_x, 1)
                    split_block(base, at + 8)
                    split_block(base, at + 12)
                    if half == 0:
                        split_block(base, 16)
                    else:
                        split_block(STREAM["conv_out"], 0)
                    act.wait_ge(granule_used, base + at + 16)
                    if half:
                        act.wait_ge(conv_y, 2 * half)
                    for j in range(2):
                        act.activation(two(C["sz"], j), psum(6 + j), ACT.Silu).then_inc(conv_z, 1)
                    for j in range(2):
                        act.wait_ge(conv_y, 2 * half + j + 1)
                        dst = slice(4 * half + 2 * j, 4 * half + 2 * j + 2)
                        act.activation(act_hi[1][:, dst, :], two(C["y"], j), ACT.Copy).then_inc(act_hi_ready, 1)
                split_block(STREAM["conv_out"], 4)

            def dilated():
                base = STREAM["dil"]
                split_block(base, 0)
                squares(21, 22)
                round_f(4)
                with act.Fori(0, 6) as it:
                    for n in range(2):
                        split_block(base, 4 * n + 4, it)
                        act.wait_ge(granule_used, it * 8 + (base + 4 * (n + 1)))
                        for j in range(2):
                            rope_move(it * 4 + (8 + 2 * n + j), 2 * n + j, bank[2 * n + j][:, :], L["xs"], L["rot"], BLOCK, DIL_HD // 2)
                for n in range(4):
                    if n < 3:
                        split_block(base, PER_BLOCK * (13 + n))
                    else:
                        split_block(STREAM["dil_out"], 0)
                    act.wait_ge(granule_used, base + PER_BLOCK * (13 + n))
                    for i in range(TILES):
                        dst = L["v" if n < 2 else "z"][:, i, n % 2 * BLOCK:(n % 2 + 1) * BLOCK]
                        act.activation(dst, bank[2 * (n % 2) + i][:, :], ACT.Copy if n < 2 else ACT.Silu).then_inc(vz_copied, 1)

                units = DIL_HEADS * TILES

                def exps(u):
                    slot = u % 2
                    act.wait_ge(nb_ready, 8 + u + 1)
                    if u >= 2:
                        act.wait_ge(pT_full, 16 + u - 1)
                    for b, to in ((0, slice(0, 2)), (1, slice(2, 3))):
                        n = SEQ * (2 - b)
                        ex = act.activation(LA["p"][:, slot, to, :], bank[2 * slot + b][:, 0:n].rearrange("p (g s) -> p g s", s=SEQ), ACT.Exp,
                                            bias=LA["nb"][:, slot:slot + 1], scale=DIL_HD ** -0.5, accum_out=LA["den"][:, slot, b:b + 1])
                    ex.then_inc(p_ready, 1)

                def copy_pT(u):
                    act.wait_ge(pT_full, 16 + u + 1)
                    if u >= 2:
                        act.wait_ge(o_full, 8 + u - 1)
                    act.activation(LA["pT"][:, u % 2, :, :], bank[4 + u % 2][:, 0:SEQ].rearrange("p (s t) -> p s t", s=TILES), ACT.Copy).then_inc(pT_ready_act, 1)

                exps(0)
                for u in range(units):
                    if u + 1 < units:
                        exps(u + 1)
                    copy_pT(u)
                round_turned(7)
                split_block(STREAM["dil_out"], 4)

            def final_norm():
                squares(25, 26)

            init()
            dsa()
            mlp(0)
            rwkv_in()
            rwkv_mid()
            scan_loop()
            rwkv_out()
            mlp(1)
            conv()
            dilated()
            final_norm()

        @block.vector
        def _(dve):
            def split_lo(base, k, it=None, turn=8):
                g, slot = number(base, k, it, turn), (base + k) % RING
                dve.wait_ge(hi_ready, g + 1)
                dve.tensor_tensor(w_lo[:, slot, :], raw[:, slot, :], w_hi[:, slot, :].bitcast(F32), ALU.subtract).then_inc(lo_ready, 1)

            def split_block(base, k0, it=None, turn=8):
                for q in range(PER_BLOCK):
                    split_lo(base, k0 + q, it, turn)

            def normalise(n):
                for i in range(TILES):
                    dve.wait_ge(rstd_ready, TILES * n + i + 1)
                    dve.tensor_scalar(xn[:, i, :], X[:, i, :], stat[:, 4 + i:5 + i], None, ALU.mult).then_inc(xn_ready, 1)

            def scale_turned(n, dst, g, ready, shift=None):
                for b in range(4):
                    dve.wait_ge(turned, 4 * n + b + 1)
                    for kk in range(2):
                        kt = 2 * b + kk
                        src = bank[4 + b][:, kk * SEQ:(kk + 1) * SEQ]
                        if shift is None:
                            st = dve.tensor_scalar(dst[:, kt, :], src, g[:, kt:kt + 1], None, ALU.mult)
                        else:
                            st = dve.tensor_scalar(dst[:, kt, :], src, g[:, kt:kt + 1], shift[:, kt:kt + 1], ALU.mult, ALU.add)
                    st.then_inc(ready, 1)

            def rest_f(s):
                for b in range(4):
                    dve.wait_ge(act_hi_ready, 4 * s + b + 1)
                    at = (slice(None), slice(2 * b, 2 * b + 2), slice(None))
                    dve.tensor_tensor(act_lo[0][at], act_f[at], act_hi[0][at].bitcast(F32), ALU.subtract).then_inc(act_lo_ready, 1)

            def rest_turned(s):
                for b in range(4):
                    dve.wait_ge(act_hi_ready, 4 * s + b + 1)
                    at = (slice(None), slice(2 * b, 2 * b + 2), slice(None))
                    dve.tensor_tensor(act_lo[0][at], bank[4 + b][:, :].rearrange("p (k t) -> p k t", k=2),
                                      act_hi[0][at].bitcast(F32), ALU.subtract).then_inc(act_lo_ready, 1)

            def rope_sum(r, k, dst, xs, rot, table, n):
                slot, groups = k % 2, n // SEQ
                def tab(a):
                    return table[:, a:a + 1, :].broadcast_to([P, groups, SEQ])
                def grp(t):
                    return t[:, slot, 0:n].rearrange("p (g t) -> p g t", g=groups)
                dve.wait_ge(rope_x, r + 1)
                dve.tensor_tensor(dst, grp(xs), tab(0), ALU.mult)
                dve.tensor_tensor(grp(rot), grp(rot), tab(1), ALU.mult).then_inc(rope_step, 1)
                dve.wait_ge(rope_step, r + 1)
                dve.tensor_tensor(dst, dst, grp(rot), ALU.add).then_inc(rope_done, 1)

            def add_out(name, n, l=None, tmp=None):
                dve.wait_ge(granule_used, STREAM[name] + PER_BLOCK * (n + 1))
                for i in range(TILES):
                    at = slice(n * BLOCK, (n + 1) * BLOCK)
                    to, src = X[:, i, at], bank[2 * n + i][:, :]
                    if l is not None:
                        step = 4 * l + 2 * n + i
                        if n:
                            dve.wait_ge(x_updated, (18 if l == 0 else 22) + i + 1)
                        dve.tensor_tensor(tmp[:, i, :], src, gate[:, l, at], ALU.mult).then_inc(x_step, 1)
                        dve.wait_ge(x_step, step + 1)
                        src = tmp[:, i, :]
                    dve.tensor_tensor(to, to, src, ALU.add).then_inc(x_updated, 1)

            def take_out(name, following, l=None, tmp=None):
                add_out(name, 0, l, tmp)
                if following:
                    for q in range(PER_BLOCK - 1):
                        split_lo(STREAM[following], q)
                add_out(name, 1, l, tmp)
                if following:
                    split_lo(STREAM[following], PER_BLOCK - 1)

            def init():
                dve.wait_ge(const_loaded, 32)
                dve.wait_ge(rows_turned, 1)
                dve.tensor_copy(pcol[:, 0:PROWS_A], bank[4][:, 0:PROWS_A]).then_inc(params_ready, 1)
                dve.wait_ge(rows_turned, 2)
                dve.tensor_copy(pcol[:, PROWS_A:], bank[5][:, 0:PROWS_B]).then_inc(params_ready, 1)
                dve.wait_ge(params_ready, 2)
                dve.tensor_tensor(head_rk[:, :, :], head_of, R_K.unsqueeze(2).broadcast_to([P, PAIRS, HEADS]), ALU.mult)

            def dsa():
                base = STREAM["dsa"]

                def rope(r, dst, n=BLOCK):
                    rope_sum(r, r, dst, S["xs"], S["rot"], rope64, n)

                normalise(0)
                split_block(base, 0)
                scale_turned(0, act_f, MIXER[0], f_ready)
                rest_f(0)
                rope(0, S["kiT"][:, :].unsqueeze(1), SEQ)
                split_block(base, 4)
                rope(1, S["qiT"][:, 0:2, :])
                rope(2, S["qiT"][:, 2:4, :])
                split_block(base, 8)
                rope(3, S["k_rot"][:, :, :])
                split_block(base, 12)
                rope(4, S["qT"][:, 0:2, :])
                rope(5, S["qT"][:, 2:4, :])
                dve.wait_ge(wi_ready, 1)
                for step in range(4):
                    i = step // 2
                    for e in range(2):
                        n = 2 * step + e
                        dve.wait_ge(idx_relu, n + 1)
                        for j in range(2):
                            h = 4 * (step % 2) + 2 * j + e
                            m = 2 * n + j
                            first = n % 4 == 0 and j == 0
                            if not first:
                                dve.wait_ge(scored, m)
                            dve.scalar_tensor_tensor(S["score"][:, i, :], S["relu"][:, n % 4, j * SEQ:(j + 1) * SEQ],
                                                     S["wi"][:, i, h:h + 1], causal[:, i, :] if first else S["score"][:, i, :],
                                                     ALU.mult, ALU.add).then_inc(scored, 1)
                split_block(STREAM["dsa_out"], 0)
                rope(6, S["qT"][:, 4:6, :])
                rope(7, S["qT"][:, 6:8, :])
                step = 0
                dve.wait_ge(scored, 16)
                for turn in range(TOPK // 8):
                    for i in range(TILES):
                        if turn:
                            dve.wait_ge(top_step, step - 1)
                        dve.max(S["top8"][:, i, :], S["score"][:, i, :]).then_inc(top_step, 1)
                        step += 1
                    for i in range(TILES):
                        dve.wait_ge(top_step, step - 1)
                        dve.match_replace(S["score"][:, i, :], S["top8"][:, i, :], S["score"][:, i, :], TAKEN).then_inc(top_step, 1)
                        step += 1
                for i in range(TILES):
                    dve.wait_ge(top_step, step - 1 + i)
                    dve.tensor_scalar(S["score"][:, i, :], S["score"][:, i, :], (TAKEN + NEG) / 2, NEG, ALU.is_gt, ALU.mult).then_inc(top_step, 1)
                    dve.wait_ge(top_step, step + 1 + i)
                    dve.tensor_tensor(S["bias"][:, i, :], S["score"][:, i, :], causal[:, i, :], ALU.add).then_inc(selected, 1)

                units = TILES * KV_HEADS

                def maxima(u):
                    slot = u % 2
                    dve.wait_ge(s_full, u + 1)
                    if u >= 2:
                        dve.wait_ge(p_ready, u - 1)
                    for e in range(2):
                        mx = dve.tensor_reduce(S["mx"][:, slot, :].rearrange("p (j e) -> p e j", e=2)[:, e, :],
                                               bank[2 * slot + e][:, :].rearrange("p (j t) -> p j t", j=2), AX.X, ALU.max)
                    mx.then_inc(max_ready, 1)
                    dve.wait_ge(max_ready, u + 1)
                    dve.tensor_scalar(S["nb"][:, slot, :], S["mx"][:, slot, :], -HD ** -0.5, None, ALU.mult).then_inc(nb_ready, 1)

                def copy_pT(u):
                    slot = u % 2
                    dve.wait_ge(pT_full, TILES * u + 1)
                    if u >= 2:
                        dve.wait_ge(o_full, u - 1)
                        dve.wait_ge(o_ready, u - 1)
                    dve.tensor_copy(S["pT"][:, slot, 0, :], bank[4][:, :]).then_inc(pT_ready, 1)
                    dve.wait_ge(p_ready, u + 1)
                    dve.reciprocal(S["rden"][:, slot, :], S["den"][:, slot, :]).then_inc(rden_ready, 1)

                def output(u):
                    i, n, slot = u // KV_HEADS, u % KV_HEADS, u % 2
                    dve.wait_ge(o_full, u + 1)
                    dve.wait_ge(rden_ready, u + 1)
                    dve.tensor_tensor(S["o"][:, i, n * SEQ:(n + 1) * SEQ].rearrange("p (c d) -> p c d", c=GROUP),
                                      bank[6 + slot][:, 0:GROUP * HD].rearrange("p (c d) -> p c d", c=GROUP),
                                      S["rden"][:, slot, :].unsqueeze(2).broadcast_to([P, GROUP, HD]), ALU.mult).then_inc(o_ready, 1)

                maxima(0)
                for u in range(units):
                    if u + 1 < units:
                        maxima(u + 1)
                    if u >= 1:
                        output(u - 1)
                    copy_pT(u)
                output(units - 1)
                rest_turned(1)
                split_block(STREAM["dsa_out"], 4)
                take_out("dsa_out", "mlp0")

            def mlp(l, following):
                base, done = STREAM[f"mlp{l}"], 2 * FF_STEPS * l
                normalise(1 + 2 * l)
                scale_turned(2 + 2 * l, act_f, MLPN[l], f_ready)
                rest_f(2 + l)

                def square(it):
                    if not isinstance(it, int) or it > 0:
                        dve.wait_ge(mid_lo, it * 2 + done)
                    for b in range(2):
                        dve.wait_ge(up_relu, it * 2 + (done + b + 1))
                        dve.tensor_tensor(M["sq"][:, b, :], M["relu"][:, b, :], M["relu"][:, b, :], ALU.mult).then_inc(up_sq, 1)

                def rest_mid(it, slot):
                    for b in range(2):
                        at = (slice(None), slot, slice(2 * b, 2 * b + 2), slice(None))
                        dve.wait_ge(mid_hi, it * 2 + (done + b + 1))
                        dve.tensor_tensor(M["lo"][at], M["sq"][:, b, :].rearrange("p (k t) -> p k t", k=2),
                                          M["hi"][at].bitcast(F32), ALU.subtract).then_inc(mid_lo, 1)

                def step(it):
                    if isinstance(it, int):
                        split_block(base, 4, it)
                        square(it)
                    else:
                        square(it)
                        split_block(base, 4, it)
                    split_lo(base, 8, it)
                    rest_mid(it, 0)
                    for q in range(1, PER_BLOCK):
                        split_lo(base, 8 + q, it)

                step(0)
                with dve.Fori(1, FF_STEPS - 1) as it:
                    step(it)
                last = FF_STEPS - 1
                square(last)
                split_lo(base, 4 + 8 * last)
                rest_mid(last, 1)
                for q in range(1, PER_BLOCK):
                    split_lo(base, 4 + 8 * last + q)
                for q in range(PER_BLOCK - 1):
                    split_lo(STREAM[following], q)
                dve.wait_ge(granule_used, base + 8 * FF_STEPS)
                for i in range(TILES):
                    for n in range(2):
                        to = X[:, i, n * BLOCK:(n + 1) * BLOCK]
                        dve.tensor_tensor(to, to, bank[2 + 2 * i + n][:, :], ALU.add).then_inc(x_updated, 1)
                split_lo(STREAM[following], PER_BLOCK - 1)
                modulation(l)

            def modulation(l):
                dve.wait_ge(mod_full, 3 * l + 1)
                dve.tensor_tensor(mod_col[:, l, :], bank[7][:, 0:2 * KT], B_MOD[l], ALU.add).then_inc(mod_ready, 1)
                dve.wait_ge(mod_ready, 4 * l + 1)
                dve.scalar_tensor_tensor(gain[:, l, :], mod_col[:, l, KT:2 * KT], 1.0, NORM2[l], ALU.add, ALU.mult).then_inc(mod_ready, 1)
                dve.wait_ge(gate_loaded, 32)
                for n, b in enumerate((6, 0)):
                    dve.wait_ge(mod_full, 3 * l + 2 + n)
                    to = gate[:, l, n * BLOCK:(n + 1) * BLOCK]
                    dve.tensor_tensor(to, to, bank[b][:, :], ALU.add).then_inc(mod_ready, 1)

            def rwkv_in():
                base = STREAM["rkv"]
                hT, xx = R["hT"], R["xx"]
                normalise(2)
                dve.wait_ge(hT_edge, 1)
                scale_turned(3, hT[:, :, 1:SEQ + 1], MIXER[1], hT_ready)
                for b in range(4):
                    dve.wait_ge(hT_ready, b + 1)
                    at = slice(2 * b, 2 * b + 2)
                    dve.tensor_tensor(xx[:, at, :], hT[:, at, 0:SEQ], hT[:, at, 1:SEQ + 1], ALU.subtract).then_inc(shifted, 1)

                def mix(c):
                    for b in range(4):
                        dve.wait_ge(shifted, b + 1)
                        for kt in (2 * b, 2 * b + 1):
                            mm = dve.scalar_tensor_tensor(act_f[:, kt, :], xx[:, kt, :], MU[c][:, kt:kt + 1],
                                                          hT[:, kt, 1:SEQ + 1], ALU.mult, ALU.add)
                        mm.then_inc(mixed, 1)

                def rest_mix(c):
                    for b in range(4):
                        dve.wait_ge(mix_hi, 4 * c + b + 1)
                        at = (slice(None), slice(2 * b, 2 * b + 2), slice(None))
                        dve.tensor_tensor(act_lo[c % 2][at], act_f[at], act_hi[c % 2][at].bitcast(F32), ALU.subtract).then_inc(mix_lo, 1)

                mix(0)
                rest_mix(0)
                split_block(base, 4)
                dve.wait_ge(mix_lo, 4)
                mix(1)
                rest_mix(1)
                split_block(base, 8)
                dve.wait_ge(mix_lo, 8)
                mix(2)
                rest_mix(2)
                split_block(base, 12)
                dve.wait_ge(mix_lo, 12)
                mix(3)
                split_block(base, 16)
                dve.wait_ge(lora_full, 1)
                mix(4)
                split_block(base, 20)
                dve.wait_ge(lora_full, 2)
                mix(5)
                split_block(STREAM["rwkv_out"], 0)

            def invert(n):
                dve.wait_ge(rw_root, n)
                dve.reciprocal(root_head[:, :], root_head[:, :]).then_inc(rw_inverse, 1)

            def rwkv_mid():
                def all_pairs(column):
                    return column.unsqueeze(2).broadcast_to([P, PAIRS, SEQ])

                rT, kT, kk, a, sg, cum, pinv = (R[n][:, :, :] for n in ("rT", "kT", "kk", "a", "sg", "cum", "pinv"))
                dve.wait_ge(rkv_copied, 8)
                dve.wait_ge(lora2_full, 8)
                dve.tensor_tensor(kk, kT, all_pairs(K_K), ALU.mult).then_inc(rw_dve, 1)
                dve.wait_ge(lora2_ready, 8)
                for pair in range(PAIRS):
                    sc = dve.tensor_tensor_scan(cum[:, pair, :], view["keep"], sg[:, pair, :], 0.0, ALU.mult, ALU.add)
                sc.then_inc(rw_dve, 1)
                dve.wait_ge(rw_dve, 2)
                dve.tensor_tensor(sg, cum, sg, ALU.subtract).then_inc(rw_dve, 1)
                dve.wait_ge(rw_pe, 1)
                dve.tensor_scalar(per_head[:, :], bank[0][0:HEADS, 0:SEQ], 1e-24, None, ALU.max).then_inc(rw_dve, 1)
                dve.scalar_tensor_tensor(pinv, a, -1.0, all_pairs(K_A), ALU.add, ALU.mult).then_inc(rw_dve, 1)
                invert(1)
                dve.wait_ge(rw_dve, 5)
                dve.scalar_tensor_tensor(kT, pinv, 1.0, kT, ALU.add, ALU.mult).then_inc(rw_dve, 1)
                dve.wait_ge(rw_dve, 6)
                dve.tensor_tensor(pinv, rT, kT, ALU.mult).then_inc(rw_dve, 1)
                for b in range(4):
                    dve.wait_ge(rw_pe, 2 + b)
                    at = slice(2 * b, 2 * b + 2)
                    nk = dve.tensor_tensor(R["kk"][:, at, :], R["kk"][:, at, :], bank[4 + b][:, :].rearrange("p (k t) -> p k t", k=2), ALU.mult)
                nk.then_inc(rw_dve, 1)
                dve.wait_ge(rw_dve, 8)
                dve.tensor_tensor(a, kk, a, ALU.mult).then_inc(sc_dve, 1)
                dve.wait_ge(rw_pe, 6)
                dve.tensor_copy(R["mid"][0:HEADS, 0, :], bank[1][0:HEADS, 0:SEQ]).then_inc(sc_dve, 1)

            def scan_loop():
                heads = [slice(0, CHUNK), slice(CHUNK, P)]

                def Q(u):
                    return R["inv"][u][:, 0, :, :]

                def M(u):
                    return R["inv"][u][:, 1, :, :]

                def N(u):
                    return scan["n"][u][:, :, :]

                def pair(t, it, u):
                    return t[:, bass.ds(it * 2 + u, 1), :]

                def operand(k, it, u):
                    a, b = ((R["kk"], R["sg"]), (R["rT"], R["cum"]), (R["a"], R["pinv"]), (R["kT"], R["pinv"]))[k]
                    a, b = (pair(x, it, u).rearrange("p a (c t) -> p (a c) t", c=CHUNKS) for x in (a, b))
                    for h, rows in enumerate(heads):
                        to = scan["prod"][u][rows, :, k, h, :] if k < 2 else scan["bk"][u][rows, :, abs(k - 2 - h), :]
                        if k == 0:
                            made = dve.scalar_tensor_tensor(to, a[rows, :, :], -1.0, b[rows, :, :], ALU.mult, ALU.mult)
                        else:
                            made = dve.tensor_tensor(to, a[rows, :, :], b[rows, :, :], ALU.mult)
                    return made

                def turn(it, following):
                    def before(n):
                        dve.wait_ge(sc_dve, it * SCAN_DVE + (SCAN_BASE + n))

                    def products(n):
                        dve.wait_ge(sc_pe, it * SCAN_PE + n)

                    def ahead(u, first, last):
                        if following:
                            for k in range(first, last):
                                op = operand(k, it + 1, u)
                            if last == 4:
                                op.then_inc(sc_prod, 1)

                    def tiles(b):
                        return bank[b][:, :].rearrange("p (c t) -> p c t", c=CHUNKS)

                    def cut(u, m):
                        for h, rows in enumerate(heads):
                            part = dve.tensor_tensor(N(u)[rows, :, h * CHUNK:(h + 1) * CHUNK], scan["att"][u][rows, CHUNKS * h:CHUNKS * (h + 1), 0, :],
                                                     split_mask[rows, m:m + 1, :].broadcast_to([CHUNK, CHUNKS, CHUNK]), ALU.mult)
                        return part

                    def grow(step, b, after=None):
                        for u in range(2):
                            inverse = Q(u)
                            products(step + u)
                            op = dve.tensor_tensor(inverse, inverse, tiles(4 * u + b), ALU.add)
                            if after:
                                op = after(u)
                            op.then_inc(sc_dve, 1)

                    for u in range(2):
                        n = 1 + 3 * u
                        products(2 * u + 2)
                        att = scan["att"][u][:, :, :, :].rearrange("p (h c) m t -> p h c m t", h=2)
                        for j in range(2):
                            for h in range(2):
                                dv = dve.tensor_tensor(att[:, h, 2 * j:2 * j + 2, :, :], bank[4 * u + 2 + j][:, :].rearrange("p (c m h t) -> p c m h t", c=2, m=2, h=2)[:, :, :, h, :],
                                                       scan_mask.unsqueeze(1).broadcast_to([P, 2, 2, CHUNK]), ALU.mult)
                        dv.then_inc(sc_dve, 1)
                        before(n)
                        cut(u, 0).then_inc(sc_dve, 1)
                        before(n + 1)
                        dve.tensor_tensor(Q(u), N(u), ident.unsqueeze(1).broadcast_to([P, CHUNKS, P]), ALU.add).then_inc(sc_dve, 1)
                    for u in range(2):
                        products(7 + u)
                        dve.tensor_copy(M(u), tiles(4 * u + 1)).then_inc(sc_dve, 1)
                    for u in range(2):
                        dve.tensor_tensor(pair(R["rT"], it, u), pair(R["rT"], it, u), pair(R["cum"], it, u), ALU.mult)
                    grow(9, 2)
                    ahead(0, 0, 2)
                    grow(11, 1)
                    ahead(0, 2, 4)
                    grow(13, 3, lambda u: cut(u, 1))
                    ahead(1, 0, 2)
                    for u in range(2):
                        products(17 + u)
                        cut(u, 2).then_inc(sc_dve, 1)
                    grow(19, 2)
                    ahead(1, 2, 4)
                    grow(25, 1)
                    for u in range(2):
                        products(27 + u)
                        for h, rows in enumerate(heads):
                            kept = dve.tensor_copy(scan["zz"][u][rows, CHUNKS * h + 2:CHUNKS * h + 4, :, :],
                                                   bank[4 * u + 3][rows, 0:2 * P].rearrange("p (c a t) -> p c a t", c=2, a=2))
                        kept.then_inc(sc_dve, 1)
                    for u in range(2):
                        products(29 + u)

                        def chunks(t, first, last):
                            return pair(t, it, u)[:, :, first * CHUNK:last * CHUNK].rearrange("p a (c t) -> p (a c) t", t=CHUNK)

                        def part(first, last):
                            return bank[4 * u][:, first * CHUNK:last * CHUNK].rearrange("p (c t) -> p c t", t=CHUNK)

                        dve.tensor_tensor(chunks(R["sg"], 1, 3), part(0, 2), unit.unsqueeze(1).broadcast_to([P, 2, RN]), ALU.add)
                        dve.tensor_tensor(chunks(R["rT"], 1, 4), part(2, 5), chunks(R["rT"], 1, 4), ALU.add)
                        decay = pair(R["pc"], it, u)[:, :, 0:3].rearrange("p a c -> p (a c)").unsqueeze(2).broadcast_to([P, 3, RN])
                        dve.tensor_tensor(chunks(R["pinv"], 0, 3), part(5, 8), decay, ALU.mult).then_inc(sc_dve, 1)

                dve.wait_ge(rw_act, 4)
                dve.wait_ge(sc_dve, SCAN_BASE)
                dve.wait_ge(sc_zero, 2)
                for u in range(2):
                    for k in range(4):
                        op = operand(k, 0, u)
                    op.then_inc(sc_prod, 1)
                with dve.Fori(0, SCAN_TURNS - 1) as it:
                    turn(it, True)
                turn(SCAN_TURNS - 1, False)

            def rwkv_out():
                F, G, Y = R["sg"], R["pinv"], R["cum"]

                def chunk(t, c):
                    return t[:, :, c * CHUNK:(c + 1) * CHUNK]

                def rows(b):
                    return bank[b][:, :].rearrange("p (a n) -> p a n", a=PAIRS)

                def add_y(c):
                    dve.wait_ge(y_full, c)
                    dve.tensor_tensor(chunk(Y, c), chunk(Y, c), rows(2 + c % 2), ALU.add).then_inc(y_ready, 1)

                dve.wait_ge(sc_act, SCAN_BASE + SCAN_ACT * SCAN_TURNS)
                for c in range(1, CHUNKS - 1):
                    dve.wait_ge(chain_full, c)
                    st = state[:, c - 1, :, :]
                    dve.tensor_tensor(st, rows(c - 1), R["pc"][:, :, c:c + 1].broadcast_to([P, PAIRS, RN]), ALU.mult).then_inc(chain_scaled, 1)
                    dve.wait_ge(chain_scaled, c)
                    dve.tensor_tensor(st, st, chunk(G, c), ALU.add).then_inc(chain_ready, 1)
                    add_y(c)
                add_y(CHUNKS - 1)
                for b in range(4):
                    at = slice(2 * b, 2 * b + 2)
                    dve.wait_ge(mean_full, b + 1)
                    dve.tensor_tensor(Y[:, at, :], Y[:, at, :], bank[4 + b][:, :].rearrange("p (k t) -> p k t", k=2), ALU.subtract).then_inc(centred, 1)
                for b in range(4):
                    at = slice(2 * b, 2 * b + 2)
                    dve.wait_ge(bonus_full, b + 1)
                    dve.wait_ge(vT_ready, 4)
                    dve.tensor_tensor(R["kT"][:, at, :], R["kT"][:, at, :], bank[b][:, :].rearrange("p (k t) -> p k t", k=2), ALU.mult).then_inc(out_step, 1)
                dve.wait_ge(var_full, 1)
                dve.tensor_scalar(per_head[:, :], bank[4][0:HEADS, 0:SEQ], 1.0 / RN, LNX_EPS, ALU.mult, ALU.add).then_inc(var_ready, 1)
                invert(2)
                for b in range(4):
                    at = slice(2 * b, 2 * b + 2)
                    dve.wait_ge(spread_full, b + 1)
                    dve.tensor_tensor(Y[:, at, :], Y[:, at, :], bank[4 + b][:, :].rearrange("p (k t) -> p k t", k=2), ALU.mult).then_inc(normed, 1)
                for b in range(4):
                    at = slice(2 * b, 2 * b + 2)
                    dve.wait_ge(lnx_ready, b + 1)
                    dve.tensor_tensor(Y[:, at, :], Y[:, at, :], R["kT"][:, at, :], ALU.add).then_inc(out_step, 1)
                for b in range(4):
                    at = slice(2 * b, 2 * b + 2)
                    dve.wait_ge(out_step, 4 + b + 1)
                    dve.wait_ge(glora_ready, b + 1)
                    dve.tensor_tensor(act_f[:, at, :], Y[:, at, :], R["a"][:, at, :], ALU.mult).then_inc(mixed, 1)
                for b in range(4):
                    at = (slice(None), slice(2 * b, 2 * b + 2), slice(None))
                    dve.wait_ge(mix_hi, 12 + b + 1)
                    dve.tensor_tensor(act_lo[0][at], act_f[at], act_hi[0][at].bitcast(F32), ALU.subtract).then_inc(mix_lo, 1)
                split_block(STREAM["rwkv_out"], 4)
                take_out("rwkv_out", "mlp1")

            def mid_norm():
                dve.wait_ge(scale_loaded, 16)
                for i in range(TILES):
                    dve.wait_ge(rstd_ready, TILES * 4 + i + 1)
                    dve.scalar_tensor_tensor(X[:, i, :], X[:, i, :], stat[:, 4 + i:5 + i], scale_row[:, :], ALU.mult, ALU.mult).then_inc(x_updated, 1)

            def conv():
                base = STREAM["conv"]
                dve.wait_ge(x_updated, 18)
                normalise(5)
                dve.wait_ge(mod_ready, 8)
                scale_turned(5, act_f, gain[:, 0, :], f_ready, mod_col[:, 0, 0:KT])
                rest_f(4)

                def two(ap, j):
                    return ap[:, 2 * j:2 * j + 2, :]

                def psum(b):
                    return bank[b][:, :].rearrange("p (k t) -> p k t", k=2)

                dve.wait_ge(conv_edge, 2)
                for half in range(2):
                    at = 16 * half
                    split_block(base, at + 4)
                    split_block(base, at + 8)
                    dve.wait_ge(granule_used, base + at + 8)
                    dve.wait_ge(conv_x, half + 1)
                    for j in range(2):
                        tt = dve.tensor_tensor(two(C["t"], j)[:, :, 1:SEQ + 1], psum(2 + j), two(C["xin"], j), ALU.mult)
                    tt.then_inc(conv_t, 1)
                    split_block(base, at + 12)
                    dve.wait_ge(conv_t, half + 1)
                    for w in range(3):
                        for f in range(4):
                            kt = 4 * half + f
                            taps = CONV_K[w][:, kt:kt + 1]
                            if w == 0:
                                tap = dve.tensor_scalar(C["cv"][:, f, :], C["t"][:, f, 0:SEQ], taps, None, ALU.mult)
                            else:
                                tap = dve.scalar_tensor_tensor(C["cv"][:, f, :], C["t"][:, f, w:w + SEQ], taps, C["cv"][:, f, :], ALU.mult, ALU.add)
                        tap.then_inc(conv_tap, 1)
                        dve.wait_ge(conv_tap, 3 * half + w + 1)
                    dve.wait_ge(granule_used, base + at + 12)
                    for j in range(2):
                        yy = dve.tensor_tensor(two(C["y"], j), psum(4 + j), two(C["cv"], j), ALU.mult)
                    yy.then_inc(conv_b, 1)
                    if half == 0:
                        split_block(base, 16)
                    else:
                        split_block(STREAM["conv_out"], 0)
                    dve.wait_ge(conv_b, half + 1)
                    for j in range(2):
                        dve.wait_ge(conv_z, 2 * half + j + 1)
                        dve.tensor_tensor(two(C["y"], j), two(C["y"], j), two(C["sz"], j), ALU.mult).then_inc(conv_y, 1)
                    for j in range(2):
                        dve.wait_ge(act_hi_ready, 4 * 5 + 2 * half + j + 1)
                        dst = slice(4 * half + 2 * j, 4 * half + 2 * j + 2)
                        dve.tensor_tensor(act_lo[1][:, dst, :], two(C["y"], j), act_hi[1][:, dst, :].bitcast(F32), ALU.subtract).then_inc(act_lo_ready, 1)
                split_block(STREAM["conv_out"], 4)
                take_out("conv_out", "dil", 0, C["tmp"])

            def dilated():
                base = STREAM["dil"]
                normalise(6)
                scale_turned(6, act_f, gain[:, 1, :], f_ready, mod_col[:, 1, 0:KT])
                rest_f(6)
                with dve.Fori(0, 6) as it:
                    for n in range(2):
                        split_block(base, 4 * n + 4, it)
                        for j in range(2):
                            rope_sum(it * 4 + (8 + 2 * n + j), 2 * n + j, L["qk"][:, bass.ds(it * 8 + (4 * n + 2 * j), 2), :], L["xs"], L["rot"], rope128, BLOCK)
                for n in range(13, 16):
                    split_block(base, PER_BLOCK * n)
                split_block(STREAM["dil_out"], 0)

                units = DIL_HEADS * TILES

                def maxima(u):
                    slot = u % 2
                    dve.wait_ge(s_full, 8 + u + 1)
                    if u >= 2:
                        dve.wait_ge(p_ready, 8 + u - 1)
                    dve.tensor_reduce(LA["mx"][:, slot, 0:1], bank[2 * slot][:, :], AX.X, ALU.max)
                    dve.tensor_reduce(LA["mx"][:, slot, 1:2], bank[2 * slot + 1][:, 0:SEQ], AX.X, ALU.max).then_inc(max_ready, 1)
                    dve.wait_ge(max_ready, 8 + u + 1)
                    dve.tensor_scalar(LA["nb"][:, slot:slot + 1], LA["mx"][:, slot, 0:1], LA["mx"][:, slot, 1:2], -DIL_HD ** -0.5, ALU.max, ALU.mult).then_inc(nb_ready, 1)

                def join(u):
                    p, den, rden = LA["p"][:, u % 2], LA["den"][:, u % 2], LA["rden"][:, u % 2]
                    dve.wait_ge(p_ready, 8 + u + 1)
                    if u >= 2:
                        dve.wait_ge(o_ready, 8 + u - 1)
                    dve.tensor_tensor(p[:, 0, :], p[:, 0, :], p[:, 1, :], ALU.add)
                    dve.tensor_tensor(rden[:, 0:1], den[:, 0:1], den[:, 1:2], ALU.add).then_inc(probs_sum, 1)
                    dve.wait_ge(probs_sum, 2 * u + 1)
                    dve.reciprocal(rden[:, 1:2], rden[:, 0:1])
                    dve.tensor_tensor(p[:, 0, :], p[:, 0, :], p[:, 2, :], ALU.add).then_inc(probs_sum, 1)

                def output(u):
                    h, i, slot = u // TILES, u % TILES, u % 2
                    dve.wait_ge(o_full, 8 + u + 1)
                    dve.wait_ge(probs_sum, 2 * u + 2)
                    z = L["z"][:, i, h * P:(h + 1) * P]
                    dve.scalar_tensor_tensor(z, bank[6 + slot][:, 0:P], LA["rden"][:, slot, 1:2], z, ALU.mult, ALU.mult).then_inc(o_ready, 1)

                dve.wait_ge(vz_copied, 8)
                maxima(0)
                for u in range(units):
                    join(u)
                    if u + 1 < units:
                        maxima(u + 1)
                    if u >= 1:
                        output(u - 1)
                output(units - 1)
                rest_turned(7)
                split_block(STREAM["dil_out"], 4)
                take_out("dil_out", None, 1, LA["tmp"])

            def final_norm():
                dve.wait_ge(scale_loaded, 32)
                for i in range(TILES):
                    dve.wait_ge(rstd_ready, TILES * 7 + i + 1)
                    dve.scalar_tensor_tensor(xn[:, i, :], X[:, i, :], stat[:, 4 + i:5 + i], scale_row[:, :], ALU.mult, ALU.mult).then_inc(out_ready, 1)

            init()
            dsa()
            mlp(0, "rkv")
            rwkv_in()
            rwkv_mid()
            scan_loop()
            rwkv_out()
            mlp(1, "conv")
            mid_norm()
            conv()
            dilated()
            final_norm()

        @block.tensor
        def _(pe):
            def token_granule(g, slot, hi, lo, kts, n, banks, first, last, used=True):
                pe.wait_ge(lo_ready, g + 1)
                for i in range(TILES):
                    for kk, kt in enumerate(kts):
                        at = slice(kk * n, (kk + 1) * n)
                        x_hi, x_lo = hi[:, kt, i * P:(i + 1) * P], lo[:, kt, i * P:(i + 1) * P]
                        begin, end = first and kk == 0, last and kk == len(kts) - 1
                        dst = banks[i]
                        pe.matmul(dst, x_hi, w_hi[:, slot, at], start=begin, stop=False, skip_group_check=True)
                        pe.matmul(dst, x_hi, w_lo[:, slot, at], start=False, stop=False, skip_group_check=True)
                        mm = pe.matmul(dst, x_lo, w_hi[:, slot, at], start=False, stop=end, skip_group_check=True)
                mm.then_inc(granule_used, 1)

            def feature_granule(g, slot, hi, lo, q, banks, groups=range(4), inc=True):
                if inc:
                    pe.wait_ge(lo_ready, g + 1)
                for f in groups:
                    dst = banks[f // 2][:, (f % 2) * SEQ:(f % 2 + 1) * SEQ]
                    for kk in range(2):
                        kt = 2 * q + kk
                        at = slice(kk * BLOCK + f * P, kk * BLOCK + (f + 1) * P)
                        begin = q == 0 and kk == 0 and f % 2 == 0
                        end = q == PER_BLOCK - 1 and kk == 1
                        pe.matmul(dst, w_hi[:, slot, at], hi[:, kt, :], start=begin, stop=False, skip_group_check=True)
                        pe.matmul(dst, w_hi[:, slot, at], lo[:, kt, :], start=False, stop=False, skip_group_check=True)
                        mm = pe.matmul(dst, w_lo[:, slot, at], hi[:, kt, :], start=False, stop=end, skip_group_check=True)
                if inc:
                    mm.then_inc(granule_used, 1)
                return mm

            def token_block(base, k0, hi, lo, banks, it=None):
                for q in range(PER_BLOCK):
                    token_granule(number(base, k0 + q, it), (base + k0 + q) % RING, hi, lo, (2 * q, 2 * q + 1), BLOCK,
                                  banks, q == 0, q == PER_BLOCK - 1)

            def feature_block(base, k0, hi, lo, banks, it=None):
                for q in range(PER_BLOCK):
                    feature_granule(number(base, k0 + q, it), (base + k0 + q) % RING, hi, lo, q, banks)

            def turn(n, src, ready=None):
                for i in range(TILES):
                    if ready is not None:
                        pe.wait_ge(xn_ready, ready + i + 1)
                    for b in range(4):
                        for kk in range(2):
                            kt = 2 * b + kk
                            mm = pe.transpose(bank[4 + b][:, (kk * TILES + i) * P:(kk * TILES + i + 1) * P],
                                              src[:, i, kt * P:(kt + 1) * P], ident)
                        if i == TILES - 1:
                            mm.then_inc(turned, 1)

            def wait_act(s, q):
                pe.wait_ge(act_lo_ready, 4 * s + q + 1)

            def out_linear(name, s, u=0):
                for b in range(2):
                    for q in range(PER_BLOCK):
                        if b == 0 and s is not None:
                            wait_act(s, q)
                        g = STREAM[name] + PER_BLOCK * b + q
                        token_granule(g, g % RING, act_hi[u], act_lo[u], (2 * q, 2 * q + 1), BLOCK,
                                      (bank[2 * b][:, :], bank[2 * b + 1][:, :]), q == 0, q == PER_BLOCK - 1)

            def init():
                pe.wait_ge(const_loaded, 32)
                pe.wait_ge(rows_loaded, 16 * 14)
                pe.transpose(bank[4][:, 0:PROWS_A], S["prow_a"][:, :], ident).then_inc(rows_turned, 1)
                pe.transpose(bank[5][:, 0:PROWS_B], S["prow_b"][:, :], ident[0:PROWS_B, 0:PROWS_B]).then_inc(rows_turned, 1)
                pe.wait_ge(params_ready, 2)

            def dsa():
                base = STREAM["dsa"]
                hi, lo = act_hi[0], act_lo[0]

                def block(k0, banks):
                    for q in range(PER_BLOCK):
                        if k0 == 0:
                            wait_act(0, q)
                        feature_granule(base + k0 + q, (base + k0 + q) % RING, hi, lo, q, banks)

                turn(0, xn, 0)
                pe.wait_ge(f_ready, 4)
                pe.wait_ge(idx_w_loaded, 48)
                for kt in range(KT):
                    mm = pe.matmul(bank[4][:, 0:SEQ], S["w_ik"][:, kt, :], act_f[:, kt, :], start=kt == 0, stop=kt == KT - 1)
                mm.then_inc(idx_proj, 1)
                for i in range(TILES):
                    for kt in range(KT):
                        mm = pe.matmul(bank[5][:, i * IDX_HEADS:(i + 1) * IDX_HEADS], act_f[:, kt, i * P:(i + 1) * P],
                                       S["w_iw"][:, kt, :], start=kt == 0, stop=kt == KT - 1)
                mm.then_inc(idx_proj, 1)
                block(0, (bank[0], bank[1]))
                for q in range(PER_BLOCK):
                    g = base + 4 + q
                    slot = g % RING
                    pe.wait_ge(lo_ready, g + 1)
                    feature_granule(g, slot, hi, lo, q, (bank[2],), range(2), False)
                    for i in range(TILES):
                        for kk in range(2):
                            kt = 2 * q + kk
                            at = slice(kk * BLOCK + KV_COLS, (kk + 1) * BLOCK)
                            x_hi, x_lo = hi[:, kt, i * P:(i + 1) * P], lo[:, kt, i * P:(i + 1) * P]
                            dst = bank[3][:, i * KV_COLS:(i + 1) * KV_COLS]
                            begin, end = q == 0 and kk == 0 and i == 0, q == PER_BLOCK - 1 and kk == 1
                            pe.matmul(dst, x_hi, w_hi[:, slot, at], start=begin, stop=False, skip_group_check=True)
                            pe.matmul(dst, x_hi, w_lo[:, slot, at], start=False, stop=False, skip_group_check=True)
                            mm = pe.matmul(dst, x_lo, w_hi[:, slot, at], start=False, stop=end, skip_group_check=True)
                    mm.then_inc(granule_used, 1)
                pe.wait_ge(rope_x, 3)
                block(8, (bank[0], bank[1]))
                pe.wait_ge(wi_ready, 1)
                pe.wait_ge(rope_done, 3)
                for step in range(4):
                    i = step // 2
                    if step >= 2:
                        pe.wait_ge(idx_relu, 2 * (step - 1))
                    for j in range(2):
                        for e in range(2):
                            pair = 2 * (step % 2) + j
                            at = slice(e * HD, (e + 1) * HD)
                            mm = pe.matmul(bank[4 + 2 * (step % 2) + e][:, j * SEQ:(j + 1) * SEQ],
                                           S["qiT"][at, pair, i * P:(i + 1) * P], S["kiT"][at, :], start=True, stop=True)
                    mm.then_inc(idx_full, 1)
                pe.wait_ge(rope_x, 4)
                pe.wait_ge(v_ready, 1)
                block(12, (bank[2], bank[3]))

                units = TILES * KV_HEADS

                def logits(u):
                    i, n, slot = u // KV_HEADS, u % KV_HEADS, u % 2
                    if u >= 2:
                        pe.wait_ge(p_ready, u - 1)
                    for e in range(2):
                        pe.matmul(bank[2 * slot + e][:, :].rearrange("p (j s) -> p j s", j=2), ident_bf,
                                  S["bias"][:, i:i + 1, :].broadcast_to([P, 2, SEQ]), start=True, stop=False, skip_group_check=True)
                    for j in range(2):
                        for e in range(2):
                            at = slice(e * HD, (e + 1) * HD)
                            mm = pe.matmul(bank[2 * slot + e][:, j * SEQ:(j + 1) * SEQ],
                                           S["qT"][at, 2 * n + j, i * P:(i + 1) * P], S["kT"][at, n, :],
                                           start=False, stop=True, skip_group_check=True)
                    mm.then_inc(s_full, 1)

                def turn_probs(u):
                    pe.wait_ge(p_ready, u + 1)
                    if u >= 1:
                        pe.wait_ge(pT_ready, u)
                        pe.wait_ge(pT_ready_act, u)
                    for s in range(TILES):
                        for c in range(GROUP):
                            mm = pe.transpose(bank[4 + s][:, c * P:(c + 1) * P], S["p"][:, u % 2, c, s * P:(s + 1) * P], ident)
                        mm.then_inc(pT_full, 1)

                def values(u):
                    n, slot = u % KV_HEADS, u % 2
                    pe.wait_ge(pT_ready, u + 1)
                    pe.wait_ge(pT_ready_act, u + 1)
                    if u >= 2:
                        pe.wait_ge(o_ready, u - 1)
                    for c in range(GROUP):
                        for s in range(TILES):
                            mm = pe.matmul(bank[6 + slot][:, c * HD:(c + 1) * HD], S["pT"][:, slot, s, c * P:(c + 1) * P],
                                           S["v"][:, s, n * HD:(n + 1) * HD], start=s == 0, stop=s == TILES - 1)
                    mm.then_inc(o_full, 1)

                pe.wait_ge(rope_x, 8)
                pe.wait_ge(rope_done, 8)
                pe.wait_ge(k_spread, 1)
                pe.wait_ge(selected, TILES)
                logits(0)
                for u in range(units):
                    if u + 1 < units:
                        logits(u + 1)
                    if u >= 1:
                        values(u - 1)
                    turn_probs(u)
                values(units - 1)
                pe.wait_ge(o_ready, units)
                turn(1, S["o"])
                out_linear("dsa_out", 1)

            def mlp(l):
                base, done = STREAM[f"mlp{l}"], 2 * FF_STEPS * l
                hi, lo = act_hi[0], act_lo[0]
                turn(2 + 2 * l, xn, TILES * (1 + 2 * l))
                for q in range(PER_BLOCK):
                    wait_act(2 + l, q)
                    feature_granule(base + q, (base + q) % RING, hi, lo, q, (bank[6], bank[7]))

                def down(it, k0, slot, first, last):
                    for q in range(PER_BLOCK):
                        g, at_slot = it * 8 + (base + k0 + q), (base + k0 + q) % RING
                        pe.wait_ge(lo_ready, g + 1)
                        if q % 2 == 0:
                            pe.wait_ge(mid_lo, it * 2 + (done + q // 2 + 1))
                        for i in range(TILES):
                            x_hi, x_lo = (m[:, slot, q, i * P:(i + 1) * P] for m in (M["hi"], M["lo"]))
                            for n in range(2):
                                at = slice(n * BLOCK, (n + 1) * BLOCK)
                                dst = bank[2 + 2 * i + n][:, :]
                                pe.matmul(dst, x_hi, w_hi[:, at_slot, at], start=first and q == 0, stop=False, skip_group_check=True)
                                pe.matmul(dst, x_hi, w_lo[:, at_slot, at], start=False, stop=False, skip_group_check=True)
                                mm = pe.matmul(dst, x_lo, w_hi[:, at_slot, at], start=False, stop=last and q == PER_BLOCK - 1,
                                               skip_group_check=True)
                        mm.then_inc(granule_used, 1)

                def step(it, first):
                    if not first:
                        pe.wait_ge(up_relu, it * 2 + (done + 2))
                    feature_block(base, 4, hi, lo, (bank[0], bank[1]), it)
                    down(it, 8, 0, first, False)

                step(0, True)
                with pe.Fori(1, FF_STEPS - 1) as it:
                    step(it, False)
                down(FF_STEPS - 1, 4, 1, False, True)
                modulation(l)

            def modulation(l):
                for n in range(3):
                    pe.wait_ge(mod_used[n], KT * (l + 1))
                pe.wait_ge(up_relu, 2 * FF_STEPS * (l + 1))
                for k in range(2 * KT):
                    mm = pe.matmul(bank[7][:, k:k + 1], M["mod_all"][:, k * P:(k + 1) * P], ones[:, 0:1], start=True, stop=True)
                mm.then_inc(mod_full, 1)
                for n, b in enumerate((6, 0)):
                    at = 2 * D + n * BLOCK
                    pe.matmul(bank[b][:, :], ones, M["mod_all"][:, at:at + BLOCK], start=True, stop=True).then_inc(mod_full, 1)
                pe.wait_ge(mod_ready, 4 * (l + 1))

            def rwkv_in():
                base = STREAM["rkv"]
                turn(3, xn, 2 * TILES)

                def lora(m, names):
                    for at, width in names:
                        for kt in range(KT):
                            if at == 0 and kt % 2 == 0:
                                pe.wait_ge(mixed, 4 * (3 + m) + kt // 2 + 1)
                            mm = pe.matmul(bank[4 + m][0:width, (at > 0) * SEQ:((at > 0) + 1) * SEQ],
                                           R[("w1", "a1", "g1")[m]][:, kt, at:at + width], act_f[:, kt, :],
                                           start=kt == 0, stop=kt == KT - 1)
                    mm.then_inc(lora_full, 1)

                pe.wait_ge(lora_loaded, 16 * 6)
                for n in range(6):
                    c = n // 2
                    hi, lo, banks = act_hi[c % 2], act_lo[c % 2], (bank[2 * (n % 2)], bank[2 * (n % 2) + 1])
                    if n >= 2:
                        pe.wait_ge(rkv_copied, 2 * (n - 1))
                    for q in range(PER_BLOCK):
                        if n % 2 == 0:
                            pe.wait_ge(mix_lo, 4 * c + q + 1)
                        g = base + PER_BLOCK * n + q
                        if c < 2:
                            feature_granule(g, g % RING, hi, lo, q, banks)
                        else:
                            token_granule(g, g % RING, hi, lo, (2 * q, 2 * q + 1), BLOCK, (banks[0][:, :], banks[1][:, :]),
                                          q == 0, q == PER_BLOCK - 1)
                    if n == 3:
                        lora(0, ((0, LORA),))
                    if n == 4:
                        lora(1, ((0, LORA),))
                lora(2, ((0, P), (P, GLORA - P)))

            def rwkv_mid():
                pe.wait_ge(mid_ready, 3)
                pe.wait_ge(rkv_copied, 12)
                for b in range(8):
                    for j in range(2):
                        pair = 2 * (b % 4) + j
                        mm = pe.matmul(bank[b][:, j * SEQ:(j + 1) * SEQ], R["w2" if b < 4 else "a2"][:, pair * P:(pair + 1) * P],
                                       R["mid"][0:LORA, b // 4, :], start=True, stop=True)
                    mm.then_inc(lora2_full, 1)

                def head_sums(b, values, of):
                    for pair in range(PAIRS):
                        mm = pe.matmul(bank[b][0:HEADS, 0:SEQ], of[:, pair, :], values[:, pair, :], start=pair == 0, stop=pair == PAIRS - 1)
                    return mm

                pe.wait_ge(lora2_ready, 8)
                pe.wait_ge(rw_act, 1)
                head_sums(0, R["pinv"], head_of).then_inc(rw_pe, 1)
                pe.wait_ge(rw_inverse, 1)
                for b in range(4):
                    spread(4 + b, root_head).then_inc(rw_pe, 1)
                pe.wait_ge(rw_dve, 7)
                head_sums(1, R["pinv"], head_rk).then_inc(rw_pe, 1)

            def spread(b, rows, first=None):
                first = 2 * (b % 4)
                for j in range(2):
                    mm = pe.matmul(bank[b][:, j * SEQ:(j + 1) * SEQ], R["rows_of"][:, first + j, :], rows[0:HEADS, :], start=True, stop=True)
                return mm

            def scan_loop():
                known = iter(range(1, SCAN_PE + 1))
                heads = [slice(0, CHUNK), slice(CHUNK, P)]
                tiles = [(c, h, heads[h]) for c in range(CHUNKS) for h in range(2)]

                def Q(u, c):
                    return R["inv"][u][:, 0, c, :]

                def M(u, c):
                    return R["inv"][u][:, 1, c, :]

                def N(u, c):
                    return scan["n"][u][:, c, :]

                with pe.Fori(0, SCAN_TURNS) as it:
                    def of(sem_, per, n):
                        pe.wait_ge(sem_, it * per + n)

                    def before(sem_, per, n):
                        value = pe.to_reg(it * per + n)
                        pe.wait_ge(hi_ready, next(known))
                        pe.wait_ge(sem_, value)

                    def each(b, left, right):
                        for c in range(CHUNKS):
                            mm = pe.matmul(bank[b][:, c * P:(c + 1) * P], left(c), right(c), start=True, stop=True)
                        return mm

                    def turn_each(u, b, a):
                        for c in range(CHUNKS):
                            mm = pe.transpose(bank[b][:, c * P:(c + 1) * P], a(u, c), ident)
                        return mm

                    def inv(u, a):
                        return lambda c: a(u, c)

                    def step(scalar, vector, products):
                        for u in range(2):
                            if scalar and vector:
                                of(sc_act, SCAN_ACT, SCAN_BASE + scalar + u)
                            before(*((sc_dve, SCAN_DVE, SCAN_BASE + vector + u) if vector else (sc_act, SCAN_ACT, SCAN_BASE + scalar + u)))
                            products(u, 4 * u).then_inc(sc_pe, 1)

                    for u in range(2):
                        B, prod = 4 * u, scan["prod"][u]
                        of(sc_act, SCAN_ACT, SCAN_BASE - 1 + u)
                        of(sc_dve, SCAN_DVE, SCAN_BASE - 1 + u)
                        of(sc_prod, 2, 1 + u)
                        for c in range(CHUNKS):
                            pe.transpose(bank[B][:, c * P:(c + 1) * P], scan["bk"][u][:, c, :, :].rearrange("p s t -> p (s t)"), ident)
                        for c in range(CHUNKS):
                            mm = pe.transpose(bank[B + 1][:, c * P:(c + 1) * P], prod[:, c, 0, :, :].rearrange("p h t -> p (h t)"), ident)
                        mm.then_inc(sc_pe, 1)
                        for c in range(CHUNKS):
                            mm = pe.matmul(bank[B + 2 + c // 2][:, c % 2 * 2 * P:(c % 2 + 1) * 2 * P],
                                           scan["bk"][u][:, c, :, :].rearrange("p s t -> p (s t)"), prod[:, c, :, :, :].rearrange("p a h t -> p (a h t)"), start=True, stop=True)
                        mm.then_inc(sc_pe, 1)

                    def first(u, B):
                        turn_each(u, B + 2, N)
                        for c, h, rows in tiles:
                            values = heads[1 - h]
                            mm = pe.matmul(bank[B + 3][rows, c * CHUNK:(c + 1) * CHUNK], scan["att"][u][values, CHUNKS * h + c, 0, :],
                                           scan["zz"][u][values, CHUNKS * h + c, 1, :], start=True, stop=True)
                        return mm

                    for u in range(2):
                        of(sc_pool, 2, 1 + u)
                        before(sc_dve, SCAN_DVE, SCAN_BASE + 2 + 3 * u)
                        first(u, 4 * u).then_inc(sc_pe, 1)

                    def squares(u, B):
                        each(B, inv(u, M), inv(u, N))
                        return each(B + 1, inv(u, N), inv(u, M))

                    def fourth(u, B):
                        each(B + 2, inv(u, M), inv(u, Q))
                        each(B + 3, inv(u, M), inv(u, N))
                        return each(B, inv(u, N), inv(u, M))

                    def eighth(u, B):
                        each(B + 1, inv(u, M), inv(u, Q))
                        return each(B + 2, inv(u, N), inv(u, M))

                    for u in range(2):
                        of(sc_dve, SCAN_DVE, SCAN_BASE + 3 + 3 * u)
                        before(sc_act, SCAN_ACT, SCAN_BASE + 3 + u)
                        squares(u, 4 * u).then_inc(sc_pe, 1)
                    step(5, 7, fourth)
                    step(7, 9, eighth)
                    step(9, 11, lambda u, B: each(B + 3, inv(u, M), inv(u, Q)))
                    step(None, 13, lambda u, B: turn_each(u, B, Q))
                    step(11, None, lambda u, B: each(B + 1, inv(u, N), inv(u, M)))
                    step(13, None, lambda u, B: each(B + 2, inv(u, M), inv(u, Q)))
                    step(None, 17, lambda u, B: turn_each(u, B + 3, Q))
                    step(15, 15, lambda u, B: each(B, inv(u, N), inv(u, M)))
                    step(17, None, lambda u, B: each(B + 1, inv(u, M), inv(u, Q)))
                    def removed_values(u, B):
                        for c in range(CHUNKS):
                            mm = pe.matmul(bank[B + 2 + c // 2][:, c % 2 * P:(c % 2 + 1) * P], Q(u, c),
                                           scan["aw"][u][:, c, :, :].rearrange("p a t -> p (a t)"), start=True, stop=True)
                        return mm

                    step(None, 19, removed_values)

                    def results(u, B):
                        zz, tok, att = scan["zz"][u], scan["tok"][u], scan["att"][u]

                        def put(b, n, rows, left, right):
                            return pe.matmul(bank[b][rows, n * CHUNK:(n + 1) * CHUNK], left, right, start=True, stop=True)

                        def removed(c, h):
                            return zz[heads[h], CHUNKS * h + c, 0, :]

                        def keys(c, h):
                            return tok[:, c, h * RN:(h + 1) * RN]

                        def both(c, h):
                            return zz[:, CHUNKS * h + c, 1, :]

                        for c, h, rows in tiles:
                            if 1 <= c <= 2:
                                put(B, c - 1, rows, removed(c, h), keys(c, h)[rows, :])
                        for c, h, rows in tiles:
                            if c >= 1:
                                put(B, 1 + c, rows, removed(c, h), att[rows, CHUNKS * h + c, 1, :])
                        for h, rows in enumerate(heads):
                            for c in range(CHUNKS):
                                if c <= 2:
                                    put(B, 5 + c, rows, keys(c, h), both(c, h))
                                mm = put(B + 1, c, rows, both(c, h), att[:, CHUNKS * h + c, 1, :])
                        return mm

                    for u in range(2):
                        of(sc_act, SCAN_ACT, SCAN_BASE + 19 + u)
                        before(sc_dve, SCAN_DVE, SCAN_BASE + 21 + u)
                        results(u, 4 * u).then_inc(sc_pe, 1)

            def rwkv_out():
                halves = [slice(0, RN), slice(RN, P)]

                def chunk_products(b, left, right):
                    for pair in range(PAIRS):
                        for at in halves:
                            mm = pe.matmul(bank[b][at, pair * RN:(pair + 1) * RN], left(at, pair), right(at, pair), start=True, stop=True)
                    return mm

                def chunk(t, c):
                    return lambda at, pair: t[at, pair, c * CHUNK:(c + 1) * CHUNK]

                def states(c):
                    return chunk(R["pinv"], 0) if c == 1 else lambda at, pair: state[at, c - 2, pair, :]

                pe.wait_ge(sc_dve, SCAN_BASE + SCAN_DVE * SCAN_TURNS)
                pe.wait_ge(sc_act, SCAN_BASE + SCAN_ACT * SCAN_TURNS)
                for c in range(1, CHUNKS):
                    if c > 1:
                        pe.wait_ge(chain_ready, c - 1)
                    if c < CHUNKS - 1:
                        chunk_products(c - 1, chunk(R["sg"], c), states(c)).then_inc(chain_full, 1)
                    if c > 2:
                        pe.wait_ge(y_ready, c - 2)
                    chunk_products(2 + c % 2, states(c), chunk(R["rT"], c)).then_inc(y_full, 1)
                    if c == 1:
                        for b in range(4):
                            for k in range(CHUNKS):
                                mm = pe.transpose(bank[4 + b][:, k * P:(k + 1) * P], R["v"][:, k, b * P:(b + 1) * P], ident)
                            mm.then_inc(vT_full, 1)
                pe.wait_ge(g2_loaded, 32)
                for b in range(4):
                    pe.wait_ge(vT_ready, b + 1)
                    for j in range(2):
                        at, dst = slice((2 * b + j) * P, (2 * b + j + 1) * P), bank[4 + b][:, j * SEQ:(j + 1) * SEQ]
                        pe.matmul(dst, R["g2a"][:, at], R["mid"][:, 2, :], start=True, stop=False)
                        mm = pe.matmul(dst, R["g2b"][:, at], R["mid"][0:GLORA - P, 3, :], start=False, stop=True)
                    mm.then_inc(glora_full, 1)
                pe.wait_ge(y_ready, CHUNKS - 1)
                for b in range(4):
                    spread(b, R["mid"][:, 0, :]).then_inc(bonus_full, 1)
                for b in range(4):
                    pe.wait_ge(glora_ready, b + 1)
                    pe.matmul(bank[4 + b][:, :], view["head_mean"], R["cum"][:, 2 * b:2 * b + 2, :], start=True, stop=True).then_inc(mean_full, 1)
                pe.wait_ge(centred, 4)
                for pair in range(PAIRS):
                    if pair % 2 == 0:
                        pe.wait_ge(dev_sq, pair // 2 + 1)
                    mm = pe.matmul(bank[4][0:HEADS, 0:SEQ], head_of[:, pair, :], R["pinv"][:, pair, :], start=pair == 0, stop=pair == PAIRS - 1)
                mm.then_inc(var_full, 1)
                pe.wait_ge(rw_inverse, 2)
                for b in range(4):
                    spread(4 + b, root_head).then_inc(spread_full, 1)
                for n in range(2):
                    for q in range(PER_BLOCK):
                        if n == 0:
                            pe.wait_ge(mix_lo, 12 + q + 1)
                        g = STREAM["rwkv_out"] + PER_BLOCK * n + q
                        token_granule(g, g % RING, act_hi[0], act_lo[0], (2 * q, 2 * q + 1), BLOCK,
                                      (bank[2 * n][:, :], bank[2 * n + 1][:, :]), q == 0, q == PER_BLOCK - 1)

            def conv():
                base = STREAM["conv"]
                hi, lo = act_hi[0], act_lo[0]
                turn(5, xn, 4 * TILES)
                for half in range(2):
                    for n, (left, count) in enumerate(((conv_x, 1), (conv_t, 1), (conv_b, 1), (conv_z, 2))):
                        if half:
                            pe.wait_ge(left, count)
                        for q in range(PER_BLOCK):
                            if n == half == 0:
                                wait_act(4, q)
                            g = base + 16 * half + 4 * n + q
                            feature_granule(g, g % RING, hi, lo, q, (bank[2 * n], bank[2 * n + 1]))
                pe.wait_ge(conv_x, 2)
                pe.wait_ge(conv_t, 2)
                out_linear("conv_out", 5, 1)

            def dilated():
                base = STREAM["dil"]
                hi, lo = act_hi[0], act_lo[0]
                turn(6, xn, 5 * TILES)
                for q in range(PER_BLOCK):
                    wait_act(6, q)
                with pe.Fori(0, 6) as it:
                    for n in range(2):
                        pe.wait_ge(rope_x, it * 4 + (6 + 2 * n))
                        feature_block(base, 4 * n, hi, lo, (bank[2 * n], bank[2 * n + 1]), it)
                for n in range(4):
                    if n < 2:
                        pe.wait_ge(rope_x, 30 + 2 * n)
                    else:
                        pe.wait_ge(vz_copied, 2 * (n - 1))
                    token_block(base, PER_BLOCK * (12 + n), hi, lo, [bank[2 * (n % 2) + i][:, :] for i in range(TILES)])

                units = DIL_HEADS * TILES

                def logits(u):
                    h, i, slot = u // TILES, u % TILES, u % 2
                    if u >= 2:
                        pe.wait_ge(p_ready, 8 + u - 1)
                    pe.matmul(bank[2 * slot][:, :].rearrange("p (g s) -> p g s", g=2), ident_bf, dil_mask[:, i, 0:2, :], start=True, stop=False, skip_group_check=True)
                    pe.matmul(bank[2 * slot + 1][:, 0:SEQ], ident_bf, dil_mask[:, i, 2, :], start=True, stop=False, skip_group_check=True)
                    for g in range(DIL_GROUPS):
                        q = g * DIL_HEADS + h
                        mm = pe.matmul(bank[2 * slot + g // 2][:, g % 2 * SEQ:(g % 2 + 1) * SEQ], L["qk"][:, q, i * P:(i + 1) * P],
                                       L["qk"][:, DIL_GROUPS * DIL_HEADS + q, :], start=False, stop=True, skip_group_check=True)
                    mm.then_inc(s_full, 1)

                def turn_probs(u):
                    pe.wait_ge(probs_sum, 2 * u + 2)
                    if u >= 2:
                        pe.wait_ge(pT_ready_act, 8 + u - 1)
                    for s in range(TILES):
                        mm = pe.transpose(bank[4 + u % 2][:, s * P:(s + 1) * P], LA["p"][:, u % 2, 0, s * P:(s + 1) * P], ident)
                    mm.then_inc(pT_full, 1)

                def values(u):
                    h, slot = u // TILES, u % 2
                    pe.wait_ge(pT_ready_act, 8 + u + 1)
                    if u >= 2:
                        pe.wait_ge(o_ready, 8 + u - 1)
                    for s in range(TILES):
                        mm = pe.matmul(bank[6 + slot][:, 0:P], LA["pT"][:, slot, s, :], L["v"][:, s, h * P:(h + 1) * P], start=s == 0, stop=s == TILES - 1)
                    mm.then_inc(o_full, 1)

                pe.wait_ge(vz_copied, 8)
                pe.wait_ge(rope_done, 32)
                logits(0)
                for u in range(units):
                    if u + 1 < units:
                        logits(u + 1)
                    if u >= 1:
                        values(u - 1)
                    turn_probs(u)
                values(units - 1)
                pe.wait_ge(o_ready, 8 + units)
                turn(7, L["z"])
                out_linear("dil_out", 7)

            init()
            dsa()
            mlp(0)
            rwkv_in()
            rwkv_mid()
            scan_loop()
            rwkv_out()
            mlp(1)
            conv()
            dilated()


def kernel(**inputs):
    import ml_dtypes
    from concourse import bacc as _bacc
    from concourse.bass_utils import run_bass_kernel_spmd

    parts, rows_of, parts_bf = shape_constants()
    arrays = {name: np.asarray(value) for name, value in inputs.items() if np.size(value)}
    arrays["const"] = np.concatenate([v.reshape(P, -1) for v in parts.values()], 1)
    arrays["const_bf"] = np.concatenate([v.reshape(P, -1) for v in parts_bf.values()], 1).astype(ml_dtypes.bfloat16)
    arrays["rows_of"] = rows_of[:HEADS].reshape(HEADS, -1)
    nc = _bacc.Bacc("TRN2", target_bir_lowering=False, num_devices=1)
    A = {name: nc.dram_tensor(f"in_{name}_dram", value.shape, mybir.dt.from_np(value.dtype), kind="ExternalInput").ap()
         for name, value in arrays.items()}
    out = nc.dram_tensor("out_dram", (1, SEQ, D), F32, kind="ExternalOutput").ap()
    program(nc, A, out)
    feed = {f"in_{name}_dram": value for name, value in arrays.items()}
    result = run_bass_kernel_spmd(nc, [feed], core_ids=[0])
    return np.asarray(result.results[0]["out_dram"])
```

```python
from contextlib import ExitStack

import numpy as np

import concourse.bass as bass
from concourse import mybir

F32 = mybir.dt.float32
F32R = mybir.dt.float32r
BF16 = mybir.dt.bfloat16
ACT = mybir.ActivationFunctionType
ALU = mybir.AluOpType
AX = mybir.AxisListType

P = 128
SEQ = 256
TILES = SEQ // P
D = 1024
KT = D // P
EPS = 1e-6
ROPE_THETA = 10000.0
NEG = -1e30
TAKEN = -2e30

GRAN = 1024
BLOCK = 512
PER_BLOCK = 4
RING = 4

HEADS, KV_HEADS, HD = 16, 4, 64
GROUP = HEADS // KV_HEADS
IDX_HEADS = 8
TOPK = SEQ // 4
Q_COLS = HEADS * HD
KV_COLS = KV_HEADS * HD
IQ_COLS = IDX_HEADS * HD
OFF_K = Q_COLS
OFF_V = OFF_K + KV_COLS
OFF_IQ = OFF_V + KV_COLS
OFF_IK = OFF_IQ + IQ_COLS
OFF_IW = OFF_IK + HD
IDX_SCALE = IDX_HEADS ** -0.5 * HD ** -0.5

PARAMS = ("mixer_norm", "mlp_norm", "norm_g_2", "rwkv_mu", "conv_k_2", "c_2", "b_mod_2", "rwkv_w0", "rwkv_a0",
          "rwkv_k_k", "rwkv_k_a", "rwkv_r_k", "rwkv_lnx_w", "rwkv_lnx_b")
PARAM_COLS = 232

FF = 4 * D
FF_STEPS = FF // BLOCK

RN = 64
PAIRS = D // P
CHUNK = 64
CHUNKS = SEQ // CHUNK
DECAY_SCALE = -float(np.exp(-0.5))
LNX_EPS = 64e-5
LORA, GLORA = 64, 160
GHALF = GLORA // 2

DIL_HEADS, DIL_HD, DIL_GROUPS = 8, 128, 3
DIL_RATES, DIL_HALF = (1, 4, 16), (64, 64, 64)

STREAM = {}
_at = 0
for _name, _blocks in (("dsa", 4), ("dsa_out", 2), ("mlp0", 16), ("rkv", 6), ("rwkv_out", 2), ("mlp1", 16),
                       ("conv", 8), ("conv_out", 2), ("dil", 16), ("dil_out", 2)):
    STREAM[_name] = _at
    _at += _blocks * PER_BLOCK


def rope_rows(dim, rows):
    inv = (1.0 / (np.float32(ROPE_THETA) ** (np.arange(0, dim, 2, dtype=np.float32) / np.float32(dim)))).astype(np.float32)
    ang = np.arange(SEQ, dtype=np.float32)[None, :] * inv[:, None]
    cos, sin = np.cos(ang), np.sin(ang)
    both = np.stack([np.concatenate([cos, cos]), np.concatenate([-sin, sin])], 1)
    return np.tile(both, (rows // dim, 1, 1)).astype(np.float32)


def shape_constants():
    p = np.arange(P)
    t = np.arange(SEQ)
    ident = np.eye(P, dtype=np.float32)
    row = p[:, None] % CHUNK
    col = np.arange(CHUNK)[None, :]
    strict, incl = (row < col).astype(np.float32), (row <= col).astype(np.float32)
    scan_mask = np.concatenate([strict, incl], 1)
    block16, block32 = (row // 16 == col // 16), (row // 32 == col // 32)
    split_mask = np.concatenate([block16, block32 & ~block16, ~block32], 1).astype(np.float32)
    head_mean = np.kron(np.eye(2), np.full((RN, RN), 1.0 / RN)).astype(np.float32)
    head_of = np.zeros((P, PAIRS, HEADS), np.float32)
    for pair in range(PAIRS):
        for h in range(2):
            head_of[h * RN:(h + 1) * RN, pair, 2 * pair + h] = 1.0
    rows_of = np.zeros((P, PAIRS, P), np.float32)
    rows_of[:HEADS] = head_of.transpose(2, 1, 0)
    parts = {
        "ident": ident,
        "rope64": rope_rows(HD, P),
        "rope128": rope_rows(DIL_HD, P),
        "unit": (row == col).astype(np.float32),
        "scan_mask": scan_mask,
        "split_mask": split_mask,
        "head_mean": head_mean,
        "keep": np.tile((t % CHUNK != 0).astype(np.float32), (P, 1)),
        "head_of": head_of,
        "ones": np.ones((P, P), np.float32),
    }
    causal = np.where(t[None, None, :] <= (p[:, None, None] + P * np.arange(TILES)[None, :, None]), 0.0, NEG)
    dil = np.zeros((P, TILES, DIL_GROUPS, SEQ))
    for i in range(TILES):
        for g in range(DIL_GROUPS):
            q, k, r = p[:, None] + P * i, t[None, :], DIL_RATES[g]
            seen = ((q - k) % r == 0) & (np.abs(q - k) <= DIL_HALF[g] * r)
            dil[:, i, g] = np.where(seen, 0.0, NEG)
    parts_bf = {"ident_bf": ident, "causal": causal, "dil_mask": dil}
    return parts, rows_of, parts_bf


def program(nc, A, out):
    parts, _, parts_bf = shape_constants()
    with ExitStack() as keep:
        def sem(name):
            return keep.enter_context(nc.semaphore(name))

        def room(stack):
            return lambda name, shape, dt=F32: stack.enter_context(nc.sbuf_tensor(name, shape, dt))

        sb = room(keep)
        bank = [keep.enter_context(nc.psum_tensor(f"bank{b}", [P, BLOCK], F32)) for b in range(8)]

        raw = sb("raw", [P, RING, GRAN])
        w_hi = sb("w_hi", [P, RING, GRAN], F32R)
        w_lo = sb("w_lo", [P, RING, GRAN], F32R)
        X = sb("X", [P, TILES, D])
        n_const = sum(int(np.prod(v.shape[1:])) for v in parts.values())
        n_const_bf = sum(int(np.prod(v.shape[1:])) for v in parts_bf.values())
        const = sb("const", [P, n_const])
        const_bf = sb("const_bf", [P, n_const_bf], BF16)
        gate = sb("gate", [P, 2, D])
        scale_row = sb("scale_row", [P, D])
        pcol = sb("pcol", [P, PARAM_COLS])
        mod_col = sb("mod_col", [P, 2, 2 * KT])
        gain = sb("gain", [P, 2, KT])
        c_col = sb("c_col", [P, KT])
        stat = sb("stat", [P, 8])
        half_neg = sb("half_neg", [P, SEQ])
        per_head = sb("per_head", [HEADS, SEQ])
        root_head = sb("root_head", [HEADS, SEQ])
        head_rk = sb("head_rk", [P, PAIRS, HEADS])

        view, at = {}, 0
        for name, v in parts.items():
            n = int(np.prod(v.shape[1:]))
            view[name] = const[:, at:at + n]
            at += n
        at = 0
        for name, v in parts_bf.items():
            n = int(np.prod(v.shape[1:]))
            view[name] = const_bf[:, at:at + n]
            at += n
        ident, ident_bf, ones, unit = view["ident"], view["ident_bf"], view["ones"], view["unit"]
        rope64 = view["rope64"].rearrange("p (a t) -> p a t", a=2)
        rope128 = view["rope128"].rearrange("p (a t) -> p a t", a=2)
        causal = view["causal"].rearrange("p (i s) -> p i s", i=TILES)
        dil_mask = view["dil_mask"].rearrange("p (i g s) -> p i g s", i=TILES, g=DIL_GROUPS)
        scan_mask = view["scan_mask"].rearrange("p (m t) -> p m t", m=2)
        split_mask = view["split_mask"].rearrange("p (m t) -> p m t", m=3)
        head_of = view["head_of"].rearrange("p (a h) -> p a h", a=PAIRS)

        def scope(plan):
            with ExitStack() as s:
                return plan(room(s))

        def scan_plan(t):
            return dict(
                prod=[t(f"prod{u}", [P, CHUNKS, 2, 2, CHUNK]) for u in range(2)],
                bk=[t(f"bk{u}", [P, CHUNKS, 2, CHUNK]) for u in range(2)],
                tok=[t(f"tok{u}", [P, CHUNKS, P]) for u in range(2)],
                aw=[t(f"aw{u}", [P, CHUNKS, 2, CHUNK]) for u in range(2)],
                att=[t(f"att{u}", [P, 8, 2, CHUNK]) for u in range(2)],
                zz=[t(f"zz{u}", [P, 8, 2, CHUNK]) for u in range(2)],
                n=[t(f"n{u}", [P, CHUNKS, P]) for u in range(2)],
            )

        def xn_plan(t):
            t("xn_under", [P, 3 * KT * SEQ])
            return t("xn", [P, TILES, D])

        scan = scope(scan_plan)
        state = scan["prod"][0][:, :, :, :, :].rearrange("p c a h n -> p (c a h) n").rearrange("p (s a) n -> p s a n", s=2)
        xn = scope(xn_plan)

        def bonus_plan(t):
            t("bonus_under", [P, 2 * (2 * SEQ * 2 + 3 * 2 * SEQ)])
            return t("bonus_prod", [P, PAIRS, SEQ])

        bonus_prod = scope(bonus_plan)
        act_f = sb("act_f", [P, KT, SEQ])
        act_hi, act_lo = [], []
        for u in range(2):
            act_hi.append(sb(f"act_hi{u}", [P, KT, SEQ], F32R))
            act_lo.append(sb(f"act_lo{u}", [P, KT, SEQ], F32R))

        def dsa_plan(t):
            return dict(
                qT=t("qT", [P, HEADS // 2, SEQ]), kT=t("kT", [P, KV_HEADS, 2, SEQ]),
                k_rot=t("k_rot", [P, 2, SEQ]),
                qiT=t("qiT", [P, IDX_HEADS // 2, SEQ]), ki_rot=t("ki_rot", [P, SEQ]), kiT=t("kiT", [P, 2, SEQ]),
                v=t("v", [P, TILES, KV_COLS]), wi=t("wi", [P, TILES, IDX_HEADS]),
                xs=t("xs", [P, 2, BLOCK]), rot=t("rot", [P, 2, BLOCK]),
                relu=t("relu", [P, 4, BLOCK]), score=t("score", [P, TILES, SEQ]),
                top8=t("top8", [P, TILES, 8]), bias=t("sel_bias", [P, TILES, SEQ], BF16),
                p=t("probs", [P, 2, GROUP, SEQ]), pT=t("probsT", [P, 2, TILES, BLOCK]),
                mx=t("mx", [P, 2, GROUP]), nb=t("nb", [P, 2, GROUP]), den=t("den", [P, 2, GROUP]),
                rden=t("rden", [P, 2, GROUP]), o=t("o_dsa", [P, TILES, D]),
                w_idx=t("w_idx", [P, KT, 2 * HD + IDX_HEADS]),
            )

        def mlp_plan(t):
            return dict(relu=t("ff_relu", [P, 2, BLOCK]), sq=t("ff_sq", [P, 2, BLOCK]),
                        mod_w=t("mod_w", [P, 3, D]),
                        mod_all=t("mod_all", [P, 3 * D]),
                        hi=t("ff_hi", [P, 2, 4, SEQ], F32R), lo=t("ff_lo", [P, 2, 4, SEQ], F32R))

        def rwkv_plan(t):
            with ExitStack() as s:
                tt = room(s)
                over = dict(rT=tt("rT", [P, PAIRS, SEQ]), kT=tt("kT_r", [P, PAIRS, SEQ]),
                            v_inv=tt("v_inv", [P, CHUNKS, D]), rows_of=tt("rows_of", [HEADS, PAIRS, P]),
                            mid=tt("mid", [P, 4, SEQ]), pc=tt("pc", [P, PAIRS, CHUNKS]))
                over["v"] = over["v_inv"][:, 0:2, :].rearrange("p a n -> p (a n)").rearrange("p (c n) -> p c n", c=CHUNKS)
                over["inv"] = [over["v_inv"][:, 2 + u, :].rearrange("p (a c t) -> p a c t", a=2, c=CHUNKS) for u in range(2)]
                over["w2a2"] = over["v_inv"][:, 2, :]
                with ExitStack() as s2:
                    t2 = room(s2)
                    over.update(hT=t2("hT", [P, KT, SEQ + 1]), xx=t2("xx", [P, KT, SEQ]),
                                w1=t2("w1", [P, KT, LORA]), a1=t2("a1", [P, KT, LORA]),
                                g1=t2("g1", [P, KT, GLORA]))
                with ExitStack() as s2:
                    t2 = room(s2)
                    for n in ("kk", "pinv", "cum", "sg", "a"):
                        over[n] = t2(n, [P, PAIRS, SEQ])
                over["g2a"] = over["kk"][0:GHALF, 0:4, :].rearrange("p a t -> p (a t)")
                over["g2b"] = over["kk"][0:GHALF, 4:8, :].rearrange("p a t -> p (a t)")
                return over

        def conv_plan(t):
            return dict(xin=t("xin", [P, 4, SEQ]), t=t("tpad", [P, 4, SEQ + 2]), cv=t("cv", [P, 4, SEQ]),
                        sz=t("sz", [P, 4, SEQ]), y=t("y_conv", [P, 4, SEQ]),
                        tmp=t("gated_conv", [P, 2, BLOCK]))

        def dil_plan(t):
            return dict(qk=t("qk", [P, 2 * DIL_GROUPS * DIL_HEADS, SEQ]), v=t("v_dil", [P, TILES, D]),
                        z=t("z_dil", [P, TILES, D]), xs=t("xs_d", [P, 2, BLOCK]), rot=t("rot_d", [P, 2, BLOCK]))

        def dil_att_plan(t):
            t("dil_under", [P, 64 * SEQ])
            return dict(p=t("p_dil", [P, 2, DIL_GROUPS, SEQ]), pT=t("pT_dil", [P, 2, TILES, P]),
                        mx=t("mx_d", [P, 2, 2]), nb=t("nb_d", [P, 2]), den=t("den_d", [P, 2, 2]), rden=t("rden_d", [P, 2, 2]),
                        tmp=t("gated_dil", [P, 2, BLOCK]))

        S = scope(dsa_plan)
        M = scope(mlp_plan)
        R = scope(rwkv_plan)
        C = scope(conv_plan)
        L = scope(dil_plan)
        LA = scope(dil_att_plan)

        def column(first, n=KT):
            return pcol[:, first:first + n]

        MIXER = [column(KT * l) for l in range(2)]
        MLPN = [column(16 + KT * l) for l in range(2)]
        NORM2 = [column(32 + KT * l) for l in range(2)]
        MU = [column(48 + KT * c) for c in range(6)]
        CONV_K = [column(96 + KT * w) for w in range(3)]
        COND = column(120)
        B_MOD = [column(128 + 24 * l, 16) for l in range(2)]
        W0, A0, K_K, K_A, R_K, LNX_W, LNX_B = (column(176 + KT * n) for n in range(7))

        loaded = [sem(f"granule_loaded{s}") for s in range(RING)]
        hi_ready, lo_ready, granule_used = sem("hi_ready"), sem("lo_ready"), sem("granule_used")
        x_loaded, ident_loaded, params_loaded, const_loaded = (sem(n) for n in ("x_loaded", "ident_loaded", "params_loaded", "const_loaded"))
        idx_w_loaded, lora_loaded, g2_loaded = sem("idx_w_loaded"), sem("lora_loaded"), sem("g2_loaded")
        scale_loaded, gate_loaded = sem("scale_loaded"), sem("gate_bias_loaded")
        half_ready = sem("half_ready")
        cond_ready = sem("cond_ready")
        squared, rstd_ready, rstd_step = sem("squared"), sem("rstd_ready"), sem("rstd_step")
        xn_ready, turned, f_ready = sem("xn_ready"), sem("turned"), sem("f_ready")
        act_hi_ready, act_lo_ready = sem("act_hi_ready"), sem("act_lo_ready")
        x_updated, x_step = sem("x_updated"), sem("x_step")
        idx_proj = sem("idx_proj")
        rope_x, rope_step, rope_done = sem("rope_x"), sem("rope_step"), sem("rope_done")
        k_spread, v_ready, wi_ready = sem("k_spread"), sem("v_ready"), sem("wi_ready")
        k_zero, ki_spread = sem("k_zeros"), sem("ki_spread")
        idx_full, idx_relu, scored, top_step, selected = (sem(n) for n in ("idx_full", "idx_relu", "scored", "top_step", "selected"))
        s_full, max_ready, nb_ready, p_ready = sem("s_full"), sem("max_ready"), sem("nb_ready"), sem("p_ready")
        pT_full, pT_ready, pT_ready_act, o_full, rden_ready, o_ready = (sem(n) for n in ("pT_full", "pT_ready", "pT_ready_act", "o_full", "rden_ready", "o_ready"))
        mod_loaded, mod_scaled, mod_used = ([sem(f"mod_{w}{n}") for n in range(3)] for w in ("loaded", "scaled", "used"))
        mod_full, mod_ready = sem("mod_full"), sem("mod_ready")
        up_relu, up_sq, mid_hi, mid_lo = sem("up_relu"), sem("up_sq"), sem("mid_hi"), sem("mid_lo")
        ff_opened = sem("ff_opened")
        hT_edge, shifted, mixed, mix_hi, mix_lo = (sem(n) for n in ("hT_edge", "shifted", "mixed", "mix_hi", "mix_lo"))
        rkv_copied = sem("rkv_copied")
        lora_full, mid_ready, lora2_full, lora2_ready = (sem(n) for n in ("lora_full", "mid_ready", "lora2_full", "lora2_ready"))
        rw_pe, rw_act, rw_dve, rw_root, rw_inverse = (sem(n) for n in ("rwkv_products", "rwkv_scalar", "rwkv_vector", "rwkv_root", "rwkv_inverse"))
        hT_ready, mid_zero, bonus_ready = sem("hT_ready"), sem("mid_zeros"), sem("bonus_products")
        chain_full, chain_scaled, chain_ready, y_full, y_ready = (sem(n) for n in ("chain_full", "chain_scaled", "chain_ready", "y_full", "y_ready"))
        vT_full, vT_ready, glora_full, glora_ready = (sem(n) for n in ("vT_full", "vT_ready", "glora_full", "glora_ready"))
        mean_full, centred, dev_sq, var_full, var_ready = (sem(n) for n in ("mean_full", "centred", "dev_sq", "var_full", "var_ready"))
        spread_full, normed, lnx_ready, bonus_full, out_step, mixer_out = (sem(n) for n in ("spread_full", "normed", "lnx_ready", "bonus_full", "out_step", "mixer_out"))
        sc_zero = sem("scan_zeros")
        sc_pe, sc_act, sc_dve, sc_pool, sc_prod = sem("scan_products"), sem("scan_scalar"), sem("scan_vector"), sem("scan_pool"), sem("scan_operands")
        conv_x, conv_t, conv_b, conv_z = (sem(n) for n in ("conv_x", "conv_t", "conv_b", "conv_z"))
        conv_edge, conv_tap, conv_y = sem("conv_edge"), sem("conv_tap"), sem("conv_y")
        vz_copied, probs_sum = sem("vz_copied"), sem("probs_sum")
        out_ready, stored = sem("out_ready"), sem("stored")

        SCAN_PE, SCAN_DVE, SCAN_ACT, SCAN_BASE, SCAN_TURNS = 30, 24, 22, 2, PAIRS // 2

        MLP_TURN = (4, 5, 2, 3)

        block = keep.enter_context(nc.Block())

        def seen(i):
            return (i + 1) * P

        def turned_units(u):
            return u + max(0, u - KV_HEADS)

        turned_before = turned_units(TILES * KV_HEADS)

        def number(base, k, it, turn=8):
            return base + k if it is None else it * turn + (base + k)

        @block.sync
        def _(sp):
            def load(base, k, src, it=None, turn=8):
                g, slot = number(base, k, it, turn), (base + k) % RING
                if it is not None or g >= RING:
                    sp.wait_ge(lo_ready, g - RING + 1)
                dst = raw[:, slot, :]
                if len(src.shape) == 3:
                    dst = dst.rearrange("p (k n) -> p k n", k=src.shape[1])
                sp.dma_start(dst, src).then_inc(loaded[slot], 16)

            def columns(w):
                return w.rearrange("(k p) (b n) -> p k b n", p=P, n=BLOCK)

            def load_out(name, w):
                for n in range(2):
                    for q in range(PER_BLOCK):
                        load(STREAM[name], PER_BLOCK * n + q, columns(w)[:, 2 * q:2 * q + 2, n, :])

            def load_dsa():
                w = A["dsa_w_in"][0].rearrange("(k p) n -> p k n", p=P)
                for n, first in enumerate((OFF_IQ, OFF_K, 0, BLOCK)):
                    for q in range(PER_BLOCK):
                        load(STREAM["dsa"], PER_BLOCK * n + q, w[:, 2 * q:2 * q + 2, first:first + BLOCK])
                load_out("dsa_out", A["dsa_w_o"][0])

            def load_mlp(l):
                base = STREAM[f"mlp{l}"]
                up = columns(A["mlp_w_up"][l])
                down = A["mlp_w_down"][l].rearrange("(j q p) n -> p j q n", p=P, q=PER_BLOCK)
                for q in range(PER_BLOCK):
                    load(base, q, up[:, 2 * q:2 * q + 2, 0, :])
                with sp.Fori(0, FF_STEPS - 1) as it:
                    for q in range(PER_BLOCK):
                        load(base, PER_BLOCK + q, up[:, 2 * q:2 * q + 2, it + 1, :], it)
                    for q in range(PER_BLOCK):
                        load(base, 2 * PER_BLOCK + q, down[:, it, q, :], it)
                for q in range(PER_BLOCK):
                    load(base, 8 * FF_STEPS - PER_BLOCK + q, down[:, FF_STEPS - 1, q, :])

            def load_rwkv():
                w = A["rwkv_w_rkv"][0].rearrange("c (k p) (b n) -> p c k b n", p=P, n=BLOCK)
                with sp.Fori(0, 3) as it:
                    for n in range(2):
                        for q in range(PER_BLOCK):
                            load(STREAM["rkv"], PER_BLOCK * n + q, w[:, it, 2 * q:2 * q + 2, n, :], it)
                load_out("rwkv_out", A["rwkv_w_o"][0])

            def load_conv():
                w = A["conv_w_in_2"][0].rearrange("(k p) (c h n) -> p k c h n", p=P, h=2, n=BLOCK)
                for half in range(2):
                    for n, kind in enumerate((2, 1, 0, 3)):
                        for q in range(PER_BLOCK):
                            load(STREAM["conv"], 16 * half + PER_BLOCK * n + q, w[:, 2 * q:2 * q + 2, kind, half, :])
                load_out("conv_out", A["conv_w_out_2"][0])

            def load_dil():
                w = columns(A["dil_w_in_2"][0])
                with sp.Fori(0, 8) as it:
                    for n in range(2):
                        for q in range(PER_BLOCK):
                            load(STREAM["dil"], PER_BLOCK * n + q, w[:, 2 * q:2 * q + 2, it * 2 + n, :], it)
                load_out("dil_out", A["dil_w_out_2"][0])

            def store():
                for i in range(TILES):
                    sp.wait_ge(out_ready, i + 1)
                    sp.dma_start(out[0, i * P:(i + 1) * P, :], xn[:, i, :]).then_inc(stored, 16)
                sp.wait_ge(stored, 16 * TILES)

            for i in range(TILES):
                sp.dma_start(X[:, i, :], A["x"][0, i * P:(i + 1) * P, :]).then_inc(x_loaded, 16)
            load_dsa()
            load_mlp(0)
            load_rwkv()
            load_mlp(1)
            load_conv()
            load_dil()
            store()

        @block.gpsimd
        def _(pool):
            def rstd(n):
                for i in range(TILES):
                    count = TILES * n + i + 1
                    pool.wait_ge(squared, count)
                    pool.tensor_scalar(stat[:, 2 + i:3 + i], stat[:, i:i + 1], 1.0 / D, EPS, ALU.mult, ALU.add).then_inc(rstd_step, 1)
                    pool.wait_ge(rstd_step, count)
                    pool.tensor_tensor(stat[:, 4 + i:5 + i], stat[:, 2 + i:3 + i], half_neg[:, 0:1], ALU.pow).then_inc(rstd_ready, 1)

            def key_zeros():
                pool.memset(S["kiT"][:, :, :], 0.0).then_inc(k_zero, 1)
                pool.memset(S["kT"][:, :, :, :], 0.0).then_inc(k_zero, 1)

            def modulation(l):
                w = A["w_mod_2"][l].rearrange("(k p) (n c) -> n k p c", p=P, c=D)
                done = KT * l

                def load(n, k):
                    pool.dma_start(M["mod_w"][:, n, :], w[n, k]).then_inc(mod_loaded[n], 16)

                def take(n, k):
                    part, total = M["mod_w"][:, n, :], M["mod_all"][:, n * D:(n + 1) * D]
                    pool.wait_ge(mod_scaled[n], k + (done + 1))
                    if isinstance(k, int) and k == 0:
                        pool.tensor_copy(total, part).then_inc(mod_used[n], 1)
                    else:
                        pool.tensor_tensor(total, total, part, ALU.add).then_inc(mod_used[n], 1)
                    pool.wait_ge(mod_used[n], k + (done + 1))

                for n in range(3):
                    load(n, 0)
                for n in range(3):
                    take(n, 0)
                    load(n, 1)
                with pool.Fori(1, KT - 1) as k:
                    for n in range(3):
                        take(n, k)
                        load(n, k + 1)
                for n in range(3):
                    take(n, KT - 1)

            def load_lora():
                pool.wait_ge(x_updated, 8)
                pool.wait_ge(mod_ready, 4)
                pool.memset(R["hT"][:, :, 0:1], 0.0).then_inc(hT_edge, 1)
                pool.memset(R["mid"][:, 0:2, :], 0.0).then_inc(mid_zero, 1)
                for name in ("w1", "a1", "g1"):
                    pool.dma_start(R[name][:], A[f"rwkv_{name}"][0].rearrange("(k p) n -> p k n", p=P)).then_inc(lora_loaded, 16)
                for name, rows in (("w2", slice(0, LORA)), ("a2", slice(LORA, P))):
                    pool.dma_start(R["w2a2"][rows, :], A[f"rwkv_{name}"][0]).then_inc(lora_loaded, 16)
                pool.dma_start(R["rows_of"][:], A["rows_of"].rearrange("h (a p) -> h a p", p=P)).then_inc(lora_loaded, 16)

            def scan_zeros():
                pool.wait_ge(lora_full, 3)
                for u in range(2):
                    pool.memset(scan["prod"][u][:, :, :, :, :], 0.0)
                    pool.memset(scan["n"][u][:, :, :], 0.0).then_inc(sc_zero, 1)
                pool.wait_ge(sc_zero, 2)

            def bonus_products():
                pool.wait_ge(rw_dve, 6)
                pool.tensor_tensor(bonus_prod[:, :, :], R["rT"][:, :, :], R["kT"][:, :, :], ALU.mult).then_inc(bonus_ready, 1)
                pool.wait_ge(bonus_ready, 1)

            def scan_values():
                with pool.Fori(0, SCAN_TURNS) as it:
                    for u in range(2):
                        pool.wait_ge(sc_dve, it * SCAN_DVE + (SCAN_BASE - 1 + u))
                        for h, rows in enumerate((slice(CHUNK, P), slice(0, CHUNK))):
                            copied = pool.tensor_copy(scan["zz"][u][rows, CHUNKS * h:CHUNKS * (h + 1), 1, :],
                                                      R["v"][rows, :, bass.ds(it * P + u * CHUNK, CHUNK)])
                        copied.then_inc(sc_pool, 1)

            def load_g2():
                pool.wait_ge(sc_prod, 2 * SCAN_TURNS)
                g2 = A["rwkv_g2"][0]
                pool.dma_start(R["g2a"], g2[0:GHALF, :]).then_inc(g2_loaded, 16)
                pool.dma_start(R["g2b"], g2[GHALF:GLORA, :]).then_inc(g2_loaded, 16)

            def conv_edges():
                pool.wait_ge(x_updated, 16)
                pool.memset(C["t"][:, :, 0:1], 0.0).then_inc(conv_edge, 1)
                pool.memset(C["t"][:, :, SEQ + 1:SEQ + 2], 0.0).then_inc(conv_edge, 1)

            pool.memset(half_neg[:, :], -0.5).then_inc(half_ready, 1)
            pool.wait_ge(half_ready, 1)
            rstd(0)
            key_zeros()
            rstd(1)
            modulation(0)
            rstd(2)
            load_lora()
            scan_zeros()
            bonus_products()
            scan_values()
            load_g2()
            rstd(3)
            modulation(1)
            rstd(4)
            conv_edges()
            rstd(5)
            rstd(6)
            rstd(7)

        @block.scalar
        def _(act):
            def split_hi(base, k, it=None, turn=8):
                g, slot = number(base, k, it, turn), (base + k) % RING
                lap = (base + k) // RING + 1
                act.wait_ge(loaded[slot], 16 * lap if it is None else it * (16 * turn // RING) + 16 * lap)
                if it is not None or g >= RING:
                    act.wait_ge(granule_used, g - RING + 1)
                act.activation(w_hi[:, slot, :], raw[:, slot, :], ACT.Copy).then_inc(hi_ready, 1)

            def split_block(base, k0, it=None, turn=8):
                for q in range(PER_BLOCK):
                    split_hi(base, k0 + q, it, turn)

            known = iter(range(1, PER_BLOCK * 6))

            def before_moving(sem_, count):
                value = act.to_reg(count)
                act.wait_ge(lo_ready, next(known))
                act.wait_ge(sem_, value)

            def square(i, sem_, count):
                act.wait_ge(sem_, count)
                act.activation(xn[:, i, :], X[:, i, :], ACT.Square, accum_out=stat[:, i:i + 1]).then_inc(squared, 1)

            def squares(*updated):
                for i in range(TILES):
                    square(i, x_updated, updated[i])

            def round_f(f):
                for b in range(4):
                    act.wait_ge(f_ready, 4 * f + b + 1)
                    act.activation(act_hi[0][:, 2 * b:2 * b + 2, :], act_f[:, 2 * b:2 * b + 2, :], ACT.Copy).then_inc(act_hi_ready, 1)

            def round_turned(n):
                for b in range(4):
                    act.wait_ge(turned, 4 * n + b + 1)
                    act.activation(act_hi[0][:, 2 * b:2 * b + 2, :].rearrange("p k t -> p (k t)"), bank[4 + b][:, :], ACT.Copy).then_inc(act_hi_ready, 1)

            def rope_move(r, k, src, xs, rot, n, half):
                if not isinstance(r, int) or r >= 2:
                    act.wait_ge(rope_done, r - 1)
                slot = k % 2
                act.activation(xs[:, slot, 0:n], src, ACT.Copy)
                for first in range(0, P, half):
                    to = first + half if (first // half) % 2 == 0 else first - half
                    mv = act.activation(rot[to:to + half, slot, 0:n], src[first:first + half, :], ACT.Copy)
                mv.then_inc(rope_x, 1)

            def init():
                act.dma_start(const[:, 0:P], A["const"][:, 0:P]).then_inc(ident_loaded, 16)
                act.dma_start(pcol[:, :], A["params"]).then_inc(params_loaded, 16)
                act.dma_start(S["w_idx"][:, :, :], A["w_idx"]).then_inc(idx_w_loaded, 16)
                for i in range(TILES):
                    square(i, x_loaded, 16 * TILES)
                act.dma_start(const[:, P:n_const], A["const"][:, P:n_const]).then_inc(const_loaded, 16)
                act.dma_start(const_bf[:, :], A["const_bf"]).then_inc(const_loaded, 16)
                act.dma_start(scale_row[:, :], A["final_norm"].partition_broadcast(P)).then_inc(scale_loaded, 16)
                for l in range(2):
                    act.dma_start(gate[:, l, :], A["b_mod_2"][l, 2 * D:3 * D].partition_broadcast(P)).then_inc(gate_loaded, 16)
                act.wait_ge(params_loaded, 16)
                act.activation(c_col[:, :], COND, ACT.Silu).then_inc(cond_ready, 1)

            def dsa():
                base = STREAM["dsa"]

                def rope_bank(r, b, n=BLOCK):
                    rope_move(r, r, bank[b][:, 0:n], S["xs"], S["rot"], n, HD // 2)

                split_block(base, 0)
                round_f(0)
                act.wait_ge(idx_proj, 1)
                rope_bank(0, 4, SEQ)
                act.wait_ge(idx_proj, 2)
                act.activation(S["wi"][:, :, :], bank[5][:, 0:TILES * IDX_HEADS].rearrange("p (i h) -> p i h", i=TILES),
                               ACT.Copy, scale=IDX_SCALE).then_inc(wi_ready, 1)
                split_block(base, 4)
                act.wait_ge(granule_used, base + 4)
                rope_bank(1, 0)
                rope_bank(2, 1)
                act.wait_ge(k_zero, 2)
                act.wait_ge(rope_done, 1)
                for half in range(2):
                    rows = slice(half * HD, (half + 1) * HD)
                    mv = act.activation(S["kiT"][rows, half, :], S["ki_rot"][rows, :], ACT.Copy)
                mv.then_inc(ki_spread, 1)
                split_block(base, 8)
                act.wait_ge(granule_used, base + 8)
                rope_bank(3, 2)
                act.activation(S["v"][:, :, :], bank[3][:, :].rearrange("p (i n) -> p i n", i=TILES), ACT.Copy).then_inc(v_ready, 1)
                for n in range(8):
                    act.wait_ge(idx_full, n // 2 + 1)
                    if n >= 4:
                        act.wait_ge(scored, 2 * (n - 3))
                    wide = 2 * seen(n // 4)
                    act.activation(S["relu"][:, n % 4, 0:wide], bank[4 + n % 4][:, 0:wide], ACT.Relu).then_inc(idx_relu, 1)
                act.wait_ge(rope_done, 4)
                for n in range(KV_HEADS):
                    for half in range(2):
                        mv = act.activation(S["kT"][half * HD:(half + 1) * HD, n, half, :],
                                            S["k_rot"][(n % 2) * HD:(n % 2 + 1) * HD, n // 2, :], ACT.Copy)
                mv.then_inc(k_spread, 1)
                split_block(base, 12)
                act.wait_ge(granule_used, base + 12)
                rope_bank(4, 0)
                rope_bank(5, 1)
                act.wait_ge(granule_used, base + 16)
                rope_bank(6, 6)

                units = TILES * KV_HEADS
                def exps(u):
                    slot = u % 2
                    act.wait_ge(nb_ready, u + 1)
                    if u >= 2:
                        act.wait_ge(pT_full, turned_units(u - 1))
                        act.wait_ge(rden_ready, u - 1)
                    w = seen(u // KV_HEADS)
                    for c in range(GROUP):
                        j, e = c // 2, c % 2
                        ex = act.activation(S["p"][:, slot, c, 0:w], bank[2 * slot + j][:, e * w:(e + 1) * w], ACT.Exp,
                                            bias=S["nb"][:, slot, c:c + 1], scale=HD ** -0.5,
                                            accum_out=S["den"][:, slot, c:c + 1])
                    ex.then_inc(p_ready, 1)

                def copy_pT(u):
                    act.wait_ge(pT_full, turned_units(u + 1))
                    if u >= 2:
                        act.wait_ge(o_full, u - 1)
                    act.activation(S["pT"][:, u % 2, 1, :], bank[5][:, :], ACT.Copy).then_inc(pT_ready_act, 1)

                for u in range(units):
                    exps(u)
                    if u == 0:
                        rope_bank(7, 7)
                    if u >= KV_HEADS:
                        copy_pT(u)
                    if u < PER_BLOCK:
                        split_hi(STREAM["dsa_out"], u)
                round_turned(1)
                split_block(STREAM["dsa_out"], 4)

            def mlp(l):
                base, done = STREAM[f"mlp{l}"], 2 * FF_STEPS * l
                split_block(base, 0)
                squares(*((3, 4) if l == 0 else (11, 12)))
                round_f(1 + l)

                def relu(it, first_bank):
                    act.wait_ge(granule_used, it * 8 + (base + (4 if isinstance(it, int) and it == 0 else 0)))
                    for b in range(2):
                        act.activation(M["relu"][:, b, :], bank[first_bank + b][:, :], ACT.Relu).then_inc(up_relu, 1)

                def round_mid(it, slot):
                    for b in range(2):
                        act.wait_ge(up_sq, it * 2 + (done + b + 1))
                        act.activation(M["hi"][:, slot, 2 * b:2 * b + 2, :], M["sq"][:, b, :].rearrange("p (k t) -> p k t", k=2), ACT.Copy).then_inc(mid_hi, 1)

                def scale_mod(k):
                    for n in range(3):
                        if isinstance(k, int):
                            act.wait_ge(mod_loaded[n], 16 * (KT * l + k + 1))
                        else:
                            before_moving(mod_loaded[n], k * 16 + 16 * (KT * l + 1))
                        act.activation(M["mod_w"][:, n, :], M["mod_w"][:, n, :], ACT.Copy,
                                       scale=c_col[:, k:k + 1] if isinstance(k, int) else c_col[:, bass.ds(k, 1)]).then_inc(mod_scaled[n], 1)

                def step(it, first_bank):
                    if isinstance(it, int):
                        split_block(base, 4, it)
                        relu(it, first_bank)
                    else:
                        relu(it, first_bank)
                        split_block(base, 4, it)
                    scale_mod(it)
                    split_hi(base, 8, it)
                    round_mid(it, 0)
                    for q in range(1, PER_BLOCK):
                        split_hi(base, 8 + q, it)

                step(0, 6)
                with act.Fori(1, FF_STEPS - 1) as it:
                    step(it, 0)
                last = FF_STEPS - 1
                scale_mod(last)
                relu(last, 0)
                split_hi(base, 4 + 8 * last)
                round_mid(last, 1)
                for q in range(1, PER_BLOCK):
                    split_hi(base, 4 + 8 * last + q)

            def rwkv_in():
                base = STREAM["rkv"]

                def round_mix(c):
                    for b in range(4):
                        act.wait_ge(mixed, 4 * c + b + 1)
                        act.activation(act_hi[c % 2][:, 2 * b:2 * b + 2, :], act_f[:, 2 * b:2 * b + 2, :], ACT.Copy).then_inc(mix_hi, 1)

                def leave(n):
                    act.wait_ge(granule_used, base + PER_BLOCK * (n + 1))
                    c, half = n // 2, n % 2
                    for j in range(2):
                        src = bank[2 * half + j][:, :]
                        if c < 2:
                            at = 4 * half + 2 * j
                            dst, src = R["rT" if c == 0 else "kT"][:, at:at + 2, :], src.rearrange("p (k t) -> p k t", k=2)
                            act.activation(dst, src, ACT.Copy).then_inc(rkv_copied, 1)
                        else:
                            for par in range(2):
                                of = src[par * CHUNK:(par + 1) * CHUNK, :].rearrange("p (a h v) -> p a h v", h=2, v=RN)
                                for h, rows in enumerate((slice(CHUNK, P), slice(0, CHUNK))):
                                    at = slice(half * BLOCK // 2, (half + 1) * BLOCK // 2)
                                    mv = act.activation(R["v"][rows, 2 * j + par, at].rearrange("p (a v) -> p a v", v=RN), of[:, :, h, :], ACT.Copy)
                            mv.then_inc(rkv_copied, 1)

                split_block(base, 0)
                squares(6, 8)
                round_mix(0)
                split_block(base, 4)
                round_mix(1)
                leave(0)
                split_block(base, 8)
                leave(1)
                round_mix(2)
                split_block(base, 12)
                leave(2)
                split_block(base, 16)
                leave(3)
                act.wait_ge(mid_zero, 1)
                act.wait_ge(lora_full, 1)
                act.activation(R["mid"][0:LORA, 0, :], bank[4][0:LORA, 0:SEQ], ACT.Tanh).then_inc(mid_ready, 1)
                split_block(base, 20)
                leave(4)
                act.wait_ge(lora_full, 2)
                act.activation(R["mid"][LORA:P, 1, :], bank[5][0:LORA, 0:SEQ], ACT.Copy).then_inc(mid_ready, 1)
                act.wait_ge(rw_dve, 1)
                act.activation(R["pinv"][:, :, :], R["kk"][:, :, :], ACT.Square).then_inc(rw_act, 1)
                split_block(STREAM["rwkv_out"], 0)
                leave(5)
                act.wait_ge(lora_full, 3)
                act.activation(R["mid"][0:GHALF, 2, :], bank[6][0:GHALF, 0:SEQ], ACT.Sigmoid)
                act.activation(R["mid"][0:GHALF, 3, :], bank[6][0:GHALF, SEQ:2 * SEQ], ACT.Sigmoid).then_inc(mid_ready, 1)

            def root(ready, count):
                act.wait_ge(ready, count)
                act.activation(root_head[:, :], per_head[:, :], ACT.Sqrt).then_inc(rw_root, 1)

            def rwkv_mid():
                for pair in range(PAIRS):
                    act.wait_ge(lora2_full, pair + 1)
                    for j, (bias, dst) in enumerate(((W0, R["sg"]), (A0, R["a"]))):
                        sg = act.activation(dst[:, pair, :], bank[pair][:, j * SEQ:(j + 1) * SEQ], ACT.Sigmoid, bias=bias[:, pair:pair + 1])
                    sg.then_inc(lora2_ready, 1)
                root(rw_dve, 2)
                act.wait_ge(rw_dve, 4)
                act.activation(R["sg"][:, :, :], R["sg"][:, :, :], ACT.Exp, scale=DECAY_SCALE)
                act.wait_ge(rw_pe, 1)
                act.activation(R["pinv"][:, :, :], R["cum"][:, :, :], ACT.Exp, scale=-DECAY_SCALE).then_inc(rw_act, 1)
                act.wait_ge(rw_act, 2)
                act.activation(R["cum"][:, :, :], R["cum"][:, :, :], ACT.Exp, scale=DECAY_SCALE).then_inc(rw_act, 2)
                act.wait_ge(rw_act, 4)
                for half in range(2):
                    at = slice(4 * half, 4 * half + 4)
                    act.activation(R["pc"][:, at, :], R["cum"][:, at, :].rearrange("p a (c t) -> p a c t", c=CHUNKS)[:, :, :, CHUNK - 1], ACT.Copy).then_inc(sc_act, 1)

            def scan_loop():
                with act.Fori(0, SCAN_TURNS) as it:
                    def step(first, move):
                        for u in range(2):
                            act.wait_ge(sc_pe, it * SCAN_PE + (first + u * (2 if first == 1 else 1)))
                            move(u, 4 * u).then_inc(sc_act, 1)

                    def tiles(b):
                        return bank[b][:, :].rearrange("p (c t) -> p c t", c=CHUNKS)

                    def M(u):
                        return R["inv"][u][:, 1, :, :]

                    def N(u):
                        return scan["n"][u][:, :, :]

                    def keep_turned(u, B):
                        act.activation(scan["tok"][u][:, :, :], bank[B][:, :].rearrange("p (c n) -> p c n", c=CHUNKS), ACT.Copy)
                        for h, rows in enumerate((slice(0, CHUNK), slice(CHUNK, P))):
                            kept = act.activation(scan["aw"][u][rows, :, 0, :], tiles(B + 1)[rows, :, h * RN:(h + 1) * RN], ACT.Copy)
                        return kept

                    def keep(to, b):
                        return lambda u, B: act.activation(to(u), tiles(B + b), ACT.Copy)

                    def both(first, second):
                        def move(u, B):
                            first(u, B)
                            return second(u, B)
                        return move

                    step(1, keep_turned)
                    step(5, both(keep(M, 2), lambda u, B: act.activation(scan["aw"][u][:, :, 1, :], bank[B + 3][:, 0:CHUNKS * CHUNK].rearrange("p (c t) -> p c t", c=CHUNKS), ACT.Copy)))
                    step(7, keep(N, 0))
                    step(9, both(keep(N, 3), keep(M, 0)))
                    step(11, keep(M, 2))
                    step(15, keep(M, 0))
                    step(17, keep(M, 1))
                    step(21, keep(M, 3))
                    step(23, keep(M, 0))

                    def keep_removed(u, B):
                        for h, rows in enumerate((slice(0, CHUNK), slice(CHUNK, P))):
                            kept = act.activation(scan["zz"][u][rows, CHUNKS * h:CHUNKS * h + 2, :, :],
                                                  bank[B + 2][rows, 0:2 * P].rearrange("p (c a t) -> p c a t", c=2, a=2), ACT.Copy)
                        return kept

                    step(27, keep_removed)
                    for u in range(2):
                        before_moving(sc_pe, it * SCAN_PE + (29 + u))
                        act.activation(R["cum"][:, bass.ds(it * 2 + u, 1), :], bank[4 * u + 1][:, 0:SEQ].unsqueeze(1), ACT.Copy).then_inc(sc_act, 1)

            def rwkv_out():
                for b in range(4):
                    act.wait_ge(vT_full, b + 1)
                    halves = (slice(0, RN), slice(RN, P))
                    for j, rows in enumerate(halves):
                        for h, to in enumerate(halves):
                            moved = act.activation(R["kT"][to, 2 * b + j, :].rearrange("p (k t) -> p k t", k=CHUNKS),
                                                   bank[4 + b][rows, :].rearrange("p (k x t) -> p k x t", k=CHUNKS, x=2)[:, :, 1 - h, :], ACT.Copy)
                    moved.then_inc(vT_ready, 1)
                for b in range(4):
                    act.wait_ge(glora_full, b + 1)
                    act.activation(R["a"][:, 2 * b:2 * b + 2, :], bank[4 + b][:, :].rearrange("p (k t) -> p k t", k=2), ACT.Copy).then_inc(glora_ready, 1)
                for b in range(4):
                    act.wait_ge(centred, b + 1)
                    act.activation(R["pinv"][:, 2 * b:2 * b + 2, :], R["cum"][:, 2 * b:2 * b + 2, :], ACT.Square).then_inc(dev_sq, 1)
                root(var_ready, 1)

                def affine(b):
                    act.wait_ge(normed, b + 1)
                    for pair in (2 * b, 2 * b + 1):
                        ln = act.activation(R["cum"][:, pair, :], R["cum"][:, pair, :], ACT.Identity, bias=LNX_B[:, pair:pair + 1], scale=LNX_W[:, pair:pair + 1])
                    ln.then_inc(lnx_ready, 1)

                def round_out(b):
                    act.wait_ge(mixed, 24 + b + 1)
                    act.activation(act_hi[0][:, 2 * b:2 * b + 2, :], act_f[:, 2 * b:2 * b + 2, :], ACT.Copy).then_inc(mix_hi, 1)

                affine(0)
                for b in range(4):
                    if b < 3:
                        affine(b + 1)
                    round_out(b)
                split_block(STREAM["rwkv_out"], 4)

            def conv():
                base = STREAM["conv"]
                split_block(base, 0)
                squares(14, 16)
                squares(17, 18)
                act.wait_ge(x_updated, 18)
                act.dma_start(scale_row[:, :], A["final_g_2"].partition_broadcast(P)).then_inc(scale_loaded, 16)
                round_f(3)

                def two(ap, j):
                    return ap[:, 2 * j:2 * j + 2, :]

                def psum(b):
                    return bank[b][:, :].rearrange("p (k t) -> p k t", k=2)

                for half in range(2):
                    at = 16 * half
                    split_block(base, at + 4)
                    act.wait_ge(granule_used, base + at + 4)
                    if half:
                        act.wait_ge(conv_t, half)
                    for j in range(2):
                        mv = act.activation(two(C["xin"], j), psum(j), ACT.Copy)
                    mv.then_inc(conv_x, 1)
                    split_block(base, at + 8)
                    split_block(base, at + 12)
                    if half == 0:
                        split_block(base, 16)
                    else:
                        split_block(STREAM["conv_out"], 0)
                    act.wait_ge(granule_used, base + at + 16)
                    if half:
                        act.wait_ge(conv_y, 2 * half)
                    for j in range(2):
                        act.activation(two(C["sz"], j), psum(6 + j), ACT.Silu).then_inc(conv_z, 1)
                    for j in range(2):
                        act.wait_ge(conv_y, 2 * half + j + 1)
                        dst = slice(4 * half + 2 * j, 4 * half + 2 * j + 2)
                        act.activation(act_hi[1][:, dst, :], two(C["y"], j), ACT.Copy).then_inc(act_hi_ready, 1)
                split_block(STREAM["conv_out"], 4)

            def dilated():
                base = STREAM["dil"]
                split_block(base, 0)
                squares(21, 22)
                round_f(4)
                with act.Fori(0, 6) as it:
                    for n in range(2):
                        split_block(base, 4 * n + 4, it)
                        act.wait_ge(granule_used, it * 8 + (base + 4 * (n + 1)))
                        for j in range(2):
                            rope_move(it * 4 + (8 + 2 * n + j), 2 * n + j, bank[2 * n + j][:, :], L["xs"], L["rot"], BLOCK, DIL_HD // 2)
                for n in range(4):
                    if n < 3:
                        split_block(base, PER_BLOCK * (13 + n))
                    else:
                        split_block(STREAM["dil_out"], 0)
                    act.wait_ge(granule_used, base + PER_BLOCK * (13 + n))
                    for i in range(TILES):
                        dst = L["v" if n < 2 else "z"][:, i, n % 2 * BLOCK:(n % 2 + 1) * BLOCK]
                        act.activation(dst, bank[2 * (n % 2) + i][:, :], ACT.Copy if n < 2 else ACT.Silu).then_inc(vz_copied, 1)

                units = DIL_HEADS * TILES

                def exps(u):
                    slot, first = u % 2, 2 * (u % 3)
                    act.wait_ge(nb_ready, 8 + u + 1)
                    if u >= 2:
                        act.wait_ge(pT_full, turned_before + u - 1)
                    for b, to in ((0, slice(0, 2)), (1, slice(2, 3))):
                        n = SEQ * (2 - b)
                        ex = act.activation(LA["p"][:, slot, to, :], bank[first + b][:, 0:n].rearrange("p (g s) -> p g s", s=SEQ), ACT.Exp,
                                            bias=LA["nb"][:, slot:slot + 1], scale=DIL_HD ** -0.5, accum_out=LA["den"][:, slot, b:b + 1])
                    ex.then_inc(p_ready, 1)

                def copy_pT(u):
                    act.wait_ge(pT_full, turned_before + u + 1)
                    if u >= 2:
                        act.wait_ge(o_full, 8 + u - 1)
                    act.activation(LA["pT"][:, u % 2, :, :], bank[6][:, 0:SEQ].rearrange("p (s t) -> p s t", s=TILES), ACT.Copy).then_inc(pT_ready_act, 1)

                exps(0)
                exps(1)
                for u in range(units):
                    copy_pT(u)
                    if u + 2 < units:
                        exps(u + 2)
                round_turned(7)
                split_block(STREAM["dil_out"], 4)

            def final_norm():
                squares(25, 26)

            init()
            dsa()
            mlp(0)
            rwkv_in()
            rwkv_mid()
            scan_loop()
            rwkv_out()
            mlp(1)
            conv()
            dilated()
            final_norm()

        @block.vector
        def _(dve):
            def split_lo(base, k, it=None, turn=8):
                g, slot = number(base, k, it, turn), (base + k) % RING
                dve.wait_ge(hi_ready, g + 1)
                dve.tensor_tensor(w_lo[:, slot, :], raw[:, slot, :], w_hi[:, slot, :].bitcast(F32), ALU.subtract).then_inc(lo_ready, 1)

            def split_block(base, k0, it=None, turn=8):
                for q in range(PER_BLOCK):
                    split_lo(base, k0 + q, it, turn)

            def normalise(n):
                for i in range(TILES):
                    dve.wait_ge(rstd_ready, TILES * n + i + 1)
                    dve.tensor_scalar(xn[:, i, :], X[:, i, :], stat[:, 4 + i:5 + i], None, ALU.mult).then_inc(xn_ready, 1)

            def scale_turned(n, b, dst, g, ready, shift=None, banks=(4, 5, 6, 7)):
                dve.wait_ge(turned, 4 * n + b + 1)
                for kk in range(2):
                    kt = 2 * b + kk
                    src = bank[banks[b]][:, kk * SEQ:(kk + 1) * SEQ]
                    if shift is None:
                        st = dve.tensor_scalar(dst[:, kt, :], src, g[:, kt:kt + 1], None, ALU.mult)
                    else:
                        st = dve.tensor_scalar(dst[:, kt, :], src, g[:, kt:kt + 1], shift[:, kt:kt + 1], ALU.mult, ALU.add)
                st.then_inc(ready, 1)

            def scale_and_split(n, s, g, shift=None, lag=1, **where):
                for b in range(4 + lag):
                    if b < 4:
                        scale_turned(n, b, act_f, g, f_ready, shift, **where)
                    if b >= lag:
                        dve.wait_ge(act_hi_ready, 4 * s + b - lag + 1)
                        at = (slice(None), slice(2 * (b - lag), 2 * (b - lag) + 2), slice(None))
                        dve.tensor_tensor(act_lo[0][at], act_f[at], act_hi[0][at].bitcast(F32), ALU.subtract).then_inc(act_lo_ready, 1)

            def rest_turned(s):
                for b in range(4):
                    dve.wait_ge(act_hi_ready, 4 * s + b + 1)
                    at = (slice(None), slice(2 * b, 2 * b + 2), slice(None))
                    dve.tensor_tensor(act_lo[0][at], bank[4 + b][:, :].rearrange("p (k t) -> p k t", k=2),
                                      act_hi[0][at].bitcast(F32), ALU.subtract).then_inc(act_lo_ready, 1)

            def rope_sum(r, k, dst, xs, rot, table, n):
                slot, groups = k % 2, n // SEQ
                def tab(a):
                    return table[:, a:a + 1, :].broadcast_to([P, groups, SEQ])
                def grp(t):
                    return t[:, slot, 0:n].rearrange("p (g t) -> p g t", g=groups)
                dve.wait_ge(rope_x, r + 1)
                dve.tensor_tensor(dst, grp(xs), tab(0), ALU.mult)
                dve.tensor_tensor(grp(rot), grp(rot), tab(1), ALU.mult).then_inc(rope_step, 1)
                dve.wait_ge(rope_step, r + 1)
                dve.tensor_tensor(dst, dst, grp(rot), ALU.add).then_inc(rope_done, 1)

            def add_out(name, n, l=None, tmp=None):
                dve.wait_ge(granule_used, STREAM[name] + PER_BLOCK * (n + 1))
                for i in range(TILES):
                    at = slice(n * BLOCK, (n + 1) * BLOCK)
                    to, src = X[:, i, at], bank[2 * n + i][:, :]
                    if l is not None:
                        step = 4 * l + 2 * n + i
                        if n:
                            dve.wait_ge(x_updated, (18 if l == 0 else 22) + i + 1)
                        dve.tensor_tensor(tmp[:, i, :], src, gate[:, l, at], ALU.mult).then_inc(x_step, 1)
                        dve.wait_ge(x_step, step + 1)
                        src = tmp[:, i, :]
                    dve.tensor_tensor(to, to, src, ALU.add).then_inc(x_updated, 1)

            def take_out(name, following, l=None, tmp=None):
                add_out(name, 0, l, tmp)
                if following:
                    for q in range(PER_BLOCK - 1):
                        split_lo(STREAM[following], q)
                add_out(name, 1, l, tmp)
                if following:
                    split_lo(STREAM[following], PER_BLOCK - 1)

            def dsa():
                base = STREAM["dsa"]

                def rope(r, dst, n=BLOCK):
                    rope_sum(r, r, dst, S["xs"], S["rot"], rope64, n)

                normalise(0)
                dve.wait_ge(params_loaded, 16)
                scale_and_split(0, 0, MIXER[0], lag=4)
                split_block(base, 0)
                dve.wait_ge(const_loaded, 32)
                dve.tensor_tensor(head_rk[:, :, :], head_of, R_K.unsqueeze(2).broadcast_to([P, PAIRS, HEADS]), ALU.mult)
                rope(0, S["ki_rot"][:, :].unsqueeze(1), SEQ)
                split_block(base, 4)
                rope(1, S["qiT"][:, 0:2, :])
                rope(2, S["qiT"][:, 2:4, :])
                split_block(base, 8)
                rope(3, S["k_rot"][:, :, :])
                dve.wait_ge(wi_ready, 1)
                score = [S["score"][:, i, 0:seen(i)] for i in range(TILES)]
                for m in range(TILES * IDX_HEADS):
                    i, h = m // IDX_HEADS, m % IDX_HEADS
                    if h % 2 == 0:
                        dve.wait_ge(idx_relu, m // 2 + 1)
                    if h:
                        dve.wait_ge(scored, m)
                    relu = S["relu"][:, m // 2 % 4, h % 2 * seen(i):(h % 2 + 1) * seen(i)]
                    dve.scalar_tensor_tensor(score[i], relu, S["wi"][:, i, h:h + 1], score[i] if h else causal[:, i, 0:seen(i)],
                                             ALU.mult, ALU.add).then_inc(scored, 1)
                step = 0
                dve.wait_ge(scored, 16)
                for turn in range(TOPK // 8):
                    for i in range(TILES):
                        if turn:
                            dve.wait_ge(top_step, step - 1)
                        dve.max(S["top8"][:, i, :], score[i]).then_inc(top_step, 1)
                        step += 1
                    for i in range(TILES):
                        dve.wait_ge(top_step, step - 1)
                        dve.match_replace(score[i], S["top8"][:, i, :], score[i], TAKEN).then_inc(top_step, 1)
                        step += 1
                    if turn % 2:
                        split_lo(base, 12 + turn // 2)
                for i in range(TILES):
                    dve.wait_ge(top_step, step - 1 + i)
                    dve.tensor_scalar(score[i], score[i], (TAKEN + NEG) / 2, NEG, ALU.is_gt, ALU.mult).then_inc(top_step, 1)
                    dve.wait_ge(top_step, step + 1 + i)
                    dve.tensor_tensor(S["bias"][:, i, 0:seen(i)], score[i], causal[:, i, 0:seen(i)], ALU.add).then_inc(selected, 1)
                for r in range(2):
                    rope(4 + r, S["qT"][:, 2 * r:2 * r + 2, :])

                units = TILES * KV_HEADS

                def maxima(u):
                    slot = u % 2
                    dve.wait_ge(s_full, u + 1)
                    if u >= 2:
                        dve.wait_ge(p_ready, u - 1)
                    for j in range(2):
                        mx = dve.tensor_reduce(S["mx"][:, slot, 2 * j:2 * j + 2], bank[2 * slot + j][:, 0:2 * seen(u // KV_HEADS)]
                                               .rearrange("p (e t) -> p e t", e=2), AX.X, ALU.max)
                    mx.then_inc(max_ready, 1)
                    dve.wait_ge(max_ready, u + 1)
                    dve.tensor_scalar(S["nb"][:, slot, :], S["mx"][:, slot, :], -HD ** -0.5, None, ALU.mult).then_inc(nb_ready, 1)

                def copy_pT(u):
                    slot = u % 2
                    dve.wait_ge(pT_full, turned_units(u) + 1)
                    if u >= 2:
                        dve.wait_ge(o_full, u - 1)
                        dve.wait_ge(o_ready, u - 1)
                    dve.tensor_copy(S["pT"][:, slot, 0, :], bank[4][:, :]).then_inc(pT_ready, 1)
                    dve.wait_ge(p_ready, u + 1)
                    dve.reciprocal(S["rden"][:, slot, :], S["den"][:, slot, :]).then_inc(rden_ready, 1)

                def output(u):
                    i, n, slot = u // KV_HEADS, u % KV_HEADS, u % 2
                    dve.wait_ge(o_full, u + 1)
                    dve.wait_ge(rden_ready, u + 1)
                    dve.tensor_tensor(S["o"][:, i, n * SEQ:(n + 1) * SEQ].rearrange("p (c d) -> p c d", c=GROUP),
                                      bank[6 + slot][:, 0:GROUP * HD].rearrange("p (c d) -> p c d", c=GROUP),
                                      S["rden"][:, slot, :].unsqueeze(2).broadcast_to([P, GROUP, HD]), ALU.mult).then_inc(o_ready, 1)

                maxima(0)
                for u in range(units):
                    if u < 2:
                        rope(6 + u, S["qT"][:, 4 + 2 * u:6 + 2 * u, :])
                    if u + 1 < units:
                        maxima(u + 1)
                    if u >= 1:
                        output(u - 1)
                    copy_pT(u)
                    if u < PER_BLOCK:
                        split_lo(STREAM["dsa_out"], u)
                output(units - 1)
                rest_turned(1)
                split_block(STREAM["dsa_out"], 4)
                take_out("dsa_out", "mlp0")

            def mlp(l, following):
                base, done = STREAM[f"mlp{l}"], 2 * FF_STEPS * l
                normalise(1 + 2 * l)
                scale_and_split(2 + 2 * l, 2 + l, MLPN[l], banks=MLP_TURN)

                def square(it):
                    if not isinstance(it, int) or it > 0:
                        dve.wait_ge(mid_lo, it * 2 + done)
                    for b in range(2):
                        dve.wait_ge(up_relu, it * 2 + (done + b + 1))
                        dve.tensor_tensor(M["sq"][:, b, :], M["relu"][:, b, :], M["relu"][:, b, :], ALU.mult).then_inc(up_sq, 1)

                def rest_mid(it, slot):
                    for b in range(2):
                        at = (slice(None), slot, slice(2 * b, 2 * b + 2), slice(None))
                        dve.wait_ge(mid_hi, it * 2 + (done + b + 1))
                        dve.tensor_tensor(M["lo"][at], M["sq"][:, b, :].rearrange("p (k t) -> p k t", k=2),
                                          M["hi"][at].bitcast(F32), ALU.subtract).then_inc(mid_lo, 1)

                def step(it):
                    if isinstance(it, int):
                        split_block(base, 4, it)
                        square(it)
                    else:
                        square(it)
                        split_block(base, 4, it)
                    split_lo(base, 8, it)
                    rest_mid(it, 0)
                    for q in range(1, PER_BLOCK):
                        split_lo(base, 8 + q, it)

                step(0)
                with dve.Fori(1, FF_STEPS - 1) as it:
                    step(it)
                last = FF_STEPS - 1
                square(last)
                split_lo(base, 4 + 8 * last)
                rest_mid(last, 1)
                for q in range(1, PER_BLOCK):
                    split_lo(base, 4 + 8 * last + q)
                for q in range(PER_BLOCK - 1):
                    split_lo(STREAM[following], q)
                dve.wait_ge(granule_used, base + 8 * FF_STEPS)
                for i in range(TILES):
                    for n in range(2):
                        to = X[:, i, n * BLOCK:(n + 1) * BLOCK]
                        dve.tensor_tensor(to, to, bank[2 + 2 * i + n][:, :], ALU.add).then_inc(x_updated, 1)
                split_lo(STREAM[following], PER_BLOCK - 1)
                modulation(l)

            def modulation(l):
                dve.wait_ge(mod_full, 3 * l + 1)
                dve.tensor_tensor(mod_col[:, l, :], bank[7][:, 0:2 * KT], B_MOD[l], ALU.add).then_inc(mod_ready, 1)
                dve.wait_ge(mod_ready, 4 * l + 1)
                dve.scalar_tensor_tensor(gain[:, l, :], mod_col[:, l, KT:2 * KT], 1.0, NORM2[l], ALU.add, ALU.mult).then_inc(mod_ready, 1)
                dve.wait_ge(gate_loaded, 32)
                for n, b in enumerate((6, 0)):
                    dve.wait_ge(mod_full, 3 * l + 2 + n)
                    to = gate[:, l, n * BLOCK:(n + 1) * BLOCK]
                    dve.tensor_tensor(to, to, bank[b][:, :], ALU.add).then_inc(mod_ready, 1)

            def rwkv_in():
                base = STREAM["rkv"]
                hT, xx = R["hT"], R["xx"]
                normalise(2)
                dve.wait_ge(hT_edge, 1)
                def mix_part(c, b):
                    dve.wait_ge(shifted, b + 1)
                    for kt in (2 * b, 2 * b + 1):
                        mm = dve.scalar_tensor_tensor(act_f[:, kt, :], xx[:, kt, :], MU[c][:, kt:kt + 1],
                                                      hT[:, kt, 1:SEQ + 1], ALU.mult, ALU.add)
                    mm.then_inc(mixed, 1)

                def rest_part(c, b):
                    dve.wait_ge(mix_hi, 4 * c + b + 1)
                    at = (slice(None), slice(2 * b, 2 * b + 2), slice(None))
                    dve.tensor_tensor(act_lo[c % 2][at], act_f[at], act_hi[c % 2][at].bitcast(F32), ALU.subtract).then_inc(mix_lo, 1)

                def mix(c):
                    for b in range(4):
                        mix_part(c, b)

                def rest_mix(c):
                    for b in range(4):
                        rest_part(c, b)

                for b in range(4):
                    scale_turned(3, b, hT[:, :, 1:SEQ + 1], MIXER[1], hT_ready)
                    if b:
                        rest_part(0, b - 1)
                    dve.wait_ge(hT_ready, b + 1)
                    at = slice(2 * b, 2 * b + 2)
                    dve.tensor_tensor(xx[:, at, :], hT[:, at, 0:SEQ], hT[:, at, 1:SEQ + 1], ALU.subtract).then_inc(shifted, 1)
                    mix_part(0, b)
                rest_part(0, 3)
                split_block(base, 4)
                dve.wait_ge(mix_lo, 4)
                mix(1)
                rest_mix(1)
                split_block(base, 8)
                dve.wait_ge(mix_lo, 8)
                mix(2)
                rest_mix(2)
                split_block(base, 12)
                dve.wait_ge(mix_lo, 12)
                mix(3)
                split_block(base, 16)
                dve.wait_ge(lora_full, 1)
                mix(4)
                split_block(base, 20)
                dve.wait_ge(lora_full, 2)
                mix(5)
                dve.wait_ge(mixed, 24)
                dve.wait_ge(rkv_copied, 8)
                dve.tensor_tensor(R["kk"][:, :, :], R["kT"][:, :, :], K_K.unsqueeze(2).broadcast_to([P, PAIRS, SEQ]), ALU.mult).then_inc(rw_dve, 1)
                split_block(STREAM["rwkv_out"], 0)

            def invert(n):
                dve.wait_ge(rw_root, n)
                dve.reciprocal(root_head[:, :], root_head[:, :]).then_inc(rw_inverse, 1)

            def rwkv_mid():
                def all_pairs(column):
                    return column.unsqueeze(2).broadcast_to([P, PAIRS, SEQ])

                rT, kT, kk, a, sg, cum, pinv = (R[n][:, :, :] for n in ("rT", "kT", "kk", "a", "sg", "cum", "pinv"))
                dve.wait_ge(rw_pe, 1)
                dve.tensor_scalar(per_head[:, :], bank[7][0:HEADS, 0:SEQ], 1e-24, None, ALU.max).then_inc(rw_dve, 1)
                for pair in range(PAIRS):
                    dve.wait_ge(lora2_ready, pair + 1)
                    sc = dve.tensor_tensor_scan(cum[:, pair, :], view["keep"], sg[:, pair, :], 0.0, ALU.mult, ALU.add)
                sc.then_inc(rw_dve, 1)
                dve.wait_ge(rw_dve, 3)
                dve.tensor_tensor(sg, cum, sg, ALU.subtract).then_inc(rw_dve, 1)
                dve.scalar_tensor_tensor(bonus_prod[:, :, :], a, -1.0, all_pairs(K_A), ALU.add, ALU.mult).then_inc(rw_dve, 1)
                invert(1)
                dve.wait_ge(rw_dve, 5)
                dve.scalar_tensor_tensor(kT, bonus_prod[:, :, :], 1.0, kT, ALU.add, ALU.mult).then_inc(rw_dve, 1)
                for b in range(4):
                    dve.wait_ge(rw_pe, 2 + b)
                    at = slice(2 * b, 2 * b + 2)
                    nk = dve.tensor_tensor(R["kk"][:, at, :], R["kk"][:, at, :], bank[4 + b][:, :].rearrange("p (k t) -> p k t", k=2), ALU.mult)
                nk.then_inc(rw_dve, 1)
                dve.wait_ge(rw_dve, 7)
                dve.tensor_tensor(a, kk, a, ALU.mult).then_inc(sc_dve, 1)
                dve.wait_ge(rw_pe, 6)
                dve.tensor_copy(R["mid"][0:HEADS, 0, :], bank[1][0:HEADS, 0:SEQ]).then_inc(sc_dve, 1)

            def scan_loop():
                heads = [slice(0, CHUNK), slice(CHUNK, P)]

                def Q(u):
                    return R["inv"][u][:, 0, :, :]

                def M(u):
                    return R["inv"][u][:, 1, :, :]

                def N(u):
                    return scan["n"][u][:, :, :]

                def pair(t, it, u):
                    return t[:, bass.ds(it * 2 + u, 1), :]

                def operand(k, it, u):
                    a, b = ((R["kk"], R["sg"]), (R["rT"], R["cum"]), (R["a"], R["pinv"]), (R["kT"], R["pinv"]))[k]
                    a, b = (pair(x, it, u).rearrange("p a (c t) -> p (a c) t", c=CHUNKS) for x in (a, b))
                    for h, rows in enumerate(heads):
                        to = scan["prod"][u][rows, :, k, h, :] if k < 2 else scan["bk"][u][rows, :, abs(k - 2 - h), :]
                        if k == 0:
                            made = dve.scalar_tensor_tensor(to, a[rows, :, :], -1.0, b[rows, :, :], ALU.mult, ALU.mult)
                        else:
                            made = dve.tensor_tensor(to, a[rows, :, :], b[rows, :, :], ALU.mult)
                    return made

                def turn(it, following):
                    def before(n):
                        dve.wait_ge(sc_dve, it * SCAN_DVE + (SCAN_BASE + n))

                    def products(n):
                        dve.wait_ge(sc_pe, it * SCAN_PE + n)

                    def ahead(u, first, last):
                        if following:
                            for k in range(first, last):
                                op = operand(k, it + 1, u)
                            if last == 4:
                                op.then_inc(sc_prod, 1)

                    def tiles(b):
                        return bank[b][:, :].rearrange("p (c t) -> p c t", c=CHUNKS)

                    def cut(u, m):
                        for h, rows in enumerate(heads):
                            part = dve.tensor_tensor(N(u)[rows, :, h * CHUNK:(h + 1) * CHUNK], scan["att"][u][rows, CHUNKS * h:CHUNKS * (h + 1), 0, :],
                                                     split_mask[rows, m:m + 1, :].broadcast_to([CHUNK, CHUNKS, CHUNK]), ALU.mult)
                        return part

                    def grow(step, b, after=None):
                        for u in range(2):
                            inverse = Q(u)
                            products(step + u)
                            op = dve.tensor_tensor(inverse, inverse, tiles(4 * u + b), ALU.add)
                            if after:
                                op = after(u)
                            op.then_inc(sc_dve, 1)

                    for u in range(2):
                        n = 1 + 3 * u
                        products(2 * u + 2)
                        att = scan["att"][u][:, :, :, :].rearrange("p (h c) m t -> p h c m t", h=2)
                        for j in range(2):
                            for h in range(2):
                                dv = dve.tensor_tensor(att[:, h, 2 * j:2 * j + 2, :, :], bank[4 * u + 2 + j][:, :].rearrange("p (c m h t) -> p c m h t", c=2, m=2, h=2)[:, :, :, h, :],
                                                       scan_mask.unsqueeze(1).broadcast_to([P, 2, 2, CHUNK]), ALU.mult)
                        dv.then_inc(sc_dve, 1)
                        before(n)
                        cut(u, 0).then_inc(sc_dve, 1)
                        before(n + 1)
                        dve.tensor_tensor(Q(u), N(u), ident.unsqueeze(1).broadcast_to([P, CHUNKS, P]), ALU.add).then_inc(sc_dve, 1)
                    for u in range(2):
                        products(7 + u)
                        dve.tensor_copy(M(u), tiles(4 * u + 1)).then_inc(sc_dve, 1)
                    for u in range(2):
                        dve.tensor_tensor(pair(R["rT"], it, u), pair(R["rT"], it, u), pair(R["cum"], it, u), ALU.mult)
                    grow(9, 2)
                    ahead(0, 0, 2)
                    grow(11, 1)
                    ahead(0, 2, 4)
                    grow(13, 3, lambda u: cut(u, 1))
                    ahead(1, 0, 2)
                    for u in range(2):
                        products(17 + u)
                        cut(u, 2).then_inc(sc_dve, 1)
                    grow(19, 2)
                    ahead(1, 2, 4)
                    grow(25, 1)
                    for u in range(2):
                        products(27 + u)
                        for h, rows in enumerate(heads):
                            kept = dve.tensor_copy(scan["zz"][u][rows, CHUNKS * h + 2:CHUNKS * h + 4, :, :],
                                                   bank[4 * u + 3][rows, 0:2 * P].rearrange("p (c a t) -> p c a t", c=2, a=2))
                        kept.then_inc(sc_dve, 1)
                    for u in range(2):
                        products(29 + u)

                        def chunks(t, first, last):
                            return pair(t, it, u)[:, :, first * CHUNK:last * CHUNK].rearrange("p a (c t) -> p (a c) t", t=CHUNK)

                        def part(first, last):
                            return bank[4 * u][:, first * CHUNK:last * CHUNK].rearrange("p (c t) -> p c t", t=CHUNK)

                        dve.tensor_tensor(chunks(R["sg"], 1, 3), part(0, 2), unit.unsqueeze(1).broadcast_to([P, 2, RN]), ALU.add)
                        dve.tensor_tensor(chunks(R["rT"], 1, 4), part(2, 5), chunks(R["rT"], 1, 4), ALU.add)
                        decay = pair(R["pc"], it, u)[:, :, 0:3].rearrange("p a c -> p (a c)").unsqueeze(2).broadcast_to([P, 3, RN])
                        dve.tensor_tensor(chunks(R["pinv"], 0, 3), part(5, 8), decay, ALU.mult).then_inc(sc_dve, 1)

                dve.wait_ge(rw_act, 4)
                dve.wait_ge(sc_dve, SCAN_BASE)
                dve.wait_ge(sc_zero, 2)
                for u in range(2):
                    for k in range(4):
                        op = operand(k, 0, u)
                    op.then_inc(sc_prod, 1)
                with dve.Fori(0, SCAN_TURNS - 1) as it:
                    turn(it, True)
                turn(SCAN_TURNS - 1, False)

            def rwkv_out():
                F, G, Y = R["sg"], R["pinv"], R["cum"]

                def chunk(t, c):
                    return t[:, :, c * CHUNK:(c + 1) * CHUNK]

                def rows(b):
                    return bank[b][:, :].rearrange("p (a n) -> p a n", a=PAIRS)

                def add_y(c):
                    dve.wait_ge(y_full, c)
                    dve.tensor_tensor(chunk(Y, c), chunk(Y, c), rows(2 + c % 2), ALU.add).then_inc(y_ready, 1)

                dve.wait_ge(sc_act, SCAN_BASE + SCAN_ACT * SCAN_TURNS)
                for c in range(1, CHUNKS - 1):
                    dve.wait_ge(chain_full, c)
                    st = state[:, c - 1, :, :]
                    dve.tensor_tensor(st, rows(c - 1), R["pc"][:, :, c:c + 1].broadcast_to([P, PAIRS, RN]), ALU.mult).then_inc(chain_scaled, 1)
                    dve.wait_ge(chain_scaled, c)
                    dve.tensor_tensor(st, st, chunk(G, c), ALU.add).then_inc(chain_ready, 1)
                    add_y(c)
                add_y(CHUNKS - 1)
                for b in range(4):
                    at = slice(2 * b, 2 * b + 2)
                    dve.wait_ge(mean_full, b + 1)
                    dve.tensor_tensor(Y[:, at, :], Y[:, at, :], bank[4 + b][:, :].rearrange("p (k t) -> p k t", k=2), ALU.subtract).then_inc(centred, 1)
                for b in range(4):
                    at = slice(2 * b, 2 * b + 2)
                    dve.wait_ge(bonus_full, b + 1)
                    dve.wait_ge(vT_ready, 4)
                    dve.tensor_tensor(R["kT"][:, at, :], R["kT"][:, at, :], bank[b][:, :].rearrange("p (k t) -> p k t", k=2), ALU.mult).then_inc(out_step, 1)
                dve.wait_ge(var_full, 1)
                dve.tensor_scalar(per_head[:, :], bank[4][0:HEADS, 0:SEQ], 1.0 / RN, LNX_EPS, ALU.mult, ALU.add).then_inc(var_ready, 1)
                invert(2)

                def norm(b):
                    at = slice(2 * b, 2 * b + 2)
                    dve.wait_ge(spread_full, b + 1)
                    dve.tensor_tensor(Y[:, at, :], Y[:, at, :], bank[4 + b][:, :].rearrange("p (k t) -> p k t", k=2), ALU.mult).then_inc(normed, 1)

                def gated(b):
                    at = slice(2 * b, 2 * b + 2)
                    dve.wait_ge(lnx_ready, b + 1)
                    dve.tensor_tensor(Y[:, at, :], Y[:, at, :], R["kT"][:, at, :], ALU.add).then_inc(out_step, 1)
                    dve.wait_ge(out_step, 4 + b + 1)
                    dve.wait_ge(glora_ready, b + 1)
                    dve.tensor_tensor(act_f[:, at, :], Y[:, at, :], R["a"][:, at, :], ALU.mult).then_inc(mixed, 1)

                def rest_out(b):
                    at = (slice(None), slice(2 * b, 2 * b + 2), slice(None))
                    dve.wait_ge(mix_hi, 12 + b + 1)
                    dve.tensor_tensor(act_lo[0][at], act_f[at], act_hi[0][at].bitcast(F32), ALU.subtract).then_inc(mix_lo, 1)

                norm(0)
                for b in range(4):
                    if b < 3:
                        norm(b + 1)
                    gated(b)
                    if b:
                        rest_out(b - 1)
                rest_out(3)
                split_block(STREAM["rwkv_out"], 4)
                take_out("rwkv_out", "mlp1")

            def mid_norm():
                dve.wait_ge(scale_loaded, 16)
                for i in range(TILES):
                    dve.wait_ge(rstd_ready, TILES * 4 + i + 1)
                    dve.scalar_tensor_tensor(X[:, i, :], X[:, i, :], stat[:, 4 + i:5 + i], scale_row[:, :], ALU.mult, ALU.mult).then_inc(x_updated, 1)

            def conv():
                base = STREAM["conv"]
                dve.wait_ge(x_updated, 18)
                normalise(5)
                dve.wait_ge(mod_ready, 8)
                scale_and_split(5, 4, gain[:, 0, :], mod_col[:, 0, 0:KT])

                def two(ap, j):
                    return ap[:, 2 * j:2 * j + 2, :]

                def psum(b):
                    return bank[b][:, :].rearrange("p (k t) -> p k t", k=2)

                dve.wait_ge(conv_edge, 2)
                for half in range(2):
                    at = 16 * half
                    split_block(base, at + 4)
                    split_block(base, at + 8)
                    dve.wait_ge(granule_used, base + at + 8)
                    dve.wait_ge(conv_x, half + 1)
                    for j in range(2):
                        tt = dve.tensor_tensor(two(C["t"], j)[:, :, 1:SEQ + 1], psum(2 + j), two(C["xin"], j), ALU.mult)
                    tt.then_inc(conv_t, 1)
                    split_block(base, at + 12)
                    dve.wait_ge(conv_t, half + 1)
                    for w in range(3):
                        for f in range(4):
                            kt = 4 * half + f
                            taps = CONV_K[w][:, kt:kt + 1]
                            if w == 0:
                                tap = dve.tensor_scalar(C["cv"][:, f, :], C["t"][:, f, 0:SEQ], taps, None, ALU.mult)
                            else:
                                tap = dve.scalar_tensor_tensor(C["cv"][:, f, :], C["t"][:, f, w:w + SEQ], taps, C["cv"][:, f, :], ALU.mult, ALU.add)
                        tap.then_inc(conv_tap, 1)
                        dve.wait_ge(conv_tap, 3 * half + w + 1)
                    dve.wait_ge(granule_used, base + at + 12)
                    for j in range(2):
                        yy = dve.tensor_tensor(two(C["y"], j), psum(4 + j), two(C["cv"], j), ALU.mult)
                    yy.then_inc(conv_b, 1)
                    if half == 0:
                        split_block(base, 16)
                    else:
                        split_block(STREAM["conv_out"], 0)
                    dve.wait_ge(conv_b, half + 1)
                    for j in range(2):
                        dve.wait_ge(conv_z, 2 * half + j + 1)
                        dve.tensor_tensor(two(C["y"], j), two(C["y"], j), two(C["sz"], j), ALU.mult).then_inc(conv_y, 1)
                    for j in range(2):
                        dve.wait_ge(act_hi_ready, 4 * 5 + 2 * half + j + 1)
                        dst = slice(4 * half + 2 * j, 4 * half + 2 * j + 2)
                        dve.tensor_tensor(act_lo[1][:, dst, :], two(C["y"], j), act_hi[1][:, dst, :].bitcast(F32), ALU.subtract).then_inc(act_lo_ready, 1)
                split_block(STREAM["conv_out"], 4)
                take_out("conv_out", "dil", 0, C["tmp"])

            def dilated():
                base = STREAM["dil"]
                normalise(6)
                scale_and_split(6, 6, gain[:, 1, :], mod_col[:, 1, 0:KT])
                with dve.Fori(0, 6) as it:
                    for n in range(2):
                        split_block(base, 4 * n + 4, it)
                        for j in range(2):
                            rope_sum(it * 4 + (8 + 2 * n + j), 2 * n + j, L["qk"][:, bass.ds(it * 8 + (4 * n + 2 * j), 2), :], L["xs"], L["rot"], rope128, BLOCK)
                for n in range(13, 16):
                    split_block(base, PER_BLOCK * n)
                split_block(STREAM["dil_out"], 0)

                units = DIL_HEADS * TILES

                def maxima(u):
                    slot, first = u % 2, 2 * (u % 3)
                    dve.wait_ge(s_full, 8 + u + 1)
                    if u >= 2:
                        dve.wait_ge(p_ready, 8 + u - 1)
                    dve.tensor_reduce(LA["mx"][:, slot, 0:1], bank[first][:, :], AX.X, ALU.max)
                    dve.tensor_reduce(LA["mx"][:, slot, 1:2], bank[first + 1][:, 0:SEQ], AX.X, ALU.max).then_inc(max_ready, 1)
                    dve.wait_ge(max_ready, 8 + u + 1)
                    dve.tensor_scalar(LA["nb"][:, slot:slot + 1], LA["mx"][:, slot, 0:1], LA["mx"][:, slot, 1:2], -DIL_HD ** -0.5, ALU.max, ALU.mult).then_inc(nb_ready, 1)

                def join(u):
                    p, den, rden = LA["p"][:, u % 2], LA["den"][:, u % 2], LA["rden"][:, u % 2]
                    dve.wait_ge(p_ready, 8 + u + 1)
                    if u >= 2:
                        dve.wait_ge(o_ready, 8 + u - 1)
                    dve.tensor_tensor(p[:, 0, :], p[:, 0, :], p[:, 1, :], ALU.add)
                    dve.tensor_tensor(rden[:, 0:1], den[:, 0:1], den[:, 1:2], ALU.add).then_inc(probs_sum, 1)
                    dve.wait_ge(probs_sum, 2 * u + 1)
                    dve.reciprocal(rden[:, 1:2], rden[:, 0:1])
                    dve.tensor_tensor(p[:, 0, :], p[:, 0, :], p[:, 2, :], ALU.add).then_inc(probs_sum, 1)

                def output(u):
                    h, i, slot = u // TILES, u % TILES, u % 2
                    dve.wait_ge(o_full, 8 + u + 1)
                    dve.wait_ge(probs_sum, 2 * u + 2)
                    z = L["z"][:, i, h * P:(h + 1) * P]
                    dve.scalar_tensor_tensor(z, bank[7][:, 0:P], LA["rden"][:, slot, 1:2], z, ALU.mult, ALU.mult).then_inc(o_ready, 1)

                dve.wait_ge(vz_copied, 8)
                maxima(0)
                maxima(1)
                for u in range(units):
                    join(u)
                    if u + 2 < units:
                        maxima(u + 2)
                    if u >= 1:
                        output(u - 1)
                output(units - 1)
                rest_turned(7)
                split_block(STREAM["dil_out"], 4)
                take_out("dil_out", None, 1, LA["tmp"])

            def final_norm():
                dve.wait_ge(scale_loaded, 32)
                for i in range(TILES):
                    dve.wait_ge(rstd_ready, TILES * 7 + i + 1)
                    dve.scalar_tensor_tensor(xn[:, i, :], X[:, i, :], stat[:, 4 + i:5 + i], scale_row[:, :], ALU.mult, ALU.mult).then_inc(out_ready, 1)

            dsa()
            mlp(0, "rkv")
            rwkv_in()
            rwkv_mid()
            scan_loop()
            rwkv_out()
            mlp(1, "conv")
            mid_norm()
            conv()
            dilated()
            final_norm()

        @block.tensor
        def _(pe):
            def token_granule(g, slot, hi, lo, kts, n, banks, first, last, used=True):
                pe.wait_ge(lo_ready, g + 1)
                for i in range(TILES):
                    for kk, kt in enumerate(kts):
                        at = slice(kk * n, (kk + 1) * n)
                        x_hi, x_lo = hi[:, kt, i * P:(i + 1) * P], lo[:, kt, i * P:(i + 1) * P]
                        begin, end = first and kk == 0, last and kk == len(kts) - 1
                        dst = banks[i]
                        pe.matmul(dst, x_hi, w_hi[:, slot, at], start=begin, stop=False, skip_group_check=True)
                        pe.matmul(dst, x_hi, w_lo[:, slot, at], start=False, stop=False, skip_group_check=True)
                        mm = pe.matmul(dst, x_lo, w_hi[:, slot, at], start=False, stop=end, skip_group_check=True)
                mm.then_inc(granule_used, 1)

            def feature_granule(g, slot, hi, lo, q, banks, groups=range(4), inc=True):
                if inc:
                    pe.wait_ge(lo_ready, g + 1)
                for f in groups:
                    dst = banks[f // 2][:, (f % 2) * SEQ:(f % 2 + 1) * SEQ]
                    for kk in range(2):
                        kt = 2 * q + kk
                        at = slice(kk * BLOCK + f * P, kk * BLOCK + (f + 1) * P)
                        begin = q == 0 and kk == 0 and f % 2 == 0
                        end = q == PER_BLOCK - 1 and kk == 1
                        pe.matmul(dst, w_hi[:, slot, at], hi[:, kt, :], start=begin, stop=False, skip_group_check=True)
                        pe.matmul(dst, w_hi[:, slot, at], lo[:, kt, :], start=False, stop=False, skip_group_check=True)
                        mm = pe.matmul(dst, w_lo[:, slot, at], hi[:, kt, :], start=False, stop=end, skip_group_check=True)
                if inc:
                    mm.then_inc(granule_used, 1)
                return mm

            def token_block(base, k0, hi, lo, banks, it=None):
                for q in range(PER_BLOCK):
                    token_granule(number(base, k0 + q, it), (base + k0 + q) % RING, hi, lo, (2 * q, 2 * q + 1), BLOCK,
                                  banks, q == 0, q == PER_BLOCK - 1)

            def feature_block(base, k0, hi, lo, banks, it=None):
                for q in range(PER_BLOCK):
                    feature_granule(number(base, k0 + q, it), (base + k0 + q) % RING, hi, lo, q, banks)

            def turn(n, src, ready=None, banks=(4, 5, 6, 7)):
                for i in range(TILES):
                    if ready is not None:
                        pe.wait_ge(xn_ready, ready + i + 1)
                    for b in range(4):
                        for kk in range(2):
                            kt = 2 * b + kk
                            mm = pe.transpose(bank[banks[b]][:, (kk * TILES + i) * P:(kk * TILES + i + 1) * P],
                                              src[:, i, kt * P:(kt + 1) * P], ident)
                        if i == TILES - 1:
                            mm.then_inc(turned, 1)

            def wait_act(s, q):
                pe.wait_ge(act_lo_ready, 4 * s + q + 1)

            def out_linear(name, s, u=0):
                for b in range(2):
                    for q in range(PER_BLOCK):
                        if b == 0 and s is not None:
                            wait_act(s, q)
                        g = STREAM[name] + PER_BLOCK * b + q
                        token_granule(g, g % RING, act_hi[u], act_lo[u], (2 * q, 2 * q + 1), BLOCK,
                                      (bank[2 * b][:, :], bank[2 * b + 1][:, :]), q == 0, q == PER_BLOCK - 1)

            def init():
                pe.wait_ge(ident_loaded, 16)

            def dsa():
                base = STREAM["dsa"]
                hi, lo = act_hi[0], act_lo[0]

                def block(k0, banks):
                    for q in range(PER_BLOCK):
                        if k0 == 0:
                            wait_act(0, q)
                        feature_granule(base + k0 + q, (base + k0 + q) % RING, hi, lo, q, banks)

                turn(0, xn, 0)
                pe.wait_ge(f_ready, 4)
                pe.wait_ge(idx_w_loaded, 16)
                for kt in range(KT):
                    mm = pe.matmul(bank[4][:, 0:SEQ], S["w_idx"][:, kt, 0:2 * HD], act_f[:, kt, :], start=kt == 0, stop=kt == KT - 1)
                mm.then_inc(idx_proj, 1)
                for i in range(TILES):
                    for kt in range(KT):
                        mm = pe.matmul(bank[5][:, i * IDX_HEADS:(i + 1) * IDX_HEADS], act_f[:, kt, i * P:(i + 1) * P],
                                       S["w_idx"][:, kt, 2 * HD:], start=kt == 0, stop=kt == KT - 1)
                mm.then_inc(idx_proj, 1)
                block(0, (bank[0], bank[1]))
                for q in range(PER_BLOCK):
                    g = base + 4 + q
                    slot = g % RING
                    pe.wait_ge(lo_ready, g + 1)
                    feature_granule(g, slot, hi, lo, q, (bank[2],), range(2), False)
                    for i in range(TILES):
                        for kk in range(2):
                            kt = 2 * q + kk
                            at = slice(kk * BLOCK + KV_COLS, (kk + 1) * BLOCK)
                            x_hi, x_lo = hi[:, kt, i * P:(i + 1) * P], lo[:, kt, i * P:(i + 1) * P]
                            dst = bank[3][:, i * KV_COLS:(i + 1) * KV_COLS]
                            begin, end = q == 0 and kk == 0 and i == 0, q == PER_BLOCK - 1 and kk == 1
                            pe.matmul(dst, x_hi, w_hi[:, slot, at], start=begin, stop=False, skip_group_check=True)
                            pe.matmul(dst, x_hi, w_lo[:, slot, at], start=False, stop=False, skip_group_check=True)
                            mm = pe.matmul(dst, x_lo, w_hi[:, slot, at], start=False, stop=end, skip_group_check=True)
                    mm.then_inc(granule_used, 1)
                pe.wait_ge(wi_ready, 1)
                pe.wait_ge(ki_spread, 1)
                pe.wait_ge(rope_done, 3)
                for step in range(4):
                    i = step // 2
                    if step >= 2:
                        pe.wait_ge(idx_relu, 2 * (step - 1))
                    for j in range(2):
                        pair = 2 * (step % 2) + j
                        mm = pe.matmul(bank[4 + pair][:, 0:2 * seen(i)].rearrange("p (e s) -> p e s", e=2),
                                       S["qiT"][:, pair, i * P:(i + 1) * P], S["kiT"][:, :, 0:seen(i)], start=True, stop=True)
                    mm.then_inc(idx_full, 1)
                block(8, (bank[0], bank[1]))
                pe.wait_ge(idx_relu, 8)
                block(12, (bank[6], bank[7]))

                units = TILES * KV_HEADS

                def logits(u):
                    i, n, slot = u // KV_HEADS, u % KV_HEADS, u % 2
                    if u >= 2:
                        pe.wait_ge(p_ready, u - 1)
                    w = seen(i)
                    if i == 0:
                        pe.wait_ge(rope_done, 5 + n)
                    for j in range(2):
                        dst = bank[2 * slot + j][:, 0:2 * w].rearrange("p (e s) -> p e s", e=2)
                        pe.matmul(dst, ident_bf, S["bias"][:, i:i + 1, 0:w].broadcast_to([P, 2, w]), start=True, stop=False, skip_group_check=True)
                        mm = pe.matmul(dst, S["qT"][:, 2 * n + j, i * P:(i + 1) * P], S["kT"][:, n, :, 0:w],
                                       start=False, stop=True, skip_group_check=True)
                    mm.then_inc(s_full, 1)

                def turn_probs(u):
                    pe.wait_ge(p_ready, u + 1)
                    if u >= 1:
                        pe.wait_ge(pT_ready, u)
                    if u > KV_HEADS:
                        pe.wait_ge(pT_ready_act, u - KV_HEADS)
                    for s in range(u // KV_HEADS + 1):
                        for c in range(GROUP):
                            mm = pe.transpose(bank[4 + s][:, c * P:(c + 1) * P], S["p"][:, u % 2, c, s * P:(s + 1) * P], ident)
                        mm.then_inc(pT_full, 1)

                def values(u):
                    n, slot = u % KV_HEADS, u % 2
                    pe.wait_ge(pT_ready, u + 1)
                    if u == 0:
                        pe.wait_ge(rope_x, 8)
                    if u >= KV_HEADS:
                        pe.wait_ge(pT_ready_act, u + 1 - KV_HEADS)
                    if u >= 2:
                        pe.wait_ge(o_ready, u - 1)
                    for c in range(GROUP):
                        for s in range(u // KV_HEADS + 1):
                            mm = pe.matmul(bank[6 + slot][:, c * HD:(c + 1) * HD], S["pT"][:, slot, s, c * P:(c + 1) * P],
                                           S["v"][:, s, n * HD:(n + 1) * HD], start=s == 0, stop=s == u // KV_HEADS)
                    mm.then_inc(o_full, 1)

                pe.wait_ge(rope_x, 6)
                pe.wait_ge(v_ready, 1)
                pe.wait_ge(k_spread, 1)
                pe.wait_ge(const_loaded, 32)
                pe.wait_ge(selected, TILES)
                logits(0)
                for u in range(units):
                    if u + 1 < units:
                        logits(u + 1)
                    if u >= 1:
                        values(u - 1)
                    turn_probs(u)
                values(units - 1)
                pe.wait_ge(o_ready, units)
                turn(1, S["o"])
                out_linear("dsa_out", 1)

            def mlp(l):
                base, done = STREAM[f"mlp{l}"], 2 * FF_STEPS * l
                hi, lo = act_hi[0], act_lo[0]
                pe.wait_ge(x_updated, 4 + 8 * l)
                turn(2 + 2 * l, xn, TILES * (1 + 2 * l), MLP_TURN)
                for q in range(PER_BLOCK):
                    wait_act(2 + l, q)
                    feature_granule(base + q, (base + q) % RING, hi, lo, q, (bank[6], bank[7]))

                def down(it, k0, slot, first, last):
                    for q in range(PER_BLOCK):
                        g, at_slot = it * 8 + (base + k0 + q), (base + k0 + q) % RING
                        pe.wait_ge(lo_ready, g + 1)
                        if q % 2 == 0:
                            pe.wait_ge(mid_lo, it * 2 + (done + q // 2 + 1))
                        for i in range(TILES):
                            x_hi, x_lo = (m[:, slot, q, i * P:(i + 1) * P] for m in (M["hi"], M["lo"]))
                            for n in range(2):
                                at = slice(n * BLOCK, (n + 1) * BLOCK)
                                dst = bank[2 + 2 * i + n][:, :]
                                pe.matmul(dst, x_hi, w_hi[:, at_slot, at], start=first and q == 0, stop=False, skip_group_check=True)
                                pe.matmul(dst, x_hi, w_lo[:, at_slot, at], start=False, stop=False, skip_group_check=True)
                                mm = pe.matmul(dst, x_lo, w_hi[:, at_slot, at], start=False, stop=last and q == PER_BLOCK - 1,
                                               skip_group_check=True)
                        mm.then_inc(granule_used, 1)

                def step(it, first):
                    if not first:
                        pe.wait_ge(up_relu, it * 2 + (done + 2))
                    feature_block(base, 4, hi, lo, (bank[0], bank[1]), it)
                    down(it, 8, 0, first, False)

                step(0, True)
                with pe.Fori(1, FF_STEPS - 1) as it:
                    step(it, False)
                down(FF_STEPS - 1, 4, 1, False, True)
                modulation(l)

            def modulation(l):
                for n in range(3):
                    pe.wait_ge(mod_used[n], KT * (l + 1))
                pe.wait_ge(up_relu, 2 * FF_STEPS * (l + 1))
                for k in range(2 * KT):
                    mm = pe.matmul(bank[7][:, k:k + 1], M["mod_all"][:, k * P:(k + 1) * P], ones[:, 0:1], start=True, stop=True)
                mm.then_inc(mod_full, 1)
                for n, b in enumerate((6, 0)):
                    at = 2 * D + n * BLOCK
                    pe.matmul(bank[b][:, :], ones, M["mod_all"][:, at:at + BLOCK], start=True, stop=True).then_inc(mod_full, 1)
                pe.wait_ge(mod_ready, 4 * (l + 1))

            def rwkv_in():
                base = STREAM["rkv"]
                turn(3, xn, 2 * TILES)

                def lora(m, names):
                    for at, width in names:
                        for kt in range(KT):
                            if at == 0 and kt % 2 == 0:
                                pe.wait_ge(mixed, 4 * (3 + m) + kt // 2 + 1)
                            mm = pe.matmul(bank[4 + m][0:width, (at > 0) * SEQ:((at > 0) + 1) * SEQ],
                                           R[("w1", "a1", "g1")[m]][:, kt, at:at + width], act_f[:, kt, :],
                                           start=kt == 0, stop=kt == KT - 1)
                    mm.then_inc(lora_full, 1)

                pe.wait_ge(lora_loaded, 16 * 6)
                for n in range(6):
                    c = n // 2
                    hi, lo, banks = act_hi[c % 2], act_lo[c % 2], (bank[2 * (n % 2)], bank[2 * (n % 2) + 1])
                    if n >= 2:
                        pe.wait_ge(rkv_copied, 2 * (n - 1))
                    for q in range(PER_BLOCK):
                        if n % 2 == 0:
                            pe.wait_ge(mix_lo, 4 * c + q + 1)
                        g = base + PER_BLOCK * n + q
                        if c < 2:
                            feature_granule(g, g % RING, hi, lo, q, banks)
                        else:
                            token_granule(g, g % RING, hi, lo, (2 * q, 2 * q + 1), BLOCK, (banks[0][:, :], banks[1][:, :]),
                                          q == 0, q == PER_BLOCK - 1)
                    if n == 3:
                        lora(0, ((0, LORA),))
                    if n == 4:
                        lora(1, ((0, LORA),))
                lora(2, ((0, GHALF), (GHALF, GHALF)))

            def rwkv_mid():
                def head_sums(b, values, of):
                    for pair in range(PAIRS):
                        mm = pe.matmul(bank[b][0:HEADS, 0:SEQ], of[:, pair, :], values[:, pair, :], start=pair == 0, stop=pair == PAIRS - 1)
                    return mm

                pe.wait_ge(rw_act, 1)
                head_sums(7, R["pinv"], head_of).then_inc(rw_pe, 1)
                pe.wait_ge(mid_ready, 3)
                pe.wait_ge(rkv_copied, 12)
                for pair in range(PAIRS):
                    if pair == PAIRS - 1:
                        pe.wait_ge(rw_dve, 2)
                    pe.matmul(bank[pair][:, :], R["w2a2"][:, pair * P:(pair + 1) * P], R["mid"][:, 0:2, :].rearrange("p a t -> p (a t)"),
                              start=True, stop=True).then_inc(lora2_full, 1)
                pe.wait_ge(lora2_ready, 8)
                pe.wait_ge(rw_inverse, 1)
                for b in range(4):
                    spread(4 + b, root_head).then_inc(rw_pe, 1)
                pe.wait_ge(bonus_ready, 1)
                head_sums(1, bonus_prod, head_rk).then_inc(rw_pe, 1)

            def spread(b, rows, first=None):
                first = 2 * (b % 4)
                for j in range(2):
                    mm = pe.matmul(bank[b][:, j * SEQ:(j + 1) * SEQ], R["rows_of"][:, first + j, :], rows[0:HEADS, :], start=True, stop=True)
                return mm

            def scan_loop():
                known = iter(range(1, SCAN_PE + 1))
                heads = [slice(0, CHUNK), slice(CHUNK, P)]
                tiles = [(c, h, heads[h]) for c in range(CHUNKS) for h in range(2)]

                def Q(u, c):
                    return R["inv"][u][:, 0, c, :]

                def M(u, c):
                    return R["inv"][u][:, 1, c, :]

                def N(u, c):
                    return scan["n"][u][:, c, :]

                with pe.Fori(0, SCAN_TURNS) as it:
                    def of(sem_, per, n):
                        pe.wait_ge(sem_, it * per + n)

                    def before(sem_, per, n):
                        value = pe.to_reg(it * per + n)
                        pe.wait_ge(hi_ready, next(known))
                        pe.wait_ge(sem_, value)

                    def each(b, left, right):
                        for c in range(CHUNKS):
                            mm = pe.matmul(bank[b][:, c * P:(c + 1) * P], left(c), right(c), start=True, stop=True)
                        return mm

                    def turn_each(u, b, a):
                        for c in range(CHUNKS):
                            mm = pe.transpose(bank[b][:, c * P:(c + 1) * P], a(u, c), ident)
                        return mm

                    def inv(u, a):
                        return lambda c: a(u, c)

                    def step(scalar, vector, products):
                        for u in range(2):
                            if scalar and vector:
                                of(sc_act, SCAN_ACT, SCAN_BASE + scalar + u)
                            before(*((sc_dve, SCAN_DVE, SCAN_BASE + vector + u) if vector else (sc_act, SCAN_ACT, SCAN_BASE + scalar + u)))
                            products(u, 4 * u).then_inc(sc_pe, 1)

                    for u in range(2):
                        B, prod = 4 * u, scan["prod"][u]
                        of(sc_act, SCAN_ACT, SCAN_BASE - 1 + u)
                        of(sc_dve, SCAN_DVE, SCAN_BASE - 1 + u)
                        of(sc_prod, 2, 1 + u)
                        for c in range(CHUNKS):
                            pe.transpose(bank[B][:, c * P:(c + 1) * P], scan["bk"][u][:, c, :, :].rearrange("p s t -> p (s t)"), ident)
                        for c in range(CHUNKS):
                            mm = pe.transpose(bank[B + 1][:, c * P:(c + 1) * P], prod[:, c, 0, :, :].rearrange("p h t -> p (h t)"), ident)
                        mm.then_inc(sc_pe, 1)
                        for c in range(CHUNKS):
                            mm = pe.matmul(bank[B + 2 + c // 2][:, c % 2 * 2 * P:(c % 2 + 1) * 2 * P],
                                           scan["bk"][u][:, c, :, :].rearrange("p s t -> p (s t)"), prod[:, c, :, :, :].rearrange("p a h t -> p (a h t)"), start=True, stop=True)
                        mm.then_inc(sc_pe, 1)

                    def first(u, B):
                        turn_each(u, B + 2, N)
                        for c, h, rows in tiles:
                            values = heads[1 - h]
                            mm = pe.matmul(bank[B + 3][rows, c * CHUNK:(c + 1) * CHUNK], scan["att"][u][values, CHUNKS * h + c, 0, :],
                                           scan["zz"][u][values, CHUNKS * h + c, 1, :], start=True, stop=True)
                        return mm

                    for u in range(2):
                        of(sc_pool, 2, 1 + u)
                        before(sc_dve, SCAN_DVE, SCAN_BASE + 2 + 3 * u)
                        first(u, 4 * u).then_inc(sc_pe, 1)

                    def squares(u, B):
                        each(B, inv(u, M), inv(u, N))
                        return each(B + 1, inv(u, N), inv(u, M))

                    def fourth(u, B):
                        each(B + 2, inv(u, M), inv(u, Q))
                        each(B + 3, inv(u, M), inv(u, N))
                        return each(B, inv(u, N), inv(u, M))

                    def eighth(u, B):
                        each(B + 1, inv(u, M), inv(u, Q))
                        return each(B + 2, inv(u, N), inv(u, M))

                    for u in range(2):
                        of(sc_dve, SCAN_DVE, SCAN_BASE + 3 + 3 * u)
                        before(sc_act, SCAN_ACT, SCAN_BASE + 3 + u)
                        squares(u, 4 * u).then_inc(sc_pe, 1)
                    step(5, 7, fourth)
                    step(7, 9, eighth)
                    step(9, 11, lambda u, B: each(B + 3, inv(u, M), inv(u, Q)))
                    step(None, 13, lambda u, B: turn_each(u, B, Q))
                    step(11, None, lambda u, B: each(B + 1, inv(u, N), inv(u, M)))
                    step(13, None, lambda u, B: each(B + 2, inv(u, M), inv(u, Q)))
                    step(None, 17, lambda u, B: turn_each(u, B + 3, Q))
                    step(15, 15, lambda u, B: each(B, inv(u, N), inv(u, M)))
                    step(17, None, lambda u, B: each(B + 1, inv(u, M), inv(u, Q)))
                    def removed_values(u, B):
                        for c in range(CHUNKS):
                            mm = pe.matmul(bank[B + 2 + c // 2][:, c % 2 * P:(c % 2 + 1) * P], Q(u, c),
                                           scan["aw"][u][:, c, :, :].rearrange("p a t -> p (a t)"), start=True, stop=True)
                        return mm

                    step(None, 19, removed_values)

                    def results(u, B):
                        zz, tok, att = scan["zz"][u], scan["tok"][u], scan["att"][u]

                        def put(b, n, rows, left, right):
                            return pe.matmul(bank[b][rows, n * CHUNK:(n + 1) * CHUNK], left, right, start=True, stop=True)

                        def removed(c, h):
                            return zz[heads[h], CHUNKS * h + c, 0, :]

                        def keys(c, h):
                            return tok[:, c, h * RN:(h + 1) * RN]

                        def both(c, h):
                            return zz[:, CHUNKS * h + c, 1, :]

                        for c, h, rows in tiles:
                            if 1 <= c <= 2:
                                put(B, c - 1, rows, removed(c, h), keys(c, h)[rows, :])
                        for c, h, rows in tiles:
                            if c >= 1:
                                put(B, 1 + c, rows, removed(c, h), att[rows, CHUNKS * h + c, 1, :])
                        for h, rows in enumerate(heads):
                            for c in range(CHUNKS):
                                if c <= 2:
                                    put(B, 5 + c, rows, keys(c, h), both(c, h))
                                mm = put(B + 1, c, rows, both(c, h), att[:, CHUNKS * h + c, 1, :])
                        return mm

                    for u in range(2):
                        of(sc_act, SCAN_ACT, SCAN_BASE + 19 + u)
                        before(sc_dve, SCAN_DVE, SCAN_BASE + 21 + u)
                        results(u, 4 * u).then_inc(sc_pe, 1)

            def rwkv_out():
                halves = [slice(0, RN), slice(RN, P)]

                def chunk_products(b, left, right):
                    for pair in range(PAIRS):
                        for at in halves:
                            mm = pe.matmul(bank[b][at, pair * RN:(pair + 1) * RN], left(at, pair), right(at, pair), start=True, stop=True)
                    return mm

                def chunk(t, c):
                    return lambda at, pair: t[at, pair, c * CHUNK:(c + 1) * CHUNK]

                def states(c):
                    return chunk(R["pinv"], 0) if c == 1 else lambda at, pair: state[at, c - 2, pair, :]

                pe.wait_ge(sc_dve, SCAN_BASE + SCAN_DVE * SCAN_TURNS)
                pe.wait_ge(sc_act, SCAN_BASE + SCAN_ACT * SCAN_TURNS)
                for c in range(1, CHUNKS):
                    if c > 1:
                        pe.wait_ge(chain_ready, c - 1)
                    if c < CHUNKS - 1:
                        chunk_products(c - 1, chunk(R["sg"], c), states(c)).then_inc(chain_full, 1)
                    if c > 2:
                        pe.wait_ge(y_ready, c - 2)
                    chunk_products(2 + c % 2, states(c), chunk(R["rT"], c)).then_inc(y_full, 1)
                    if c == 1:
                        for b in range(4):
                            for k in range(CHUNKS):
                                mm = pe.transpose(bank[4 + b][:, k * P:(k + 1) * P], R["v"][:, k, b * P:(b + 1) * P], ident)
                            mm.then_inc(vT_full, 1)
                pe.wait_ge(g2_loaded, 32)
                for b in range(4):
                    pe.wait_ge(vT_ready, b + 1)
                    for j in range(2):
                        at, dst = slice((2 * b + j) * P, (2 * b + j + 1) * P), bank[4 + b][:, j * SEQ:(j + 1) * SEQ]
                        pe.matmul(dst, R["g2a"][:, at], R["mid"][0:GHALF, 2, :], start=True, stop=False)
                        mm = pe.matmul(dst, R["g2b"][:, at], R["mid"][0:GHALF, 3, :], start=False, stop=True)
                    mm.then_inc(glora_full, 1)
                pe.wait_ge(y_ready, CHUNKS - 1)
                for b in range(4):
                    spread(b, R["mid"][:, 0, :]).then_inc(bonus_full, 1)
                for b in range(4):
                    pe.wait_ge(glora_ready, b + 1)
                    pe.matmul(bank[4 + b][:, :], view["head_mean"], R["cum"][:, 2 * b:2 * b + 2, :], start=True, stop=True).then_inc(mean_full, 1)
                pe.wait_ge(centred, 4)
                for pair in range(PAIRS):
                    if pair % 2 == 0:
                        pe.wait_ge(dev_sq, pair // 2 + 1)
                    mm = pe.matmul(bank[4][0:HEADS, 0:SEQ], head_of[:, pair, :], R["pinv"][:, pair, :], start=pair == 0, stop=pair == PAIRS - 1)
                mm.then_inc(var_full, 1)
                pe.wait_ge(rw_inverse, 2)
                for b in range(4):
                    spread(4 + b, root_head).then_inc(spread_full, 1)
                for n in range(2):
                    for q in range(PER_BLOCK):
                        if n == 0:
                            pe.wait_ge(mix_lo, 12 + q + 1)
                        g = STREAM["rwkv_out"] + PER_BLOCK * n + q
                        token_granule(g, g % RING, act_hi[0], act_lo[0], (2 * q, 2 * q + 1), BLOCK,
                                      (bank[2 * n][:, :], bank[2 * n + 1][:, :]), q == 0, q == PER_BLOCK - 1)

            def conv():
                base = STREAM["conv"]
                hi, lo = act_hi[0], act_lo[0]
                turn(5, xn, 4 * TILES)
                for half in range(2):
                    for n, (left, count) in enumerate(((conv_x, 1), (conv_t, 1), (conv_b, 1), (conv_z, 2))):
                        if half:
                            pe.wait_ge(left, count)
                        for q in range(PER_BLOCK):
                            if n == half == 0:
                                wait_act(4, q)
                            g = base + 16 * half + 4 * n + q
                            feature_granule(g, g % RING, hi, lo, q, (bank[2 * n], bank[2 * n + 1]))
                pe.wait_ge(conv_x, 2)
                pe.wait_ge(conv_t, 2)
                out_linear("conv_out", 5, 1)

            def dilated():
                base = STREAM["dil"]
                hi, lo = act_hi[0], act_lo[0]
                turn(6, xn, 5 * TILES)
                with pe.Fori(0, 6) as it:
                    for n in range(2):
                        pe.wait_ge(rope_x, it * 4 + (6 + 2 * n))
                        for q in range(PER_BLOCK):
                            wait_act(6, q)
                            feature_granule(number(base, 4 * n + q, it), (base + 4 * n + q) % RING, hi, lo, q, (bank[2 * n], bank[2 * n + 1]))
                for n in range(4):
                    if n < 2:
                        pe.wait_ge(rope_x, 30 + 2 * n)
                    else:
                        pe.wait_ge(vz_copied, 2 * (n - 1))
                    token_block(base, PER_BLOCK * (12 + n), hi, lo, [bank[2 * (n % 2) + i][:, :] for i in range(TILES)])

                units = DIL_HEADS * TILES

                def logits(u):
                    h, i, first = u // TILES, u % TILES, 2 * (u % 3)
                    if u >= 3:
                        pe.wait_ge(p_ready, 8 + u - 2)
                    pe.matmul(bank[first][:, :].rearrange("p (g s) -> p g s", g=2), ident_bf, dil_mask[:, i, 0:2, :], start=True, stop=False, skip_group_check=True)
                    pe.matmul(bank[first + 1][:, 0:SEQ], ident_bf, dil_mask[:, i, 2, :], start=True, stop=False, skip_group_check=True)
                    for g in range(DIL_GROUPS):
                        q = g * DIL_HEADS + h
                        mm = pe.matmul(bank[first + g // 2][:, g % 2 * SEQ:(g % 2 + 1) * SEQ], L["qk"][:, q, i * P:(i + 1) * P],
                                       L["qk"][:, DIL_GROUPS * DIL_HEADS + q, :], start=False, stop=True, skip_group_check=True)
                    mm.then_inc(s_full, 1)

                def turn_probs(u):
                    pe.wait_ge(probs_sum, 2 * u + 2)
                    if u >= 1:
                        pe.wait_ge(pT_ready_act, KV_HEADS + u)
                    for s in range(TILES):
                        mm = pe.transpose(bank[6][:, s * P:(s + 1) * P], LA["p"][:, u % 2, 0, s * P:(s + 1) * P], ident)
                    mm.then_inc(pT_full, 1)

                def values(u):
                    h, slot = u // TILES, u % 2
                    pe.wait_ge(pT_ready_act, KV_HEADS + u + 1)
                    if u >= 1:
                        pe.wait_ge(o_ready, 8 + u)
                    for s in range(TILES):
                        mm = pe.matmul(bank[7][:, 0:P], LA["pT"][:, slot, s, :], L["v"][:, s, h * P:(h + 1) * P], start=s == 0, stop=s == TILES - 1)
                    mm.then_inc(o_full, 1)

                pe.wait_ge(vz_copied, 8)
                pe.wait_ge(rope_done, 32)
                logits(0)
                logits(1)
                for u in range(units):
                    if u + 2 < units:
                        logits(u + 2)
                    if u >= 1:
                        values(u - 1)
                    turn_probs(u)
                values(units - 1)
                pe.wait_ge(o_ready, 8 + units)
                turn(7, L["z"])
                out_linear("dil_out", 7)

            init()
            dsa()
            mlp(0)
            rwkv_in()
            rwkv_mid()
            scan_loop()
            rwkv_out()
            mlp(1)
            conv()
            dilated()


def laid_out(inputs):
    parts, rows_of, parts_bf = shape_constants()
    arrays = {name: np.asarray(value) for name, value in inputs.items() if np.size(value)}
    columns = np.concatenate([arrays[name].reshape(-1, P) for name in PARAMS])
    arrays["params"] = np.ascontiguousarray(columns.T)
    idx = arrays["dsa_w_in"][0][:, OFF_IK:OFF_IW + IDX_HEADS].reshape(KT, P, HD + IDX_HEADS).transpose(1, 0, 2)
    arrays["w_idx"] = np.concatenate([idx[:, :, :HD], idx], 2)
    arrays["const"] = np.concatenate([v.reshape(P, -1) for v in parts.values()], 1)
    arrays["const_bf"] = np.concatenate([v.reshape(P, -1) for v in parts_bf.values()], 1)
    arrays["rows_of"] = rows_of[:HEADS].reshape(HEADS, -1)
    return arrays


def kernel(**inputs):
    import ml_dtypes
    from concourse import bacc as _bacc
    from concourse.bass_utils import run_bass_kernel_spmd

    arrays = laid_out(inputs)
    arrays["const_bf"] = arrays["const_bf"].astype(ml_dtypes.bfloat16)
    nc = _bacc.Bacc("TRN2", target_bir_lowering=False, num_devices=1)
    A = {name: nc.dram_tensor(f"in_{name}_dram", value.shape, mybir.dt.from_np(value.dtype), kind="ExternalInput").ap()
         for name, value in arrays.items()}
    out = nc.dram_tensor("out_dram", (1, SEQ, D), F32, kind="ExternalOutput").ap()
    program(nc, A, out)
    feed = {f"in_{name}_dram": value for name, value in arrays.items()}
    result = run_bass_kernel_spmd(nc, [feed], core_ids=[0])
    return np.asarray(result.results[0]["out_dram"])
```
